# Optimizing a Trainium2 kernel written in Bass

```python
import math
import jax, jax.numpy as jnp
from jax import lax
import numpy as np

D_MODEL = 1024
BATCH = 1
SEQ = 1024
DEPTH = 1

GRID_W = 64
CTX_LEN = 256
HEAD_DIM = 64
DIFF_HEADS = 4
DIFF_V_DIM = 2 * HEAD_DIM
GQA_HEADS = 8
GQA_KV_HEADS = 2
MIX_WIDTH = DIFF_HEADS * DIFF_V_DIM + GQA_HEADS * HEAD_DIM
IN_SIZES = (DIFF_HEADS * 2 * HEAD_DIM, DIFF_HEADS * 2 * HEAD_DIM, DIFF_HEADS * DIFF_V_DIM,
            GQA_HEADS * HEAD_DIM, GQA_KV_HEADS * HEAD_DIM, GQA_KV_HEADS * HEAD_DIM)
IN_WIDTH = sum(IN_SIZES)
ROPE_THETA = 10000.0
Q_BLOCK = 128
N_EXPERTS = 64
N_GROUPS = 8
TOPK_GROUPS = 4
TOP_K = 8
EXPERT_DIM = 256
SHARED_DIM = 256
ROUTED_SCALE = 2.5
EXPERT_BLOCK = 256
N_MOD = 6
EPS = 1e-6

kernel_name = "hybrid_diffattn_gqa_moe_dit_block"

def rmsnorm(x, g):
    xf = x.astype(jnp.float32)
    y = xf * lax.rsqrt(jnp.mean(xf * xf, axis=-1, keepdims=True) + EPS)
    return (y * g.astype(jnp.float32)).astype(x.dtype)

def modulate(h, shift, scale):
    return h * (1.0 + scale) + shift

def rope_rotate(x, ang):
    q = ang.shape[-1]
    shape = (1, ang.shape[0]) + (1,) * (x.ndim - 3) + (q,)
    cos = jnp.cos(ang).reshape(shape).astype(x.dtype)
    sin = jnp.sin(ang).reshape(shape).astype(x.dtype)
    a, b = x[..., :q], x[..., q:]
    return jnp.concatenate([a * cos - b * sin, a * sin + b * cos], axis=-1)

def rope_2d(x, ang_row, ang_col):
    half = x.shape[-1] // 2
    return jnp.concatenate([rope_rotate(x[..., :half], ang_row),
                            rope_rotate(x[..., half:], ang_col)], axis=-1)

def attend(q, k, v, scale):
    b, s, hq, d = q.shape
    hk, dv = k.shape[2], v.shape[-1]
    g = hq // hk
    nblk = s // Q_BLOCK
    qb = q.reshape(b, nblk, Q_BLOCK, hk, g, d).swapaxes(0, 1)

    def one_block(qi):
        sc = jnp.einsum("bqhgd,bkhd->bhgqk", qi, k, preferred_element_type=jnp.float32) * scale
        p = jax.nn.softmax(sc, axis=-1).astype(v.dtype)
        return jnp.einsum("bhgqk,bkhe->bqhge", p, v)

    o = lax.map(one_block, qb)
    return o.swapaxes(0, 1).reshape(b, s, hq, dv)

def project(h, w_in, q_g, k_g):
    b, L, _ = h.shape
    p = h @ w_in
    offs = [int(o) for o in np.cumsum(IN_SIZES)[:-1]]
    dq, dk, dv, gq, gk, gv = jnp.split(p, offs, axis=-1)
    dq = dq.reshape(b, L, DIFF_HEADS, 2, HEAD_DIM)
    dk = dk.reshape(b, L, DIFF_HEADS, 2, HEAD_DIM)
    dv = dv.reshape(b, L, DIFF_HEADS, DIFF_V_DIM)
    gq = rmsnorm(gq.reshape(b, L, GQA_HEADS, HEAD_DIM), q_g)
    gk = rmsnorm(gk.reshape(b, L, GQA_KV_HEADS, HEAD_DIM), k_g)
    gv = gv.reshape(b, L, GQA_KV_HEADS, HEAD_DIM)
    return dq, dk, dv, gq, gk, gv

def mix_groups(dq, dk, dv, gq, gk, gv, lam, lam_init, subln_g):
    b, L = dq.shape[:2]
    sc = HEAD_DIM ** -0.5
    o1 = attend(dq[:, :, :, 0], dk[:, :, :, 0], dv, sc)
    o2 = attend(dq[:, :, :, 1], dk[:, :, :, 1], dv, sc)
    o_diff = rmsnorm(o1 - lam.astype(o2.dtype) * o2, subln_g) * (1.0 - lam_init)
    o_gqa = attend(gq, gk, gv, sc)
    return jnp.concatenate([o_diff.reshape(b, L, -1), o_gqa.reshape(b, L, -1)], axis=-1)

def swiglu(h, wg, wu, wd):
    return (jax.nn.silu(h @ wg) * (h @ wu)) @ wd

def moe(h, w_router, router_bias, w_eg, w_eu, w_ed, w_sg, w_su, w_sd):
    t, d = h.shape
    s = jax.nn.sigmoid(jnp.dot(h, w_router, preferred_element_type=jnp.float32))
    s_sel = s + router_bias.astype(jnp.float32)
    grp = s_sel.reshape(t, N_GROUPS, N_EXPERTS // N_GROUPS)
    grp_score = lax.top_k(grp, 2)[0].sum(-1)
    _, top_groups = lax.top_k(grp_score, TOPK_GROUPS)
    group_mask = jnp.any(top_groups[..., None] == jnp.arange(N_GROUPS), axis=1)
    expert_mask = jnp.repeat(group_mask, N_EXPERTS // N_GROUPS, axis=1)
    _, idx = lax.top_k(jnp.where(expert_mask, s_sel, -jnp.inf), TOP_K)
    w = jnp.take_along_axis(s, idx, axis=1)
    w = w / jnp.sum(w, axis=-1, keepdims=True) * ROUTED_SCALE

    n = t * TOP_K
    flat_e = idx.reshape(-1)
    flat_tok = jnp.repeat(jnp.arange(t, dtype=jnp.int32), TOP_K)
    flat_w = w.reshape(-1)
    order = jnp.argsort(flat_e)
    se, stok, sw = flat_e[order], flat_tok[order], flat_w[order]
    counts = jnp.bincount(flat_e, length=N_EXPERTS)
    start = jnp.cumsum(counts) - counts
    padded = (counts + EXPERT_BLOCK - 1) // EXPERT_BLOCK * EXPERT_BLOCK
    block_end = jnp.cumsum(padded)
    pstart = block_end - padded
    dest = pstart[se] + (jnp.arange(n) - start[se])
    n_blocks = (n + EXPERT_BLOCK - 1) // EXPERT_BLOCK + N_EXPERTS
    n_pad = n_blocks * EXPERT_BLOCK
    tok_buf = jnp.full((n_pad,), t, jnp.int32).at[dest].set(stok)
    w_buf = jnp.zeros((n_pad,), jnp.float32).at[dest].set(sw)
    block_expert = jnp.minimum(
        jnp.searchsorted(block_end, jnp.arange(n_blocks) * EXPERT_BLOCK, side="right"), N_EXPERTS - 1)
    h_pad = jnp.concatenate([h, jnp.zeros((1, d), h.dtype)], axis=0)

    def run_block(args):
        tok, wt, e = args
        y = swiglu(h_pad[tok], w_eg[e], w_eu[e], w_ed[e])
        return y * wt[:, None].astype(y.dtype)

    y_blocks = lax.map(run_block, (tok_buf.reshape(n_blocks, EXPERT_BLOCK),
                                   w_buf.reshape(n_blocks, EXPERT_BLOCK), block_expert))
    routed = jax.ops.segment_sum(y_blocks.reshape(n_pad, d), tok_buf, num_segments=t + 1)[:t]
    return routed + swiglu(h, w_sg, w_su, w_sd)

def setup_inputs(seed: int = 0) -> dict:
    key = jax.random.key(seed)
    ks = jax.random.split(key, 32)
    f32 = jnp.float32

    def nrm(k, shape, scale):
        return jax.random.normal(k, shape, f32) * scale

    def gain(k, shape):
        return 1.0 + 0.1 * jax.random.normal(k, shape, f32)

    L, D = DEPTH, D_MODEL
    return {
        "x": nrm(ks[0], (BATCH, SEQ, D), 1.0),
        "c": nrm(ks[1], (BATCH, D), 1.0),
        "ctx": nrm(ks[2], (BATCH, CTX_LEN, D), 1.0),
        "c_ctx": nrm(ks[3], (D,), 1.0),
        "w_mod": nrm(ks[4], (L, D, N_MOD * D), D ** -0.5),
        "b_mod": nrm(ks[5], (L, N_MOD * D), 0.02),
        "g_pre_mix": gain(ks[6], (L, D)),
        "g_post_mix": gain(ks[7], (L, D)),
        "w_in": nrm(ks[8], (L, D, IN_WIDTH), D ** -0.5),
        "q_norm_g": gain(ks[9], (L, HEAD_DIM)),
        "k_norm_g": gain(ks[10], (L, HEAD_DIM)),
        "lambda_q1": nrm(ks[11], (L, HEAD_DIM), 0.1),
        "lambda_k1": nrm(ks[12], (L, HEAD_DIM), 0.1),
        "lambda_q2": nrm(ks[13], (L, HEAD_DIM), 0.1),
        "lambda_k2": nrm(ks[14], (L, HEAD_DIM), 0.1),
        "subln_g": gain(ks[15], (L, DIFF_V_DIM)),
        "w_out": nrm(ks[16], (L, MIX_WIDTH, D), MIX_WIDTH ** -0.5),
        "g_pre_ffn": gain(ks[17], (L, D)),
        "g_post_ffn": gain(ks[18], (L, D)),
        "w_router": nrm(ks[19], (L, D, N_EXPERTS), D ** -0.5),
        "router_bias": nrm(ks[20], (L, N_EXPERTS), 0.01),
        "w_exp_gate": nrm(ks[21], (L, N_EXPERTS, D, EXPERT_DIM), D ** -0.5),
        "w_exp_up": nrm(ks[22], (L, N_EXPERTS, D, EXPERT_DIM), D ** -0.5),
        "w_exp_down": nrm(ks[23], (L, N_EXPERTS, EXPERT_DIM, D), EXPERT_DIM ** -0.5),
        "w_sh_gate": nrm(ks[24], (L, D, SHARED_DIM), D ** -0.5),
        "w_sh_up": nrm(ks[25], (L, D, SHARED_DIM), D ** -0.5),
        "w_sh_down": nrm(ks[26], (L, SHARED_DIM, D), SHARED_DIM ** -0.5),
    }

def reference(x, c, ctx, c_ctx, w_mod, b_mod, g_pre_mix, g_post_mix, w_in, q_norm_g, k_norm_g,
              lambda_q1, lambda_k1, lambda_q2, lambda_k2, subln_g, w_out, g_pre_ffn, g_post_ffn,
              w_router, router_bias, w_exp_gate, w_exp_up, w_exp_down, w_sh_gate, w_sh_up, w_sh_down):
    b, s, d = x.shape
    rows = s // GRID_W
    row_ids = jnp.repeat(jnp.arange(rows), GRID_W).astype(jnp.float32)
    col_ids = jnp.tile(jnp.arange(GRID_W), rows).astype(jnp.float32)
    n_freq = HEAD_DIM // 4
    inv_freq = ROPE_THETA ** (-jnp.arange(n_freq, dtype=jnp.float32) / n_freq)
    ang_row = row_ids[:, None] * inv_freq
    ang_col = col_ids[:, None] * inv_freq

    for l in range(DEPTH):
        lam_init = 0.8 - 0.6 * math.exp(-0.3 * l)
        lam = (jnp.exp(jnp.sum(lambda_q1[l].astype(jnp.float32) * lambda_k1[l].astype(jnp.float32)))
               - jnp.exp(jnp.sum(lambda_q2[l].astype(jnp.float32) * lambda_k2[l].astype(jnp.float32)))
               + lam_init)
        mod = jax.nn.silu(c) @ w_mod[l] + b_mod[l]
        mod_c = jax.nn.silu(c_ctx) @ w_mod[l] + b_mod[l]
        sh1, sc1, gt1, sh2, sc2, gt2 = jnp.split(mod[:, None, :], N_MOD, axis=-1)
        csh1, csc1, cgt1, csh2, csc2, cgt2 = jnp.split(mod_c, N_MOD)

        h = modulate(rmsnorm(x, g_pre_mix[l]), sh1, sc1)
        hc = modulate(rmsnorm(ctx, g_pre_mix[l]), csh1, csc1)
        dq, dk, dv, gq, gk, gv = project(h, w_in[l], q_norm_g[l], k_norm_g[l])
        dqc, dkc, dvc, gqc, gkc, gvc = project(hc, w_in[l], q_norm_g[l], k_norm_g[l])
        dq, dk = rope_2d(dq, ang_row, ang_col), rope_2d(dk, ang_row, ang_col)
        gq, gk = rope_2d(gq, ang_row, ang_col), rope_2d(gk, ang_row, ang_col)
        mixed = mix_groups(dq, jnp.concatenate([dkc, dk], axis=1), jnp.concatenate([dvc, dv], axis=1),
                           gq, jnp.concatenate([gkc, gk], axis=1), jnp.concatenate([gvc, gv], axis=1),
                           lam, lam_init, subln_g[l])
        x = x + gt1 * rmsnorm(mixed @ w_out[l], g_post_mix[l])

        h2 = modulate(rmsnorm(x, g_pre_ffn[l]), sh2, sc2)
        y = moe(h2.reshape(b * s, d), w_router[l], router_bias[l], w_exp_gate[l], w_exp_up[l],
                w_exp_down[l], w_sh_gate[l], w_sh_up[l], w_sh_down[l]).reshape(b, s, d)
        x = x + gt2 * rmsnorm(y, g_post_ffn[l])

        if l + 1 < DEPTH:
            mixed_c = mix_groups(dqc, dkc, dvc, gqc, gkc, gvc, lam, lam_init, subln_g[l])
            ctx = ctx + cgt1 * rmsnorm(mixed_c @ w_out[l], g_post_mix[l])
            h2c = modulate(rmsnorm(ctx, g_pre_ffn[l]), csh2, csc2)
            yc = moe(h2c.reshape(-1, d), w_router[l], router_bias[l], w_exp_gate[l], w_exp_up[l],
                     w_exp_down[l], w_sh_gate[l], w_sh_up[l], w_sh_down[l]).reshape(ctx.shape)
            ctx = ctx + cgt2 * rmsnorm(yc, g_post_ffn[l])
    return x


_drawn_inputs = setup_inputs


def setup_inputs(seed=0):
    import zlib

    import numpy as np

    out = dict(_drawn_inputs(seed))
    spreads = {}
    factors = {}
    for name, (base, spread) in spreads.items():
        noise = np.random.default_rng([zlib.crc32(name.encode()), seed]).standard_normal(out[name].shape)
        drawn = base * np.exp(spread * noise) if base else spread * noise
        out[name] = __import__('jax').numpy.asarray(drawn.astype(out[name].dtype))
    for name, factor in factors.items():
        out[name] = (out[name] * factor).astype(out[name].dtype)
    return out
```

```python
import math
from contextlib import ExitStack

import numpy as np

import concourse.bass as bass
from concourse import mybir

F32 = mybir.dt.float32
BF16 = mybir.dt.bfloat16
I32 = mybir.dt.int32
U32 = mybir.dt.uint32
ALU = mybir.AluOpType
ACT = mybir.ActivationFunctionType
AX = mybir.AxisListType

P = 128
D = 1024
KD = D // P
SEQ, CTX = 1024, 256
NT, NC = SEQ // P, CTX // P
KT_N = NT + NC
KEYS = SEQ + CTX
HD = 64
DH, GH, GKV = 4, 8, 2
NP = 8
NH = 2 * NP
QKW = 1664
NHEADS = QKW // HD
VW = 640
INW = 2304
E, FE = 64, 256
NG, TOPG, TOPK = 8, 4, 8
GRID_W = 64
ROUTED_SCALE = 2.5
LAM_INIT = 0.8 - 0.6 * math.exp(-0.3 * 0)
EPS = 1e-6
BIG = 1e30
DIFF_V = 2 * HD
NBLK = SEQ * TOPK // P + E
WS = 4
NPC = 6
SCALE = HD ** -0.5



class Build:

    def __init__(self, nc):
        self.nc = nc

    def sb(self, st, name, shape, dt=F32):
        return st.enter_context(self.nc.sbuf_tensor(name, shape, dt))

    def pb(self, st, name, shape, dt=F32):
        return st.enter_context(self.nc.psum_tensor(name, shape, dt))

    def sem(self, st, name):
        return st.enter_context(self.nc.semaphore(name))


def chain(eng, s, start=0):
    n = [0]

    def step(ins):
        n[0] += 1
        ins.then_inc(s, 1)
        eng.wait_ge(s, start + n[0])
    step.n = n
    return step


A1, B1, A1C, B1C, A2, B2, G1, G2 = range(8)


def modulation(b, a, ident, rows, nlam, mhalf, w_in, s_win):
    nc = b.nc
    SL, SW = 2, 512
    NS = 6 * D // SW
    with ExitStack() as ph:
        ring = b.sb(ph, "w_mod_ring", [P, SL, KD, SW])
        cs = b.sb(ph, "c_cols", [P, 2, KD])
        sg = b.sb(ph, "c_sig", [P, 2, KD])
        silu = b.sb(ph, "c_silu", [P, KD, 2])
        mrow = b.sb(ph, "mod_row", [2, 6, D])
        brow = b.sb(ph, "b_mod_row", [2, 6 * D])
        grow = b.sb(ph, "gain_row", [2, 4, D])
        sel = b.sb(ph, "row_select", [2, 2, P])
        lamv = b.sb(ph, "lambda_vecs", [P, 4, HD])
        lamj = b.sb(ph, "lambda_prod", [P, 2, HD])
        lamt = b.sb(ph, "lambda_terms", [P, 8])
        ps = b.pb(ph, "ps_mod", [P, 8, 512])
        s_c = b.sem(ph, "c_loaded")
        s_small = b.sem(ph, "small_loaded")
        s_slab = [b.sem(ph, f"slab_loaded{u}") for u in range(SL)]
        s_exp = b.sem(ph, "m_exp")
        s_silu = b.sem(ph, "silu_ready")
        s_lam = b.sem(ph, "lambda_sums")
        s_prod = b.sem(ph, "slab_multiplied")
        s_row = b.sem(ph, "row_part_out")
        s_rows = b.sem(ph, "rows_ready")
        s_bc = b.sem(ph, "row_broadcast")
        s_out = b.sem(ph, "broadcast_out")
        s_dve = b.sem(ph, "m_dve")
        block = ph.enter_context(nc.Block())
        NSMALL = 2 + 1 + 4 + 4

        @block.gpsimd
        def _(pool):
            nc.gpsimd.memset(mhalf[:, 0:16], -0.5)
            nc.gpsimd.memset(mhalf[:, 16:32], EPS)

        @block.sync
        def _(sp):
            sp.dma_start(cs[:, 0, :], a["c"].rearrange("o (p k) -> (o p) k", k=KD)).then_inc(s_c, 16)
            sp.dma_start(cs[:, 1, :], a["c_ctx"].rearrange("(p k) -> p k", k=KD)).then_inc(s_c, 16)
            wm = a["w_mod"][0].rearrange("(p k) n -> p k n", k=KD)
            for u in range(SL):
                sp.dma_start(ring[:, u], wm[:, :, u * SW:(u + 1) * SW]).then_inc(s_slab[u], 16)
            with sp.Fori(1, NS // SL) as i:
                for u in range(SL):
                    sp.wait_ge(s_prod, i * SL + (u - SL + 1))
                    sp.dma_start(ring[:, u], wm[:, :, ds(i * (SL * SW) + u * SW, SW)]).then_inc(s_slab[u], 16)
            sp.dma_start(w_in[:], a["w_in"][0].rearrange("(k p) n -> p k n", p=P)).then_inc(s_win, 16)

        @block.scalar
        def _(act):
            act.dma_start(ident[:], a["k_ident"]).then_inc(s_small, 16)
            act.dma_start(sel[:], a["k_select"]).then_inc(s_small, 16)
            act.dma_start(brow[:], a["b_mod"].broadcast_to([2, 6 * D])).then_inc(s_small, 16)
            for j, g in enumerate(("g_pre_mix", "g_post_mix", "g_pre_ffn", "g_post_ffn")):
                act.dma_start(grow[:, j], a[g].broadcast_to([2, D])).then_inc(s_small, 16)
            for j, v in enumerate(("lambda_q1", "lambda_k1", "lambda_q2", "lambda_k2")):
                act.dma_start(lamv[:, j], a[v].broadcast_to([P, HD])).then_inc(s_small, 16)
            act.wait_ge(s_c, 32)
            act.activation(sg[:], cs[:], ACT.Exp, scale=-1.0).then_inc(s_exp, 1)
            act.wait_ge(s_lam, 1)
            act.activation(lamt[:, 2:4], lamt[:, 0:2], ACT.Exp).then_inc(s_exp, 1)
            for n in range(1, 16, 2):
                act.wait_ge(s_bc, n + 1)
                r, h = divmod(n, 2)
                act.activation(rows[:, r, h * 512:(h + 1) * 512], ps[:, n % 8], ACT.Copy).then_inc(s_out, 1)

        @block.vector
        def _(dve):
            step = chain(dve, s_dve)
            dve.wait_ge(s_c, 32)
            dve.wait_ge(s_exp, 1)
            step(nc.vector.tensor_scalar_add(sg[:], sg[:], 1.0))
            step(nc.vector.reciprocal(sg[:], sg[:]))
            nc.vector.tensor_tensor(silu[:].rearrange("p k c -> p c k"), sg[:], cs[:], ALU.mult).then_inc(s_silu, 1)
            dve.wait_ge(s_small, NSMALL * 16)
            step(nc.vector.tensor_tensor(lamj[:, 0], lamv[:, 0], lamv[:, 1], ALU.mult))
            step(nc.vector.tensor_tensor(lamj[:, 1], lamv[:, 2], lamv[:, 3], ALU.mult))
            nc.vector.tensor_reduce(lamt[:, 0:2], lamj[:], AX.X, ALU.add).then_inc(s_lam, 1)
            dve.wait_ge(s_exp, 2)
            step(nc.vector.tensor_tensor(lamt[:, 4:5], lamt[:, 3:4], lamt[:, 2:3], ALU.subtract))
            step(nc.vector.tensor_scalar_add(nlam[:], lamt[:, 4:5], -LAM_INIT))
            mflat = mrow[:].rearrange("c s d -> c (s d)")
            with dve.Fori(0, NS // SL) as i:
                for u in range(SL):
                    dve.wait_ge(s_prod, i * SL + u + 1)
                    at = i * (SL * SW) + u * SW
                    nc.vector.tensor_tensor(mflat[:, ds(at, SW)], ps[0:2, u], brow[:, ds(at, SW)], ALU.add).then_inc(s_row, 1)
            dve.wait_ge(s_row, NS)
            nc.vector.scalar_tensor_tensor(mrow[:, 1], mrow[:, 1], 1.0, grow[:, 0], ALU.add, ALU.mult)
            nc.vector.scalar_tensor_tensor(mrow[:, 4], mrow[:, 4], 1.0, grow[:, 2], ALU.add, ALU.mult)
            nc.vector.tensor_tensor(mrow[:, 2], mrow[:, 2], grow[:, 1], ALU.mult)
            nc.vector.tensor_tensor(mrow[:, 5], mrow[:, 5], grow[:, 3], ALU.mult).then_inc(s_rows, 1)
            for n in range(0, 16, 2):
                dve.wait_ge(s_bc, n + 1)
                r, h = divmod(n, 2)
                nc.vector.tensor_copy(rows[:, r, h * 512:(h + 1) * 512], ps[:, n % 8]).then_inc(s_out, 1)

        @block.tensor
        def _(pe):
            pe.wait_ge(s_silu, 1)
            with pe.Fori(0, NS // SL) as i:
                for u in range(SL):
                    pe.wait_ge(s_slab[u], i * 16 + 16)
                    if u == 0:
                        with pe.If(i > 0):
                            pe.wait_ge(s_row, i * SL)
                            pe.nop()
                    for k in range(KD):
                        last = nc.tensor.matmul(ps[0:2, u], silu[:, k], ring[:, u, k], start=(k == 0), stop=(k == KD - 1))
                    last.then_inc(s_prod, 1)
            pe.wait_ge(s_rows, 1)
            srcs = [(1, 0), (0, 0), (1, 1), (0, 1), (4, 0), (3, 0), (2, 0), (5, 0)]
            for n in range(16):
                r, h = divmod(n, 2)
                src, who = srcs[r]
                if n >= 8:
                    pe.wait_ge(s_out, 8)
                nc.tensor.matmul(ps[:, n % 8], sel[:, who], mrow[:, src, h * 512:(h + 1) * 512],
                                 start=True, stop=True).then_inc(s_bc, 1)


def projections(b, a, ident, rows, mhalf, w_in, s_win, kT, vv, qT_d):
    nc = b.nc
    TURNS = KT_N // 2
    with ExitStack() as ph:
        xt = [b.sb(ph, f"x_tile{u}", [P, D]) for u in range(2)]
        hT = [b.sb(ph, f"hT{u}", [P, KD, P]) for u in range(2)]
        qk = b.sb(ph, "qk_rows", [P, QKW])
        t1 = b.sb(ph, "rope_a", [P, QKW])
        t2 = b.sb(ph, "rope_b", [P, QKW])
        rt = [b.sb(ph, f"rope_table{u}", [P, 2, HD]) for u in range(2)]
        junk = b.sb(ph, "square_out", [P, D], BF16)
        ssq = b.sb(ph, "sum_squares", [P, 2, 2])
        hss = b.sb(ph, "head_squares", [P, 32])
        gq = b.sb(ph, "q_gain", [P, HD])
        gk = b.sb(ph, "k_gain", [P, HD])
        qTs = b.sb(ph, "qT_stage", [P, NP, P])
        psT = b.pb(ph, "ps_transpose", [P, 3, 512])
        psC = b.pb(ph, "ps_chunk", [P, 5, 512])
        s_x = [b.sem(ph, f"x_loaded{u}") for u in range(2)]
        s_rt = [b.sem(ph, f"rope_loaded{u}") for u in range(2)]
        s_gain = b.sem(ph, "gain_loaded")
        s_sq = b.sem(ph, "sum_square")
        s_h = b.sem(ph, "h_ready")
        s_T = b.sem(ph, "group_transposed")
        s_Te = b.sem(ph, "group_out")
        s_ch = b.sem(ph, "chunk_done")
        s_che = b.sem(ph, "chunk_out")
        s_rh = b.sem(ph, "h_rstd")
        s_hv = b.sem(ph, "head_mean_square")
        s_rr = b.sem(ph, "head_rstd")
        s_pool = b.sem(ph, "p_pool")
        s_rope = b.sem(ph, "rope_done")
        s_qd = b.sem(ph, "qT_stored")
        s_dve = b.sem(ph, "p_dve")
        block = ph.enter_context(nc.Block())
        CH = [(1024, 512, [(0, 512, "v", 0)]), (512, 512, [(0, 512, "qk", 1024)]),
              (2048, 256, [(0, 128, "qk", 1536), (128, 128, "v", 512)]),
              (0, 512, [(0, 512, "qk", 0)]), (1536, 512, [(0, 512, "gq", 512)])]
        HG, QG = (0, 2), (4, 8)
        NGR = 12
        QKG = [([1024 + j * P for j in range(4)], "k", 0), ([1536], "k", 4),
               ([j * P for j in range(4)], "q", 0), ([512 + j * P for j in range(4)], "q", 4)]
        xa, rope = a["tokens"], a["k_rope"]

        @block.sync
        def _(sp):
            sp.dma_start(gq[:], a["q_norm_g"].broadcast_to([P, HD])).then_inc(s_gain, 16)
            sp.dma_start(gk[:], a["k_norm_g"].broadcast_to([P, HD])).then_inc(s_gain, 16)
            for u in range(2):
                sp.dma_start(xt[u][:], xa[u * P:(u + 1) * P, :]).then_inc(s_x[u], 16)
                sp.dma_start(rt[u][:], rope[u * P:(u + 1) * P]).then_inc(s_rt[u], 16)

            def turn(i, last):
                if not last:
                    for u in range(2):
                        sp.wait_ge(s_T, i * NGR + (HG[u] + 2))
                        sp.dma_start(xt[u][:], xa[ds(i * (2 * P) + (2 + u) * P, P), :]).then_inc(s_x[u], 16)
                for u in range(2):
                    if not last:
                        sp.wait_ge(s_rope, i * 2 + (u + 1))
                        sp.dma_start(rt[u][:], rope[ds(i * (2 * P) + (2 + u) * P, P)]).then_inc(s_rt[u], 16)
                    sp.wait_ge(s_Te, i * NGR + (QG[u] + 4))
                    sp.dma_start(qT_d[ds(i * 2 + u, 1)].rearrange("o p n -> (o p) n"),
                                 qTs[:].rearrange("p j n -> p (j n)")).then_inc(s_qd, 16)

            with sp.Fori(0, TURNS - 1) as i:
                turn(i, False)
            turn(TURNS - 1, True)
            sp.wait_ge(s_qd, KT_N * 16)

        @block.scalar
        def _(act):
            def square(i, u):
                act.wait_ge(s_x[u], i * 16 + 16)
                if not (isinstance(i, int) and i + u == 0):
                    act.wait_ge(s_sq, i * 2 + u)
                act.activation(junk[:], xt[u][:], ACT.Square, scale=D ** -0.5, accum_out=ssq[:, u, 0:1]).then_inc(s_sq, 1)

            def out_h(i, u):
                for g in range(2):
                    act.wait_ge(s_T, i * NGR + (HG[u] + g + 1))
                    act.activation(hT[u][:, 4 * g:4 * g + 4], psT[:, (HG[u] + g) % 3].rearrange("p (k n) -> p k n", k=4),
                                   ACT.Copy).then_inc(s_Te, 1)

            def out_chunk(i, u, c):
                act.wait_ge(s_ch, i * 10 + (5 * u + c + 1))
                if c == 1 and u == 1:
                    act.wait_ge(s_rope, i * 2 + 1)
                if c == 1 and u == 0 and not (isinstance(i, int) and i == 0):
                    act.wait_ge(s_rope, i * 2)
                for o, w, kind, at in CH[c][2]:
                    src = psC[:, c, o:o + w]
                    if kind == "gq":
                        src = src.rearrange("p (a j d) -> p a j d", a=2, d=HD)
                        dst = qk[:, at:at + w].rearrange("p (j a d) -> p a j d", a=2, d=HD)
                    elif kind == "qk":
                        dst = qk[:, at:at + w]
                    else:
                        dst = vv[:, ds(i * 2 + u, 1), at:at + w].rearrange("p o n -> p (o n)")
                    ins = act.activation(dst, src, ACT.Copy)
                ins.then_inc(s_che, 1)

            def out_qk(i, u):
                for g, (cols, kind, at) in enumerate(QKG):
                    n = QG[u] + g
                    act.wait_ge(s_T, i * NGR + (n + 1))
                    w = len(cols) * P
                    src = psT[:, n % 3, 0:w].rearrange("p (k n) -> p k n", n=P)
                    if kind == "k":
                        dst = kT[:, at:at + len(cols), ds(i * (2 * P) + u * P, P)]
                    else:
                        dst = qTs[:, at:at + 4]
                        if at == 0 and not (isinstance(i, int) and i == 0 and u == 0):
                            act.wait_ge(s_qd, i * 32 + 16 * u)
                    act.activation(dst, src, ACT.Copy).then_inc(s_Te, 1)

            def turn(i, last):
                out_h(i, 0)
                for c in range(5):
                    out_chunk(i, 0, c)
                out_h(i, 1)
                if not last:
                    square(i + 1, 0)
                for c in range(5):
                    out_chunk(i, 1, c)
                    if c == 2 and not last:
                        square(i + 1, 1)
                out_qk(i, 0)
                out_qk(i, 1)

            square(0, 0)
            square(0, 1)
            turn(0, False)
            with act.Fori(1, TURNS - 1) as i:
                turn(i, False)
            turn(TURNS - 1, True)

        @block.gpsimd
        def _(pool):
            def rstd_h(i, u, own):
                pool.wait_ge(s_sq, i * 2 + (u + 1))
                nc.gpsimd.tensor_tensor(ssq[:, u, 1:2], ssq[:, u, 0:1], mhalf[:, 16:17], ALU.add).then_inc(s_pool, 1)
                pool.wait_ge(s_pool, own)
                nc.gpsimd.tensor_tensor(ssq[:, u, 1:2], ssq[:, u, 1:2], mhalf[:, 0:1], ALU.pow).then_inc(s_rh, 1)

            def rstd_heads(i, u, own):
                pool.wait_ge(s_hv, i * 2 + (u + 1))
                nc.gpsimd.tensor_tensor(hss[:, 16:26], hss[:, 0:10], mhalf[:, 16:26], ALU.add).then_inc(s_pool, 1)
                pool.wait_ge(s_pool, own)
                nc.gpsimd.tensor_tensor(hss[:, 16:26], hss[:, 16:26], mhalf[:, 0:10], ALU.pow).then_inc(s_rr, 1)

            def turn(i, last):
                rstd_heads(i, 0, i * 4 + 3)
                if not last:
                    rstd_h(i + 1, 0, i * 4 + 4)
                    rstd_h(i + 1, 1, i * 4 + 5)
                rstd_heads(i, 1, i * 4 + (4 if last else 6))

            rstd_h(0, 0, 1)
            rstd_h(0, 1, 2)
            with pool.Fori(0, TURNS - 1) as i:
                turn(i, False)
            turn(TURNS - 1, True)

        @block.vector
        def _(dve):
            STEPS = 2 * (1 + 6 + 1)

            def make_h(step, u, i):
                dve.wait_ge(s_rh, i * 2 + (u + 1))
                sc = ssq[:, u, 1:2]
                ra, rb = (A1C, B1C) if isinstance(i, int) and i == 0 else (A1, B1)
                step(nc.vector.scalar_tensor_tensor(xt[u][:], xt[u][:], sc, rows[:, ra], ALU.mult, ALU.mult))
                nc.vector.tensor_tensor(xt[u][:], xt[u][:], rows[:, rb], ALU.add).then_inc(s_h, 1)

            def rotary(step, u, i):
                dve.wait_ge(s_che, i * 10 + (5 * u + 5))
                if not (isinstance(i, int) and i == 0 and u == 0):
                    dve.wait_ge(s_T, i * NGR + (QG[0] + 4 if u else 0))
                normed = [(1536, 2, gk, 8), (512, 8, gq, 0)]
                for at, nh, gain, hs in normed:
                    X = qk[:, at:at + nh * HD].rearrange("p (h d) -> p h d", d=HD)
                    J = t2[:, at:at + nh * HD].rearrange("p (h d) -> p h d", d=HD)
                    step(nc.vector.scalar_tensor_tensor(J, X, 1.0 / HD, X, ALU.mult, ALU.mult))
                    ins = nc.vector.tensor_reduce(hss[:, hs:hs + nh], J, AX.X, ALU.add)
                ins.then_inc(s_hv, 1)
                dve.wait_ge(s_rr, i * 2 + (u + 1))
                for at, nh, gain, hs in normed:
                    X = qk[:, at:at + nh * HD].rearrange("p (h d) -> p h d", d=HD)
                    r = hss[:, 16 + hs:16 + hs + nh]
                    step(nc.vector.tensor_tensor(X, X, r.unsqueeze(2).broadcast_to([P, nh, HD]), ALU.mult))
                    step(nc.vector.tensor_tensor(X, X, gain[:].unsqueeze(1).broadcast_to([P, nh, HD]), ALU.mult))
                dve.wait_ge(s_rt[u], i * 16 + 16)
                cosb = rt[u][:, 0:1, :].broadcast_to([P, NHEADS, HD])
                nc.vector.tensor_tensor(t1[:].rearrange("p (h d) -> p h d", d=HD),
                                        qk[:].rearrange("p (h d) -> p h d", d=HD), cosb, ALU.mult)
                for f in range(2):
                    X5 = qk[:].rearrange("p (h f s d) -> p f h s d", f=2, s=2, d=16)[:, f]
                    T5 = t2[:].rearrange("p (h f s d) -> p f h s d", f=2, s=2, d=16)[:, f]
                    S5 = rt[u][:, 1, :].rearrange("p (f s d) -> p f s d", f=2, s=2)[:, f]
                    for s_ in range(2):
                        ins = nc.vector.tensor_tensor(T5[:, :, s_], X5[:, :, 1 - s_],
                                                      S5[:, s_:s_ + 1].broadcast_to([P, NHEADS, 16]), ALU.mult)
                step(ins)
                nc.vector.tensor_tensor(t1[:], t1[:], t2[:], ALU.add).then_inc(s_rope, 1)

            def turn(i, last, base):
                step = chain(dve, s_dve, base)
                rotary(step, 0, i)
                if not last:
                    make_h(step, 0, i + 1)
                    make_h(step, 1, i + 1)
                rotary(step, 1, i)
                assert step.n[0] == (14 if last else STEPS), step.n[0]

            dve.wait_ge(s_gain, 32)
            step = chain(dve, s_dve)
            make_h(step, 0, 0)
            make_h(step, 1, 0)
            turn(0, False, 2)
            with dve.Fori(1, TURNS - 1) as i:
                turn(i, False, i * STEPS + 2)
            turn(TURNS - 1, True, (TURNS - 1) * STEPS + 2)

        @block.tensor
        def _(pe):
            def bank_free(i, n):
                if isinstance(i, int) and i * NGR + n < 3:
                    return
                pe.wait_ge(s_Te, i * NGR + (n - 2))

            def t_h(i, u):
                pe.wait_ge(s_h, i * 2 + (u + 1))
                for g in range(2):
                    bank_free(i, HG[u] + g)
                    for k in range(4):
                        c = (4 * g + k) * P
                        last = nc.tensor.transpose(psT[:, (HG[u] + g) % 3, k * P:(k + 1) * P], xt[u][:, c:c + P], ident[:])
                    last.then_inc(s_T, 1)

            def chunks(i, u):
                for c, (src, w, _) in enumerate(CH):
                    if c == 0:
                        pe.wait_ge(s_Te, i * NGR + (HG[u] + 2))
                    if not (isinstance(i, int) and i == 0 and u == 0):
                        pe.wait_ge(s_che, i * 10 + (5 * (u - 1) + c + 1))
                    for k in range(KD):
                        last = nc.tensor.matmul(psC[:, c, 0:w], hT[u][:, k], w_in[:, k, src:src + w],
                                                start=(k == 0), stop=(k == KD - 1))
                    last.then_inc(s_ch, 1)

            def t_qk(i, u):
                pe.wait_ge(s_rope, i * 2 + (u + 1))
                for g, (cols, _, _) in enumerate(QKG):
                    n = QG[u] + g
                    bank_free(i, n)
                    for k, c in enumerate(cols):
                        last = nc.tensor.transpose(psT[:, n % 3, k * P:(k + 1) * P], t1[:, c:c + P], ident[:])
                    last.then_inc(s_T, 1)

            def turn(i):
                for u in range(2):
                    t_h(i, u)
                    chunks(i, u)
                t_qk(i, 0)
                t_qk(i, 1)

            pe.wait_ge(s_win, 16)
            turn(0)
            with pe.Fori(1, TURNS) as i:
                turn(i)


def attention(b, a, ident, nlam, mhalf, kT, vv, qT_d, o_d):
    nc = b.nc
    CW = [(0, 512), (512, 512), (1024, 256)]
    with ExitStack() as ph:
        qT = b.sb(ph, "qT", [P, NP, P])
        pr = b.sb(ph, "probs", [P, 2, KEYS])
        pT = b.sb(ph, "probsT", [P, 2, KT_N, P])
        mx = b.sb(ph, "chunk_max", [P, 4, 4])
        nb = b.sb(ph, "neg_max", [P, 4])
        sm = b.sb(ph, "chunk_sum", [P, 4, 4])
        rs = b.sb(ph, "row_scale", [P, 8])
        o1 = b.sb(ph, "o_first", [P, DIFF_V])
        o2 = b.sb(ph, "o_diff", [P, DIFF_V])
        oj = b.sb(ph, "o_square", [P, DIFF_V])
        ob = b.sb(ph, "o_tile", [P, D])
        sg = b.sb(ph, "sub_gain", [P, DIFF_V])
        psS = b.pb(ph, "ps_scores", [P, 3, 512])
        psP = b.pb(ph, "ps_probsT", [P, 3, 512])
        psO = b.pb(ph, "ps_out", [P, 2, 512])
        s_q = [b.sem(ph, f"qT_loaded{h}") for h in range(2)]
        s_g = b.sem(ph, "sub_gain_loaded")
        s_qk = b.sem(ph, "scores_chunk")
        s_nb = b.sem(ph, "neg_max_ready")
        s_exp = b.sem(ph, "probs_chunk")
        s_tp = b.sem(ph, "probsT_chunk")
        s_pta = b.sem(ph, "probsT_by_act")
        s_ptd = b.sem(ph, "probsT_by_dve")
        s_pv = b.sem(ph, "pv_done")
        s_of = b.sem(ph, "o_bank_read")
        s_ov = b.sem(ph, "o_mean_square")
        s_or = b.sem(ph, "o_rstd")
        s_ob = b.sem(ph, "o_part")
        s_od = b.sem(ph, "o_stored")
        s_obfree = b.sem(ph, "o_tile_free")
        s_carry = b.sem(ph, "a_carry")
        s_dve = b.sem(ph, "a_dve")
        block = ph.enter_context(nc.Block())
        C3 = 3 * NH

        def half(tile, h):
            return qT_d[ds(tile, 1)].rearrange("o p n -> (o p) n")[:, h * 512:(h + 1) * 512]

        @block.sync
        def _(sp):
            sp.dma_start(sg[:], a["subln_g"].broadcast_to([P, DIFF_V])).then_inc(s_g, 16)
            for h in range(2):
                sp.dma_start(qT[:, 4 * h:4 * h + 4].rearrange("p j n -> p (j n)"), half(NC, h)).then_inc(s_q[h], 16)
            with sp.Fori(0, NT - 1) as i:
                for h in range(2):
                    sp.wait_ge(s_qk, i * C3 + (h + 1) * (C3 // 2))
                    sp.dma_start(qT[:, 4 * h:4 * h + 4].rearrange("p j n -> p (j n)"), half(i + (NC + 1), h)).then_inc(s_q[h], 16)

        @block.gpsimd
        def _(pool):
            pool.sem_inc(s_obfree, 1)
            with pool.Fori(0, NT) as i:
                for p in range(DH):
                    pool.wait_ge(s_ov, i * DH + (p + 1))
                    nc.gpsimd.tensor_tensor(rs[:, 5:6], rs[:, 3:4], mhalf[:, 0:1], ALU.pow).then_inc(s_or, 1)
                pool.wait_ge(s_ob, i * DH + DH)
                pool.wait_ge(s_of, i * NH + (NH + 2))
                pool.sem_inc(s_carry, 1)
                pool.dma_start(o_d[ds(i * P, P), :], ob[:]).then_inc(s_od, 16)
                pool.wait_ge(s_od, i * 16 + 16)
                pool.sem_inc(s_obfree, 1)

        @block.scalar
        def _(act):
            act.sem_inc(s_exp, 3)
            with act.Fori(0, NT) as i:
                def exps(k):
                    act.wait_ge(s_nb, i * NH + (k + 1))
                    for j, (o, w) in enumerate(CW):
                        act.activation(pr[:, k % 2, o:o + w], psS[:, j, 0:w], ACT.Exp, bias=nb[:, k % 4:k % 4 + 1],
                                       scale=SCALE, accum_out=sm[:, k % 4, j:j + 1]).then_inc(s_exp, 1)

                exps(0)
                for k in range(NH):
                    for j in (0, 2):
                        o, w = CW[j]
                        act.wait_ge(s_tp, i * C3 + (3 * k + j + 1))
                        act.activation(pT[:, k % 2, o // P:(o + w) // P], psP[:, j, 0:w].rearrange("p (t n) -> p t n", n=P),
                                       ACT.Copy).then_inc(s_pta, 1)
                    if k + 1 < NH:
                        exps(k + 1)

        @block.vector
        def _(dve):
            dve.sem_inc(s_of, 2)
            dve.wait_ge(s_g, 16)
            first = chain(dve, s_dve)
            first(nc.vector.tensor_scalar_mul(sg[:], sg[:], 1.0 - LAM_INIT))
            STEPS = NH * 3 + DH * (2 + 3) + GH * 2
            with dve.Fori(0, NT) as i:
                step = chain(dve, s_dve, i * STEPS + 1)

                def maxes(k):
                    for j, (o, w) in enumerate(CW):
                        dve.wait_ge(s_qk, i * C3 + (3 * k + j + 1))
                        ins = nc.vector.reduce_max(mx[:, k % 4, j:j + 1], psS[:, j, 0:w], AX.X)
                        if j == 1:
                            step(ins)
                    step(ins)
                    step(nc.vector.reduce_max(mx[:, k % 4, 3:4], mx[:, k % 4, 0:3], AX.X))
                    nc.vector.tensor_scalar_mul(nb[:, k % 4:k % 4 + 1], mx[:, k % 4, 3:4], -SCALE).then_inc(s_nb, 1)

                def finish(k):
                    p, h = divmod(k, 2)
                    dve.wait_ge(s_pv, i * NH + (k + 1))
                    r = rs[:, 0:1]
                    step(nc.vector.reduce_sum(r, sm[:, k % 4, 0:3], AX.X))
                    step(nc.vector.reciprocal(rs[:, 1:2], r))
                    r = rs[:, 1:2]
                    if p < DH and h == 0:
                        nc.vector.tensor_scalar_mul(o1[:], psO[:, k % 2, 0:DIFF_V], r).then_inc(s_of, 1)
                    elif p < DH:
                        step(nc.vector.tensor_tensor(rs[:, 2:3], r, nlam[:], ALU.mult))
                        dve.wait_ge(s_of, i * NH + (k + 2))
                        nc.vector.scalar_tensor_tensor(o2[:], psO[:, k % 2, 0:DIFF_V], rs[:, 2:3], o1[:], ALU.mult, ALU.add).then_inc(s_of, 1)
                        dve.wait_ge(s_of, i * NH + (k + 3))
                        nc.vector.tensor_tensor_reduce(out=oj[:], in0=o2[:], in1=o2[:], scale=1.0 / DIFF_V, scalar=EPS,
                                                       op0=ALU.mult, op1=ALU.add, accum_out=rs[:, 3:4]).then_inc(s_ov, 1)
                        dve.wait_ge(s_or, i * DH + (p + 1))
                        nc.vector.scalar_tensor_tensor(ob[:, p * DIFF_V:(p + 1) * DIFF_V], o2[:], rs[:, 5:6], sg[:],
                                                       ALU.mult, ALU.mult).then_inc(s_ob, 1)
                    else:
                        j = p - DH
                        at = 512 + (j + 4 * h) * HD
                        nc.vector.tensor_scalar_mul(ob[:, at:at + HD], psO[:, k % 2, 0:HD], r).then_inc(s_of, 1)

                maxes(0)
                for k in range(NH):
                    if k + 1 < NH:
                        maxes(k + 1)
                    o, w = CW[1]
                    dve.wait_ge(s_tp, i * C3 + (3 * k + 2))
                    nc.vector.tensor_copy(pT[:, k % 2, o // P:(o + w) // P], psP[:, 1, 0:w].rearrange("p (t n) -> p t n", n=P)).then_inc(s_ptd, 1)
                    if k == 1:
                        dve.wait_ge(s_obfree, i + 1)
                    if k >= 1:
                        finish(k - 1)
                finish(NH - 1)
                assert step.n[0] == STEPS, step.n[0]

        @block.tensor
        def _(pe):
            with pe.Fori(0, NT) as i:
                def qk_(k):
                    p, h = divmod(k, 2)
                    kp = min(p, 4)
                    if k % 8 == 0:
                        pe.wait_ge(s_q[k // 8], i * 16 + 16)
                    for j, (o, w) in enumerate(CW):
                        pe.wait_ge(s_exp, i * C3 + (3 * k + j + 1))
                        nc.tensor.matmul(psS[:, j, 0:w], qT[h * HD:(h + 1) * HD, p], kT[h * HD:(h + 1) * HD, kp, o:o + w],
                                         start=True, stop=True).then_inc(s_qk, 1)

                qk_(0)
                for k in range(NH):
                    if k + 1 < NH:
                        qk_(k + 1)
                    for j, (o, w) in enumerate(CW):
                        pe.wait_ge(s_exp, i * C3 + (3 * k + j + 4))
                        for t in range(w // P):
                            last = nc.tensor.transpose(psP[:, j, t * P:(t + 1) * P], pr[:, k % 2, o + t * P:o + (t + 1) * P], ident[:])
                        last.then_inc(s_tp, 1)
                    p, h = divmod(k, 2)
                    c, w = (p * DIFF_V, DIFF_V) if p < DH else (512 + h * HD, HD)
                    for t in range(KT_N):
                        if t == 0:
                            pe.wait_ge(s_of, i * NH + (k + 1))
                            pe.wait_ge(s_pta, i * (2 * NH) + (2 * k + 1))
                        if t == 4:
                            pe.wait_ge(s_ptd, i * NH + (k + 1))
                        if t == 8:
                            pe.wait_ge(s_pta, i * (2 * NH) + (2 * k + 2))
                        last = nc.tensor.matmul(psO[:, k % 2, 0:w], pT[:, k % 2, t], vv[:, t, c:c + w],
                                                start=(t == 0), stop=(t == KT_N - 1))
                    last.then_inc(s_pv, 1)


def output_and_router(b, a, ident, rows, mhalf, x1, entry, mask, o_d, h2_d, y_d):
    nc = b.nc
    TURNS = NT // 2
    with ExitStack() as ph:
        w_o = b.sb(ph, "w_out_sb", [P, KD, D])
        w_r = b.sb(ph, "w_router_sb", [P, KD, E])
        w_g = b.sb(ph, "w_shared_gu", [P, KD, 2 * FE])
        w_d = b.sb(ph, "w_shared_down", [P, 2, D])
        bias = b.sb(ph, "router_bias_row", [P, E])
        ot = [b.sb(ph, f"o_in{u}", [P, D]) for u in range(2)]
        xr = [b.sb(ph, f"x_in{u}", [P, D]) for u in range(2)]
        oT = [b.sb(ph, f"oT{u}", [P, KD, P]) for u in range(2)]
        hT = [b.sb(ph, f"h2T{u}", [P, KD, P]) for u in range(2)]
        h2 = [b.sb(ph, f"h2_row{u}", [P, D]) for u in range(2)]
        tmp = b.sb(ph, "row_tmp", [P, D])
        rwb = b.sb(ph, "weight_piece", [P, 3, E], BF16)
        yb = [b.sb(ph, f"y_shared{u}", [P, D]) for u in range(2)]
        aT = b.sb(ph, "act_T", [P, 2, P])
        ga = [b.sb(ph, f"gate_a{u}", [P, FE]) for u in range(2)]
        gb = b.sb(ph, "gate_b", [P, FE])
        junk = b.sb(ph, "square_junk", [P, D], BF16)
        ms = b.sb(ph, "mean_squares", [P, 2, 8])
        sc = b.sb(ph, "scores", [P, 2, E])
        rw = b.sb(ph, "router_work", [P, 6, E])
        g8 = b.sb(ph, "group_top", [P, NG, 8])
        r8 = b.sb(ph, "router_small", [P, 6, 8])
        psT = b.pb(ph, "ps_t", [P, 2, 512])
        psY = b.pb(ph, "ps_y", [P, 4, 512])
        psR = b.pb(ph, "ps_r", [P, 512])
        psG = b.pb(ph, "ps_g", [P, 512])
        S = {n: b.sem(ph, "r_" + n) for n in (
            "weights", "T", "Te", "proj", "sqP", "rs1", "x1", "sqX", "rs2", "h2", "logit", "expR", "gu", "expG",
            "act", "down", "yout", "routed", "h2_stored", "y_stored", "dve", "pool", "hold", "carry")}
        s_o = [b.sem(ph, f"o_loaded{u}") for u in range(2)]
        s_xr = [b.sem(ph, f"xr_loaded{u}") for u in range(2)]
        block = ph.enter_context(nc.Block())
        GR = 10
        GO, GHT, GA = (0, 2), (4, 6), (8, 9)
        NW = 6

        @block.sync
        def _(sp):
            for u in range(2):
                sp.dma_start(ot[u][:], o_d[u * P:(u + 1) * P, :]).then_inc(s_o[u], 16)
                sp.dma_start(xr[u][:], a["tokens"][CTX + u * P:CTX + (u + 1) * P, :]).then_inc(s_xr[u], 16)
            with sp.Fori(0, TURNS - 1) as i:
                for u in range(2):
                    sp.wait_ge(S["T"], i * GR + (GO[u] + 2))
                    sp.dma_start(ot[u][:], o_d[ds(i * (2 * P) + (2 + u) * P, P), :]).then_inc(s_o[u], 16)
                    sp.wait_ge(S["x1"], i * 2 + (u + 1))
                    sp.dma_start(xr[u][:], a["tokens"][ds(i * (2 * P) + (CTX + (2 + u) * P), P), :]).then_inc(s_xr[u], 16)

        @block.gpsimd
        def _(pool):
            with pool.Fori(0, TURNS) as i:
                for u in range(2):
                    m = ms[:, u]
                    pool.wait_ge(S["sqP"], i * 4 + (2 * u + 2))
                    nc.gpsimd.tensor_tensor(m[:, 2:3], m[:, 0:1], m[:, 1:2], ALU.add).then_inc(S["pool"], 1)
                    pool.wait_ge(S["pool"], i * 6 + (3 * u + 1))
                    nc.gpsimd.tensor_tensor(m[:, 3:4], m[:, 2:3], mhalf[:, 16:17], ALU.add).then_inc(S["pool"], 1)
                    pool.wait_ge(S["pool"], i * 6 + (3 * u + 2))
                    nc.gpsimd.tensor_tensor(m[:, 4:5], m[:, 3:4], mhalf[:, 0:1], ALU.pow).then_inc(S["rs1"], 1)
                    pool.wait_ge(S["sqX"], i * 2 + (u + 1))
                    nc.gpsimd.tensor_tensor(m[:, 6:7], m[:, 5:6], mhalf[:, 16:17], ALU.add).then_inc(S["pool"], 1)
                    pool.wait_ge(S["pool"], i * 6 + (3 * u + 3))
                    nc.gpsimd.tensor_tensor(m[:, 7:8], m[:, 6:7], mhalf[:, 0:1], ALU.pow).then_inc(S["rs2"], 1)
                    pool.wait_ge(S["h2"], i * 2 + (u + 1))
                    pool.sem_inc(S["carry"], 1)
                    pool.dma_start(h2_d[ds(i * (2 * P) + u * P, P), :], h2[u][:]).then_inc(S["h2_stored"], 16)
                for u in range(2):
                    pool.wait_ge(S["yout"], i * 2 + (u + 3))
                    pool.sem_inc(S["carry"], 1)
                    pool.dma_start(y_d[ds(i * (2 * P) + u * P, P), :], yb[u][:]).then_inc(S["y_stored"], 16)
                pool.wait_ge(S["h2_stored"], i * 32 + 32)
                pool.wait_ge(S["y_stored"], i * 32 + 32)
                pool.sem_inc(S["hold"], 1)

        @block.scalar
        def _(act):
            act.dma_start(w_o[:], a["w_out"][0].rearrange("(k p) n -> p k n", p=P)).then_inc(S["weights"], 16)
            act.dma_start(w_r[:], a["w_router"][0].rearrange("(p k) n -> p k n", k=KD)).then_inc(S["weights"], 16)
            act.dma_start(w_g[:, :, 0:FE], a["w_sh_gate"][0].rearrange("(p k) n -> p k n", k=KD)).then_inc(S["weights"], 16)
            act.dma_start(w_g[:, :, FE:], a["w_sh_up"][0].rearrange("(p k) n -> p k n", k=KD)).then_inc(S["weights"], 16)
            act.dma_start(w_d[:], a["w_sh_down"][0].rearrange("(k p) n -> p k n", p=P)).then_inc(S["weights"], 16)
            act.dma_start(bias[:], a["router_bias"].broadcast_to([P, E])).then_inc(S["weights"], 16)
            act.sem_inc(S["Te"], 2)
            act.sem_inc(S["yout"], 2)
            act.sem_inc(S["expR"], 1)
            with act.Fori(0, TURNS) as i:
                def out_T(dst, n, w=4):
                    act.wait_ge(S["T"], i * GR + (n + 1))
                    act.activation(dst, psT[:, n % 2, 0:w * P].rearrange("p (k n) -> p k n", n=P), ACT.Copy).then_inc(S["Te"], 1)

                def squares(u):
                    for h in range(2):
                        act.wait_ge(S["proj"], i * 4 + (2 * u + h + 1))
                        act.activation(junk[:, h * 512:(h + 1) * 512], psY[:, 2 * u + h], ACT.Square, scale=D ** -0.5,
                                       accum_out=ms[:, u, h:h + 1]).then_inc(S["sqP"], 1)
                    act.wait_ge(S["sqP"], i * 4 + (2 * u + 2))
                    act.wait_ge(S["x1"], i * 2 + (u + 1))
                    act.activation(junk[:], x1[:, ds(i * 2 + u, 1)].rearrange("p o n -> p (o n)"), ACT.Square,
                                   scale=D ** -0.5, accum_out=ms[:, u, 5:6]).then_inc(S["sqX"], 1)
                    act.wait_ge(S["sqX"], i * 2 + (u + 1))

                def exps(u):
                    act.wait_ge(S["logit"], i * 2 + (u + 1))
                    act.activation(sc[:, u], psR[:, 0:E], ACT.Exp, scale=-1.0).then_inc(S["expR"], 1)
                    act.wait_ge(S["gu"], i * 2 + (u + 1))
                    act.activation(ga[u][:], psG[:, 0:FE], ACT.Exp, scale=-1.0).then_inc(S["expG"], 1)

                def y_out(u):
                    for h in range(2):
                        act.wait_ge(S["down"], i * 4 + (2 * u + h + 1))
                        ins = act.activation(yb[u][:, h * 512:(h + 1) * 512], psY[:, 2 * u + h], ACT.Copy)
                    ins.then_inc(S["yout"], 1)

                for u in range(2):
                    for g in range(2):
                        out_T(oT[u][:, 4 * g:4 * g + 4], GO[u] + g)
                squares(0)
                for g in range(2):
                    out_T(hT[0][:, 4 * g:4 * g + 4], GHT[0] + g)
                squares(1)
                exps(0)
                for g in range(2):
                    out_T(hT[1][:, 4 * g:4 * g + 4], GHT[1] + g)
                exps(1)
                for u in range(2):
                    out_T(aT[:], GA[u], 2)
                    if u == 0:
                        act.wait_ge(S["hold"], i + 1)
                    y_out(u)

        @block.vector
        def _(dve):
            STEPS = 2 * (2 + 3 + 23)
            dve.sem_inc(S["hold"], 1)
            dve.sem_inc(S["act"], 1)
            dve.wait_ge(S["weights"], NW * 16)
            with dve.Fori(0, TURNS) as i:
                step = chain(dve, S["dve"], i * STEPS)

                def residual(u):
                    X = x1[:, ds(i * 2 + u, 1)].rearrange("p o n -> p (o n)")
                    dve.wait_ge(s_xr[u], i * 16 + 16)
                    dve.wait_ge(S["rs1"], i * 2 + (u + 1))
                    Y = psY[:, 2 * u:2 * u + 2].rearrange("p b n -> p (b n)")
                    step(nc.vector.scalar_tensor_tensor(tmp[:], Y, ms[:, u, 4:5], rows[:, G1], ALU.mult, ALU.mult))
                    nc.vector.tensor_tensor(X, tmp[:], xr[u][:], ALU.add).then_inc(S["x1"], 1)
                    dve.wait_ge(S["rs2"], i * 2 + (u + 1))
                    dve.wait_ge(S["x1"], i * 2 + (u + 1))
                    step(nc.vector.scalar_tensor_tensor(tmp[:], X, ms[:, u, 7:8], rows[:, A2], ALU.mult, ALU.mult))
                    if u == 0:
                        dve.wait_ge(S["hold"], i + 1)
                    nc.vector.tensor_tensor(h2[u][:].rearrange("p (k q) -> p q k", k=KD), tmp[:].rearrange("p (q k) -> p q k", k=KD),
                                            rows[:, B2].rearrange("p (q k) -> p q k", k=KD), ALU.add).then_inc(S["h2"], 1)

                def shared_act(u):
                    dve.wait_ge(S["expG"], i * 2 + (u + 1))
                    step(nc.vector.tensor_scalar_add(gb[:], ga[u][:], 1.0))
                    step(nc.vector.reciprocal(gb[:], gb[:]))
                    step(nc.vector.tensor_tensor(gb[:], gb[:], psG[:, 0:FE], ALU.mult))
                    nc.vector.tensor_tensor(ga[u][:], gb[:], psG[:, FE:2 * FE], ALU.mult).then_inc(S["act"], 1)

                def route(u):
                    def steph(ins):
                        step(ins)
                        dve.sem_inc(S["carry"], 1)
                    s, sel, m, W = sc[:, u], rw[:, 0], rw[:, 1], rw[:, 2]
                    dve.wait_ge(S["expR"], i * 2 + (u + 2))
                    step(nc.vector.tensor_scalar_add(s, s, 1.0))
                    step(nc.vector.reciprocal(s, s))
                    steph(nc.vector.tensor_tensor(sel, s, bias[:], ALU.add))
                    for g in range(NG):
                        ins = nc.vector.max(g8[:, g], sel[:, g * 8:(g + 1) * 8])
                    step(ins)
                    steph(nc.vector.tensor_tensor(r8[:, 0], g8[:, :, 0], g8[:, :, 1], ALU.add))
                    step(nc.vector.max(r8[:, 1], r8[:, 0]))
                    steph(nc.vector.memset(r8[:, 1, TOPG:8], -BIG))
                    step(nc.vector.match_replace(r8[:, 2], r8[:, 1], r8[:, 0], BIG))
                    step(nc.vector.tensor_scalar(r8[:, 3], r8[:, 2], BIG / 2, None, ALU.is_ge))
                    step(nc.vector.tensor_scalar(r8[:, 4], r8[:, 3], -1.0, BIG, ALU.add, ALU.mult))
                    v3 = lambda t: t.rearrange("p (g e) -> p g e", g=NG)
                    gm = r8[:, 3].unsqueeze(2).broadcast_to([P, NG, 8])
                    pen = r8[:, 4].unsqueeze(2).broadcast_to([P, NG, 8])
                    step(nc.vector.tensor_tensor(v3(m), v3(sel), gm, ALU.mult))
                    steph(nc.vector.tensor_tensor(v3(m), v3(m), pen, ALU.add))
                    steph(nc.vector.max(r8[:, 5], m))
                    step(nc.vector.match_replace(W, r8[:, 5], m, BIG))
                    step(nc.vector.tensor_scalar(rw[:, 3], W, BIG / 2, None, ALU.is_ge))
                    M = mask[:, ds(i * 2 + u, 1)].rearrange("p o e -> p (o e)")
                    nc.vector.tensor_copy(M, rw[:, 3])
                    step(nc.vector.tensor_tensor_reduce(out=W, in0=s, in1=rw[:, 3], scale=1.0, scalar=0.0, op0=ALU.mult,
                                                        op1=ALU.add, accum_out=r8[:, 1, 0:1]))
                    step(nc.vector.reciprocal(r8[:, 1, 1:2], r8[:, 1, 0:1]))
                    step(nc.vector.tensor_scalar(W, W, r8[:, 1, 1:2], ROUTED_SCALE, ALU.mult, ALU.mult))
                    EN = entry[:, ds(i * 2 + u, 1)].rearrange("p o e c -> p (o e) c")
                    for c in range(3):
                        step(nc.vector.tensor_copy(rwb[:, c], W))
                        ins = nc.vector.tensor_copy(EN[:, :, 2 + c], rwb[:, c])
                        if c < 2:
                            step(nc.vector.tensor_tensor(W, W, rwb[:, c], ALU.subtract))
                    ins.then_inc(S["routed"], 1)

                residual(0)
                residual(1)
                shared_act(0)
                route(0)
                shared_act(1)
                route(1)
                assert step.n[0] == STEPS, step.n[0]

        @block.tensor
        def _(pe):
            pe.wait_ge(S["weights"], NW * 16)
            with pe.Fori(0, TURNS) as i:
                def free(n):
                    pe.wait_ge(S["Te"], i * GR + (n + 1))

                def t8(src, n0):
                    for g in range(2):
                        free(n0 + g)
                        for k in range(4):
                            c = (4 * g + k) * P
                            last = nc.tensor.transpose(psT[:, (n0 + g) % 2, k * P:(k + 1) * P], src[:, c:c + P], ident[:])
                        last.then_inc(S["T"], 1)

                for u in range(2):
                    pe.wait_ge(s_o[u], i * 16 + 16)
                    t8(ot[u], GO[u])
                    pe.wait_ge(S["Te"], i * GR + (GO[u] + 4))
                    pe.wait_ge(S["yout"], i * 2 + (u + 1))
                    for h in range(2):
                        for k in range(KD):
                            last = nc.tensor.matmul(psY[:, 2 * u + h], oT[u][:, k], w_o[:, k, h * 512:(h + 1) * 512],
                                                    start=(k == 0), stop=(k == KD - 1))
                        last.then_inc(S["proj"], 1)
                for u in range(2):
                    pe.wait_ge(S["h2"], i * 2 + (u + 1))
                    t8(h2[u], GHT[u])
                    pe.wait_ge(S["Te"], i * GR + (GHT[u] + 4))
                    pe.wait_ge(S["expR"], i * 2 + (u + 1))
                    for k in range(KD):
                        last = nc.tensor.matmul(psR[:, 0:E], hT[u][:, k], w_r[:, k], start=(k == 0), stop=(k == KD - 1))
                    last.then_inc(S["logit"], 1)
                    pe.wait_ge(S["act"], i * 2 + (u + 1))
                    for k in range(KD):
                        last = nc.tensor.matmul(psG[:], hT[u][:, k], w_g[:, k], start=(k == 0), stop=(k == KD - 1))
                    last.then_inc(S["gu"], 1)
                for u in range(2):
                    pe.wait_ge(S["act"], i * 2 + (u + 2))
                    free(GA[u])
                    for k in range(2):
                        last = nc.tensor.transpose(psT[:, GA[u] % 2, k * P:(k + 1) * P], ga[u][:, k * P:(k + 1) * P], ident[:])
                    last.then_inc(S["T"], 1)
                    pe.wait_ge(S["Te"], i * GR + (GA[u] + 3))
                    for h in range(2):
                        for k in range(2):
                            last = nc.tensor.matmul(psY[:, 2 * u + h], aT[:, k], w_d[:, k, h * 512:(h + 1) * 512],
                                                    start=(k == 0), stop=(k == 1))
                        last.then_inc(S["down"], 1)


def routing_tables(b, a, ident, entry, mask, rank, tab):
    nc = b.nc
    with ExitStack() as ph:
        before = b.sb(ph, "before", [P, P])
        part = b.sb(ph, "partition", [P, 1])
        bb = b.sb(ph, "before_bf", [P, P], BF16)
        ones = b.sb(ph, "ones_bf", [P, P], BF16)
        w = b.sb(ph, "table_work", [P, 12, E])
        one = b.sb(ph, "ones_row", [P, E])
        ci = b.sb(ph, "count_int", [P, E], I32)
        col = b.sb(ph, "columns", [P, 8])
        cl = b.sb(ph, "block_columns", [P, 6])
        ps = b.pb(ph, "ps_rank", [P, 512])
        pc = b.pb(ph, "ps_count", [P, 512])
        pt = b.pb(ph, "ps_table", [P, 2, 512])
        s_ld = b.sem(ph, "t_loaded")
        s_cst = b.sem(ph, "t_const")
        s_rk = b.sem(ph, "t_rank")
        s_col = b.sem(ph, "t_cols")
        s_row = b.sem(ph, "t_rows")
        s_dve = b.sem(ph, "t_dve")
        block = ph.enter_context(nc.Block())

        @block.sync
        def _(sp):
            sp.dma_start(before[:], a["k_before"]).then_inc(s_ld, 16)
            sp.dma_start(part[:], a["k_part"]).then_inc(s_ld, 16)

        @block.gpsimd
        def _(pool):
            pool.wait_ge(s_ld, 32)
            for t in range(NT):
                nc.gpsimd.memset(entry[:, t, :, 0], float(t))
            nc.gpsimd.memset(entry[:, :, :, NPC - 1], 1.0)
            nc.gpsimd.tensor_copy(entry[:, :, :, 1].rearrange("p t e -> p (t e)"), part[:].broadcast_to([P, NT * E]))

        @block.vector
        def _(dve):
            step = chain(dve, s_dve)
            dve.wait_ge(s_ld, 32)
            nc.vector.memset(one[:], 1.0)
            nc.vector.memset(ones[:], 1.0)
            nc.vector.tensor_copy(bb[:], before[:]).then_inc(s_cst, 1)
            dve.wait_ge(s_rk, 2)
            mf = mask[:].rearrange("p t e -> p (t e)")
            rk = rank[:].rearrange("p t e -> p (t e)")
            step(nc.vector.scalar_tensor_tensor(rk, ps[:], 1.0, mf, ALU.add, ALU.mult))
            step(nc.vector.tensor_scalar_add(rk, rk, -1.0))
            cf, nbk, cum, ne, od, cmp, t0, t1, t2, t3 = (w[:, j] for j in range(10))
            step(nc.vector.tensor_scalar_add(cf, pc[:, 0:E], P - 1.0))
            step(nc.vector.tensor_copy(ci[:], cf))
            step(nc.vector.tensor_single_scalar(ci[:], ci[:], 7, ALU.arith_shift_right))
            step(nc.vector.tensor_copy(nbk, ci[:]))
            step(nc.vector.tensor_tensor_scan(cum, one[:], nbk, 0.0, ALU.mult, ALU.add))
            step(nc.vector.tensor_scalar_min(ne, nbk, 1.0))
            step(nc.vector.tensor_tensor_scan(od, one[:], ne, 0.0, ALU.mult, ALU.add))
            lastb, pcl, st, p3 = (col[:, j:j + 1] for j in range(4))
            step(nc.vector.tensor_scalar_add(lastb, cum[:, E - 1:E], -1.0))
            step(nc.vector.tensor_tensor(pcl, part[:], lastb, ALU.min))
            step(nc.vector.tensor_scalar(cmp, cum, pcl, None, ALU.is_le))
            step(nc.vector.tensor_tensor(t0, cmp, nbk, ALU.mult))
            step(nc.vector.tensor_tensor(t1, cmp, ne, ALU.mult))
            step(nc.vector.reduce_sum(cl[:, 0:1], cmp, AX.X))
            step(nc.vector.reduce_sum(st, t0, AX.X))
            step(nc.vector.reduce_sum(cl[:, 2:3], t1, AX.X))
            step(nc.vector.tensor_tensor(cl[:, 1:2], part[:], st, ALU.subtract))
            step(nc.vector.tensor_scalar_min(cl[:, 1:2], cl[:, 1:2], 8.0))
            step(nc.vector.tensor_scalar(t2, od, part[:], None, ALU.is_le))
            step(nc.vector.reduce_sum(cl[:, 3:4], t2, AX.X))
            step(nc.vector.tensor_scalar_add(p3, part[:], -(WS - 1.0)))
            step(nc.vector.tensor_scalar(t3, od, p3, None, ALU.is_le))
            step(nc.vector.tensor_tensor(t3, t3, nbk, ALU.mult))
            step(nc.vector.reduce_sum(cl[:, 4:5], t3, AX.X))
            step(nc.vector.tensor_scalar_min(cl[:, 3:4], cl[:, 3:4], E - 1.0))
            nc.vector.tensor_copy(cl[:, 5:6], lastb).then_inc(s_col, 1)
            dve.wait_ge(s_row, 1)
            for c in range(6):
                nc.vector.tensor_copy(tab[0:1, c, 0:P], pt[0:1, c // 3, (c % 3) * P:(c % 3 + 1) * P])
                step(nc.vector.tensor_copy(tab[0:1, c, P:P + 8],
                                           pt[0:1, c // 3, (c % 3 + 1) * P - 1:(c % 3 + 1) * P].broadcast_to([1, 8])))
            step(nc.vector.tensor_scalar_add(cl[0:1, 0:1], cum[0:1, E - 1:E], 0.0))
            step(nc.vector.tensor_copy(tab[0:1, 5, 0:1], cl[0:1, 0:1]))
            step(nc.vector.tensor_copy(tab[0:1, 5, 1:2], od[0:1, E - 1:E]))

        @block.tensor
        def _(pe):
            pe.wait_ge(s_cst, 1)
            for t in range(NT):
                nc.tensor.matmul(ps[:, t * E:(t + 1) * E], bb[:], mask[:, t], start=True, stop=(t == 0))
                for q in range(t):
                    nc.tensor.matmul(ps[:, t * E:(t + 1) * E], ones[:], mask[:, q], start=False, stop=(q == t - 1))
            for t in range(NT):
                last = nc.tensor.matmul(pc[:, 0:E], ones[:], mask[:, t], start=(t == 0), stop=(t == NT - 1))
            last.then_inc(s_rk, 2)
            pe.wait_ge(s_col, 1)
            for c in range(6):
                last = nc.tensor.matmul(pt[0:1, c // 3, (c % 3) * P:(c % 3 + 1) * P], cl[:, c:c + 1], ident[:],
                                        start=True, stop=True)
            last.then_inc(s_row, 1)


def experts(b, a, ident, entry, rank, tab, h2_d, y_d):
    nc = b.nc
    with ExitStack() as ph:
        wgu = b.sb(ph, "w_gate_up", [P, WS, KD, 2 * FE])
        wdn = b.sb(ph, "w_down", [P, WS, 2, D])
        count = b.sb(ph, "count_row", [P, 9 * P])
        part = b.sb(ph, "partition_p", [P, 2])
        oh = b.sb(ph, "one_hot", [P, NT, P], BF16)
        xg = b.sb(ph, "gathered", [P, D])
        hT = b.sb(ph, "gatheredT", [P, KD, P])
        ga = b.sb(ph, "e_gate_a", [P, FE])
        gb = b.sb(ph, "e_gate_b", [P, FE])
        aT = b.sb(ph, "e_act_T", [P, 2, P])
        yb = b.sb(ph, "e_y", [P, D])
        pc = b.sb(ph, "e_pieces", [P, 8])
        tk = b.sb(ph, "e_token", [P, 4])
        wr = b.sb(ph, "e_weight_ring", [P, 4])
        sr = b.sb(ph, "e_target_ring", [P, 4])
        wn = b.sb(ph, "e_weight", [P, 1])
        ti = b.sb(ph, "e_gather_index", [P, 1], U32)
        si = b.sb(ph, "e_target_index", [P, 1], U32)
        psX = b.pb(ph, "ps_x", [P, 2, 512])
        psG = b.pb(ph, "ps_gu", [P, 512])
        psA = b.pb(ph, "ps_a", [P, 512])
        psY = b.pb(ph, "ps_ye", [P, 2, 512])
        psI = b.pb(ph, "ps_i", [P, 512])
        S = {n: b.sem(ph, "e_" + n) for n in (
            "const", "oh", "pieces", "piecesout", "tok", "gather", "xT", "hTa", "hTd", "gu", "exp", "act", "aTp",
            "aT", "dn", "y0", "y1", "target", "scat", "scatok", "landed", "dve", "zero")}
        s_w = [b.sem(ph, f"e_weights_loaded{u}") for u in range(WS)]
        block = ph.enter_context(nc.Block())

        def read(eng, c, at, hi):
            return eng.value_load(tab[0:1, c, ds(at, 1)], min_val=0, max_val=hi)

        def blocks(eng, body):
            total = eng.value_load(tab[0:1, 5, 0:1], min_val=1, max_val=NBLK - 1)
            with eng.Fori(0, total) as n:
                body(n)
            return total

        @block.sync
        def _(sp):
            sp.dma_start(count[:], a["k_count"]).then_inc(S["const"], 16)
            sp.dma_start(part[:, 0:1], a["k_part"]).then_inc(S["const"], 16)
            loaded = sp.value_load(tab[0:1, 5, 1:2], min_val=1, max_val=E)

            def load(n, u):
                e = read(sp, 3, n, E - 1)
                sp.dma_start(wgu[:, u, :, 0:FE], a["w_exp_gate"][0, ds(e, 1)].rearrange("o (p k) n -> (o p) k n", k=KD)).then_inc(s_w[u], 16)
                sp.dma_start(wgu[:, u, :, FE:], a["w_exp_up"][0, ds(e, 1)].rearrange("o (p k) n -> (o p) k n", k=KD)).then_inc(s_w[u], 16)
                sp.dma_start(wdn[:, u], a["w_exp_down"][0, ds(e, 1)].rearrange("o (k p) n -> p (o k) n", p=P)).then_inc(s_w[u], 16)

            load(0, 0)
            with sp.Fori(0, E // WS) as i:
                for u in range(WS):
                    n = i * WS + (u + 1)
                    with sp.If(n < loaded):
                        done = read(sp, 4, n, NBLK)
                        sp.wait_ge(S["dn"], done * 2 + 1)
                        load(n, (u + 1) % WS)
                        sp.wait_ge(s_w[u], i * 48 + 48)
                        sp.sem_inc(S["landed"], 1)
            for u in range(WS):
                with sp.If(((loaded + (WS - 1)) & (WS - 1)) == u):
                    sp.wait_ge(s_w[u], ((loaded + (WS - 1)) // WS) * 48)
                    sp.sem_inc(S["landed"], 1)

        @block.gpsimd
        def _(pool):
            def gather(n, first=False):
                pool.wait_ge(S["tok"], n + 1)
                if not first:
                    pool.wait_ge(S["xT"], n * 2)
                pool.sem_inc(S["zero"], 1)
                pool.indirect_dma_start(xg[:], None, h2_d, bass.IndirectOffsetOnAxis(ap=ti[:, 0:1], axis=0),
                                        bounds_check=SEQ - 1).then_inc(S["gather"], 16)

            def body(n):
                gather(n + 3)
                pool.wait_ge(S["y0"], n + 1)
                pool.wait_ge(S["y1"], n + 1)
                pool.wait_ge(S["target"], n + 1)
                pool.sem_inc(S["zero"], 1)
                pool.indirect_dma_start(y_d, bass.IndirectOffsetOnAxis(ap=si[:, 0:1], axis=0), yb[:], None,
                                        bounds_check=SEQ + P - 1, compute_op=ALU.add).then_inc(S["scat"], 16)
                pool.wait_ge(S["scat"], n * 16 + 16)
                pool.sem_inc(S["scatok"], 1)

            pool.sem_inc(S["scatok"], 1)
            gather(0, True)
            gather(1)
            gather(2)
            total = blocks(pool, body)
            pool.wait_ge(S["gather"], total * 16 + 48)

        @block.scalar
        def _(act):
            def out_x(n):
                act.wait_ge(S["xT"], n * 2 + 1)
                act.activation(hT[:, 0:4], psX[:, 0].rearrange("p (k n) -> p k n", n=P), ACT.Copy).then_inc(S["hTa"], 1)

            def out_exp(n):
                act.wait_ge(S["gu"], n + 1)
                act.activation(ga[:], psG[:, 0:FE], ACT.Exp, scale=-1.0).then_inc(S["exp"], 1)

            def out_a(n):
                act.wait_ge(S["aTp"], n + 1)
                act.activation(aT[:], psA[:, 0:2 * P].rearrange("p (k n) -> p k n", n=P), ACT.Copy).then_inc(S["aT"], 1)

            def body(n):
                out_exp(n + 1)
                out_x(n + 2)
                act.wait_ge(S["target"], n + 1)
                act.wait_ge(S["dn"], n * 2 + 2)
                act.activation(yb[:, 0:512], psY[:, 0], ACT.Copy, scale=wn[:, 0:1]).then_inc(S["y0"], 1)
                out_a(n + 1)

            out_x(0)
            out_exp(0)
            out_x(1)
            out_a(0)
            blocks(act, body)

        @block.vector
        def _(dve):
            HEAD, STEPS = 1 + 3 * 6 + 3, 3 + 6 + 1
            dve.wait_ge(S["const"], 32)
            first = chain(dve, S["dve"])
            first(nc.vector.tensor_scalar_add(part[:, 1:2], part[:, 0:1], float(SEQ)))

            def one_hot(n, head=False):
                e = read(dve, 0, n, E - 1)
                j = read(dve, 1, n, 8)
                if not head:
                    dve.wait_ge(S["pieces"], n)
                nc.vector.tensor_tensor(oh[:], count[:, ds(j * P, P)].unsqueeze(1).broadcast_to([P, NT, P]),
                                        rank[:, :, ds(e, 1)].broadcast_to([P, NT, P]), ALU.is_equal).then_inc(S["oh"], 1)

            def indices(n, step, head=False):
                dve.wait_ge(S["pieces"], n + 1)
                nc.vector.tensor_copy(pc[:, 0:NPC], psI[:, 0:NPC]).then_inc(S["piecesout"], 1)
                dve.wait_ge(S["piecesout"], n + 1)
                at = n & 3
                W, T = wr[:, ds(at, 1)], sr[:, ds(at, 1)]
                step(nc.vector.scalar_tensor_tensor(tk[:, 0:1], pc[:, 0:1], float(P), pc[:, 1:2], ALU.mult, ALU.add))
                step(nc.vector.tensor_scalar(tk[:, 1:2], pc[:, NPC - 1:NPC], -1.0, 1.0, ALU.mult, ALU.add))
                step(nc.vector.tensor_tensor(tk[:, 1:2], tk[:, 1:2], part[:, 1:2], ALU.mult))
                step(nc.vector.tensor_tensor(T, tk[:, 0:1], tk[:, 1:2], ALU.add))
                step(nc.vector.tensor_tensor(tk[:, 2:3], pc[:, 2:3], pc[:, 3:4], ALU.add))
                step(nc.vector.tensor_tensor(W, tk[:, 2:3], pc[:, 4:5], ALU.add))
                if not head:
                    dve.wait_ge(S["gather"], n * 16)
                nc.vector.tensor_copy(ti[:], tk[:, 0:1]).then_inc(S["tok"], 1)

            def out_x(n):
                dve.wait_ge(S["xT"], n * 2 + 2)
                nc.vector.tensor_copy(hT[:, 4:8], psX[:, 1].rearrange("p (k n) -> p k n", n=P)).then_inc(S["hTd"], 1)

            def gate(n, step):
                dve.wait_ge(S["exp"], n + 1)
                step(nc.vector.tensor_scalar_add(gb[:], ga[:], 1.0))
                step(nc.vector.reciprocal(gb[:], gb[:]))
                step(nc.vector.tensor_tensor(gb[:], gb[:], psG[:, 0:FE], ALU.mult))
                nc.vector.tensor_tensor(ga[:], gb[:], psG[:, FE:2 * FE], ALU.mult).then_inc(S["act"], 1)

            def body(n):
                step = chain(dve, S["dve"], n * STEPS + HEAD)
                one_hot(n + 3)
                gate(n + 1, step)
                indices(n + 3, step)
                out_x(n + 2)
                dve.wait_ge(S["scatok"], n + 1)
                step(nc.vector.tensor_copy(wn[:], wr[:, ds(n & 3, 1)]))
                nc.vector.tensor_copy(si[:], sr[:, ds(n & 3, 1)]).then_inc(S["target"], 1)
                dve.wait_ge(S["dn"], n * 2 + 3)
                nc.vector.tensor_scalar_mul(yb[:, 512:1024], psY[:, 1], wn[:, 0:1]).then_inc(S["y1"], 1)
                assert step.n[0] == STEPS

            one_hot(0, True)
            indices(0, first, True)
            one_hot(1)
            indices(1, first)
            out_x(0)
            one_hot(2)
            indices(2, first)
            gate(0, first)
            out_x(1)
            assert first.n[0] == HEAD
            blocks(dve, body)

        @block.tensor
        def _(pe):
            def pieces(n, head=False):
                e = read(pe, 0, n, E - 1)
                pe.wait_ge(S["oh"], n + 1)
                if not head:
                    pe.wait_ge(S["piecesout"], n)
                for t in range(NT):
                    last = nc.tensor.matmul(psI[:, 0:NPC], oh[:, t], entry[:, t, ds(e, 1)].rearrange("p o c -> p (o c)"),
                                            start=(t == 0), stop=(t == NT - 1))
                last.then_inc(S["pieces"], 1)

            def t_x(n):
                pe.wait_ge(S["gather"], n * 16 + 16)
                for g in range(2):
                    for k in range(4):
                        c = (4 * g + k) * P
                        last = nc.tensor.transpose(psX[:, g, k * P:(k + 1) * P], xg[:, c:c + P], ident[:])
                    last.then_inc(S["xT"], 1)

            def gate_up(n):
                q = read(pe, 2, n, E - 1)
                pe.wait_ge(S["landed"], q + 1)
                pe.wait_ge(S["hTa"], n + 1)
                pe.wait_ge(S["hTd"], n + 1)
                for k in range(KD):
                    last = nc.tensor.matmul(psG[:], hT[:, k], wgu[:, ds(q & (WS - 1), 1), k].rearrange("p o n -> p (o n)"),
                                            start=(k == 0), stop=(k == KD - 1))
                last.then_inc(S["gu"], 1)

            def t_a(n):
                pe.wait_ge(S["act"], n + 1)
                for k in range(2):
                    last = nc.tensor.transpose(psA[:, k * P:(k + 1) * P], ga[:, k * P:(k + 1) * P], ident[:])
                last.then_inc(S["aTp"], 1)

            def body(n):
                pieces(n + 3)
                gate_up(n + 1)
                t_x(n + 2)
                q = read(pe, 2, n, E - 1)
                pe.wait_ge(S["aT"], n + 1)
                pe.wait_ge(S["scatok"], n + 1)
                for h in range(2):
                    for k in range(2):
                        last = nc.tensor.matmul(psY[:, h], aT[:, k], wdn[:, ds(q & (WS - 1), 1), k, h * 512:(h + 1) * 512].rearrange("p o n -> p (o n)"),
                                                start=(k == 0), stop=(k == 1))
                    last.then_inc(S["dn"], 1)
                t_a(n + 1)

            pe.sem_inc(S["dn"], 1)
            pieces(0, True)
            pieces(1)
            t_x(0)
            pieces(2)
            gate_up(0)
            t_x(1)
            t_a(0)
            blocks(pe, body)


def final(b, a, rows, mhalf, x1, y_d, out):
    nc = b.nc
    with ExitStack() as ph:
        yt = b.sb(ph, "y_tiles", [P, NT, D])
        junk = b.sb(ph, "f_square", [P, 2, D], BF16)
        ms = b.sb(ph, "f_mean", [P, 3, NT])
        s_y = [b.sem(ph, f"y_loaded{t}") for t in range(NT)]
        s_sq = b.sem(ph, "f_sq")
        s_rs = b.sem(ph, "f_rs")
        s_pool = b.sem(ph, "f_pool")
        s_o = b.sem(ph, "f_out")
        s_dve = b.sem(ph, "f_dve")
        s_st = b.sem(ph, "f_stored")
        block = ph.enter_context(nc.Block())

        @block.sync
        def _(sp):
            for t in range(NT):
                sp.dma_start(yt[:, t], y_d[t * P:(t + 1) * P, :]).then_inc(s_y[t], 16)
            for t in range(NT):
                sp.wait_ge(s_o, t + 1)
                sp.dma_start(out[0, t * P:(t + 1) * P, :], yt[:, t]).then_inc(s_st, 16)
            sp.wait_ge(s_st, NT * 16)

        @block.scalar
        def _(act):
            for t in range(NT):
                act.wait_ge(s_y[t], 16)
                if t >= 2:
                    act.wait_ge(s_sq, t - 1)
                act.activation(junk[:, t % 2], yt[:, t], ACT.Square, scale=D ** -0.5, accum_out=ms[:, 0, t:t + 1]).then_inc(s_sq, 1)

        @block.gpsimd
        def _(pool):
            for t in range(NT):
                pool.wait_ge(s_sq, t + 1)
                nc.gpsimd.tensor_tensor(ms[:, 1, t:t + 1], ms[:, 0, t:t + 1], mhalf[:, 16:17], ALU.add).then_inc(s_pool, 1)
                pool.wait_ge(s_pool, t + 1)
                nc.gpsimd.tensor_tensor(ms[:, 2, t:t + 1], ms[:, 1, t:t + 1], mhalf[:, 0:1], ALU.pow).then_inc(s_rs, 1)

        @block.vector
        def _(dve):
            step = chain(dve, s_dve)
            for t in range(NT):
                dve.wait_ge(s_rs, t + 1)
                step(nc.vector.scalar_tensor_tensor(yt[:, t], yt[:, t], ms[:, 2, t:t + 1], rows[:, G2], ALU.mult, ALU.mult))
                nc.vector.tensor_tensor(yt[:, t], yt[:, t], x1[:, t], ALU.add).then_inc(s_o, 1)


def ds(start, size):
    return bass.ds(start, size)


def program(nc, a, out):
    b = Build(nc)
    qT_d = nc.dram_tensor("qT_scratch", [KT_N, P, NP * P], F32).ap()
    o_d = nc.dram_tensor("o_scratch", [SEQ, D], F32).ap()
    h2_d = nc.dram_tensor("h2_scratch", [SEQ, D], F32).ap()
    y_d = nc.dram_tensor("y_scratch", [SEQ + P, D], F32).ap()
    with ExitStack() as top:
        ident = b.sb(top, "ident", [P, P])
        rows = b.sb(top, "mod_rows", [P, 8, D])
        nlam = b.sb(top, "neg_lambda", [P, 1])
        mhalf = b.sb(top, "minus_half_eps", [P, 32])
        s_win = b.sem(top, "w_in_loaded")
        with ExitStack() as kv:
            with ExitStack() as ph:
                w_in = ph.enter_context(nc.sbuf_tensor("w_in_sb", [P, KD, INW], F32, side="right"))
                modulation(b, a, ident, rows, nlam, mhalf, w_in, s_win)
                kT = b.sb(kv, "kT", [P, 5, KEYS])
                vv = b.sb(kv, "values", [P, KT_N, VW])
                projections(b, a, ident, rows, mhalf, w_in, s_win, kT, vv, qT_d)
            attention(b, a, ident, nlam, mhalf, kT, vv, qT_d, o_d)
        x1 = b.sb(top, "x1", [P, NT, D])
        entry = b.sb(top, "entries", [P, NT, E, NPC], BF16)
        mask = b.sb(top, "chosen", [P, NT, E], BF16)
        output_and_router(b, a, ident, rows, mhalf, x1, entry, mask, o_d, h2_d, y_d)
        rank = b.sb(top, "rank", [P, NT, E])
        tab = b.sb(top, "block_table", [1, 6, P + 8], I32)
        routing_tables(b, a, ident, entry, mask, rank, tab)
        experts(b, a, ident, entry, rank, tab, h2_d, y_d)
        final(b, a, rows, mhalf, x1, y_d, out)


def rope_table():
    n = HD // 4
    inv = np.float32(10000.0) ** (-np.arange(n, dtype=np.float32) / np.float32(n))
    row = np.repeat(np.arange(SEQ // GRID_W), GRID_W).astype(np.float32)[:, None] * inv
    col = np.tile(np.arange(GRID_W), SEQ // GRID_W).astype(np.float32)[:, None] * inv
    t = np.zeros((KEYS, 2, HD), np.float32)
    t[:, 0] = 1.0
    t[CTX:, 0] = np.concatenate([np.cos(row)] * 2 + [np.cos(col)] * 2, axis=1)
    t[CTX:, 1] = np.concatenate([-np.sin(row), np.sin(row), -np.sin(col), np.sin(col)], axis=1)
    return t


def kernel(**inputs):
    import concourse.bacc as bacc
    from concourse.bass_utils import run_bass_kernel_spmd

    nc = bacc.Bacc("TRN2", target_bir_lowering=False, num_devices=1)
    host = {k: np.ascontiguousarray(v) for k, v in inputs.items() if k not in ("x", "ctx")}
    host["tokens"] = np.concatenate([np.asarray(inputs["ctx"])[0], np.asarray(inputs["x"])[0]], axis=0)
    select = np.zeros((2, 2, P), np.float32)
    select[0, 0] = select[1, 1] = 1.0
    tok = np.arange(P)
    host["k_ident"] = np.eye(P, dtype=np.float32)
    host["k_select"] = select
    host["k_rope"] = rope_table()
    host["k_before"] = (tok[:, None] < tok[None, :]).astype(np.float32)
    host["k_count"] = np.ascontiguousarray(np.broadcast_to(np.arange(9 * P, dtype=np.float32), (P, 9 * P)))
    host["k_part"] = np.arange(P, dtype=np.float32)[:, None]
    arrays, a = {}, {}
    for name, v in host.items():
        v = np.ascontiguousarray(v)
        arrays[f"in_{name}"] = v
        a[name] = nc.dram_tensor(f"in_{name}", v.shape, mybir.dt.from_np(v.dtype), kind="ExternalInput").ap()
    out = nc.dram_tensor("out", (1, SEQ, D), F32, kind="ExternalOutput").ap()
    program(nc, a, out)
    r = run_bass_kernel_spmd(nc, [arrays], core_ids=[0])
    return r.results[0]["out"]
```

```python
import math
from contextlib import ExitStack

import numpy as np

import concourse.bass as bass
from concourse import mybir

F32 = mybir.dt.float32
BF16 = mybir.dt.bfloat16
I32 = mybir.dt.int32
U32 = mybir.dt.uint32
ALU = mybir.AluOpType
ACT = mybir.ActivationFunctionType
AX = mybir.AxisListType

P = 128
D = 1024
KD = D // P
SEQ, CTX = 1024, 256
NT, NC = SEQ // P, CTX // P
KT_N = NT + NC
KEYS = SEQ + CTX
HD = 64
DH, GH, GKV = 4, 8, 2
NP = 8
NH = 2 * NP
QKW = 1664
NHEADS = QKW // HD
VW = 640
INW = 2304
E, FE = 64, 256
NG, TOPG, TOPK = 8, 4, 8
GRID_W = 64
ROUTED_SCALE = 2.5
LAM_INIT = 0.8 - 0.6 * math.exp(-0.3 * 0)
EPS = 1e-6
BIG = 1e30
DIFF_V = 2 * HD
NBLK = SEQ * TOPK // P + E
WS = 4
NPC = 6
SCALE = HD ** -0.5



class Build:

    def __init__(self, nc):
        self.nc = nc

    def sb(self, st, name, shape, dt=F32):
        return st.enter_context(self.nc.sbuf_tensor(name, shape, dt))

    def pb(self, st, name, shape, dt=F32):
        return st.enter_context(self.nc.psum_tensor(name, shape, dt))

    def sem(self, st, name):
        return st.enter_context(self.nc.semaphore(name))


def chain(eng, s, start=0):
    n = [0]

    def step(ins):
        n[0] += 1
        ins.then_inc(s, 1)
        eng.wait_ge(s, start + n[0])
    step.n = n
    return step


A1, B1, A1C, B1C, A2, B2, G1, G2 = range(8)


def modulation(b, a, ident, rows, nlam, mhalf, w_in, s_win):
    nc = b.nc
    SL, SW = 2, 512
    NS = 6 * D // SW
    with ExitStack() as ph:
        ring = b.sb(ph, "w_mod_ring", [P, SL, KD, SW])
        cs = b.sb(ph, "c_cols", [P, 2, KD])
        sg = b.sb(ph, "c_sig", [P, 2, KD])
        silu = b.sb(ph, "c_silu", [P, KD, 2])
        mrow = b.sb(ph, "mod_row", [2, 6, D])
        brow = b.sb(ph, "b_mod_row", [2, 6 * D])
        grow = b.sb(ph, "gain_row", [2, 4, D])
        sel = b.sb(ph, "row_select", [2, 2, P])
        lamv = b.sb(ph, "lambda_vecs", [P, 4, HD])
        lamj = b.sb(ph, "lambda_prod", [P, 2, HD])
        lamt = b.sb(ph, "lambda_terms", [P, 8])
        ps = b.pb(ph, "ps_mod", [P, 8, 512])
        s_c = b.sem(ph, "c_loaded")
        s_small = b.sem(ph, "small_loaded")
        s_slab = [b.sem(ph, f"slab_loaded{u}") for u in range(SL)]
        s_exp = b.sem(ph, "m_exp")
        s_silu = b.sem(ph, "silu_ready")
        s_lam = b.sem(ph, "lambda_sums")
        s_prod = b.sem(ph, "slab_multiplied")
        s_row = b.sem(ph, "row_part_out")
        s_rows = b.sem(ph, "rows_ready")
        s_bc = b.sem(ph, "row_broadcast")
        s_out = b.sem(ph, "broadcast_out")
        s_dve = b.sem(ph, "m_dve")
        block = ph.enter_context(nc.Block())
        NSMALL = 2 + 1 + 4 + 4

        @block.gpsimd
        def _(pool):
            nc.gpsimd.memset(mhalf[:, 0:16], -0.5)
            nc.gpsimd.memset(mhalf[:, 16:32], EPS)

        @block.sync
        def _(sp):
            sp.dma_start(cs[:, 0, :], a["c"].rearrange("o (p k) -> (o p) k", k=KD)).then_inc(s_c, 16)
            sp.dma_start(cs[:, 1, :], a["c_ctx"].rearrange("(p k) -> p k", k=KD)).then_inc(s_c, 16)
            wm = a["w_mod"][0].rearrange("(p k) n -> p k n", k=KD)
            for u in range(SL):
                sp.dma_start(ring[:, u], wm[:, :, u * SW:(u + 1) * SW]).then_inc(s_slab[u], 16)
            with sp.Fori(1, NS // SL) as i:
                for u in range(SL):
                    sp.wait_ge(s_prod, i * SL + (u - SL + 1))
                    sp.dma_start(ring[:, u], wm[:, :, ds(i * (SL * SW) + u * SW, SW)]).then_inc(s_slab[u], 16)
            sp.dma_start(w_in[:], a["w_in"][0].rearrange("(k p) n -> p k n", p=P)).then_inc(s_win, 16)

        @block.scalar
        def _(act):
            act.dma_start(ident[:], a["k_ident"]).then_inc(s_small, 16)
            act.dma_start(sel[:], a["k_select"]).then_inc(s_small, 16)
            act.dma_start(brow[:], a["b_mod"].broadcast_to([2, 6 * D])).then_inc(s_small, 16)
            for j, g in enumerate(("g_pre_mix", "g_post_mix", "g_pre_ffn", "g_post_ffn")):
                act.dma_start(grow[:, j], a[g].broadcast_to([2, D])).then_inc(s_small, 16)
            for j, v in enumerate(("lambda_q1", "lambda_k1", "lambda_q2", "lambda_k2")):
                act.dma_start(lamv[:, j], a[v].broadcast_to([P, HD])).then_inc(s_small, 16)
            act.wait_ge(s_c, 32)
            act.activation(sg[:], cs[:], ACT.Exp, scale=-1.0).then_inc(s_exp, 1)
            act.wait_ge(s_lam, 1)
            act.activation(lamt[:, 2:4], lamt[:, 0:2], ACT.Exp).then_inc(s_exp, 1)
            for n in range(1, 16, 2):
                act.wait_ge(s_bc, n + 1)
                r, h = divmod(n, 2)
                act.activation(rows[:, r, h * 512:(h + 1) * 512], ps[:, n % 8], ACT.Copy).then_inc(s_out, 1)

        @block.vector
        def _(dve):
            step = chain(dve, s_dve)
            dve.wait_ge(s_c, 32)
            dve.wait_ge(s_exp, 1)
            step(nc.vector.tensor_scalar_add(sg[:], sg[:], 1.0))
            step(nc.vector.reciprocal(sg[:], sg[:]))
            nc.vector.tensor_tensor(silu[:].rearrange("p k c -> p c k"), sg[:], cs[:], ALU.mult).then_inc(s_silu, 1)
            dve.wait_ge(s_small, NSMALL * 16)
            step(nc.vector.tensor_tensor(lamj[:, 0], lamv[:, 0], lamv[:, 1], ALU.mult))
            step(nc.vector.tensor_tensor(lamj[:, 1], lamv[:, 2], lamv[:, 3], ALU.mult))
            nc.vector.tensor_reduce(lamt[:, 0:2], lamj[:], AX.X, ALU.add).then_inc(s_lam, 1)
            dve.wait_ge(s_exp, 2)
            step(nc.vector.tensor_tensor(lamt[:, 4:5], lamt[:, 3:4], lamt[:, 2:3], ALU.subtract))
            step(nc.vector.tensor_scalar_add(nlam[:], lamt[:, 4:5], -LAM_INIT))
            mflat = mrow[:].rearrange("c s d -> c (s d)")
            with dve.Fori(0, NS // SL) as i:
                for u in range(SL):
                    dve.wait_ge(s_prod, i * SL + u + 1)
                    at = i * (SL * SW) + u * SW
                    nc.vector.tensor_tensor(mflat[:, ds(at, SW)], ps[0:2, u], brow[:, ds(at, SW)], ALU.add).then_inc(s_row, 1)
            dve.wait_ge(s_row, NS)
            nc.vector.scalar_tensor_tensor(mrow[:, 1], mrow[:, 1], 1.0, grow[:, 0], ALU.add, ALU.mult)
            nc.vector.scalar_tensor_tensor(mrow[:, 4], mrow[:, 4], 1.0, grow[:, 2], ALU.add, ALU.mult)
            nc.vector.tensor_tensor(mrow[:, 2], mrow[:, 2], grow[:, 1], ALU.mult)
            nc.vector.tensor_tensor(mrow[:, 5], mrow[:, 5], grow[:, 3], ALU.mult).then_inc(s_rows, 1)
            for n in range(0, 16, 2):
                dve.wait_ge(s_bc, n + 1)
                r, h = divmod(n, 2)
                nc.vector.tensor_copy(rows[:, r, h * 512:(h + 1) * 512], ps[:, n % 8]).then_inc(s_out, 1)

        @block.tensor
        def _(pe):
            pe.wait_ge(s_silu, 1)
            with pe.Fori(0, NS // SL) as i:
                for u in range(SL):
                    pe.wait_ge(s_slab[u], i * 16 + 16)
                    if u == 0:
                        with pe.If(i > 0):
                            pe.wait_ge(s_row, i * SL)
                            pe.nop()
                    for k in range(KD):
                        last = nc.tensor.matmul(ps[0:2, u], silu[:, k], ring[:, u, k], start=(k == 0), stop=(k == KD - 1))
                    last.then_inc(s_prod, 1)
            pe.wait_ge(s_rows, 1)
            srcs = [(1, 0), (0, 0), (1, 1), (0, 1), (4, 0), (3, 0), (2, 0), (5, 0)]
            for n in range(16):
                r, h = divmod(n, 2)
                src, who = srcs[r]
                if n >= 8:
                    pe.wait_ge(s_out, 8)
                nc.tensor.matmul(ps[:, n % 8], sel[:, who], mrow[:, src, h * 512:(h + 1) * 512],
                                 start=True, stop=True).then_inc(s_bc, 1)


def projections(b, a, ident, rows, mhalf, w_in, s_win, kT, vv, qT_d):
    nc = b.nc
    TURNS = KT_N // 2
    with ExitStack() as ph:
        xt = [b.sb(ph, f"x_tile{u}", [P, D]) for u in range(2)]
        hT = [b.sb(ph, f"hT{u}", [P, KD, P]) for u in range(2)]
        qk = b.sb(ph, "qk_rows", [P, QKW])
        t1 = b.sb(ph, "rope_a", [P, QKW])
        t2 = b.sb(ph, "rope_b", [P, QKW])
        rt = [b.sb(ph, f"rope_table{u}", [P, 2, HD]) for u in range(2)]
        junk = b.sb(ph, "square_out", [P, D], BF16)
        ssq = b.sb(ph, "sum_squares", [P, 2, 2])
        hss = b.sb(ph, "head_squares", [P, 32])
        gq = b.sb(ph, "q_gain", [P, HD])
        gk = b.sb(ph, "k_gain", [P, HD])
        qTs = b.sb(ph, "qT_stage", [P, NP, P])
        psT = b.pb(ph, "ps_transpose", [P, 3, 512])
        psC = b.pb(ph, "ps_chunk", [P, 5, 512])
        s_x = [b.sem(ph, f"x_loaded{u}") for u in range(2)]
        s_rt = [b.sem(ph, f"rope_loaded{u}") for u in range(2)]
        s_gain = b.sem(ph, "gain_loaded")
        s_sq = b.sem(ph, "sum_square")
        s_h = b.sem(ph, "h_ready")
        s_T = b.sem(ph, "group_transposed")
        s_Te = b.sem(ph, "group_out")
        s_ch = b.sem(ph, "chunk_done")
        s_che = b.sem(ph, "chunk_out")
        s_rh = b.sem(ph, "h_rstd")
        s_hv = b.sem(ph, "head_mean_square")
        s_rr = b.sem(ph, "head_rstd")
        s_pool = b.sem(ph, "p_pool")
        s_rope = b.sem(ph, "rope_done")
        s_qd = b.sem(ph, "qT_stored")
        s_dve = b.sem(ph, "p_dve")
        block = ph.enter_context(nc.Block())
        CH = [(1024, 512, [(0, 512, "v", 0)]), (512, 512, [(0, 512, "qk", 1024)]),
              (2048, 256, [(0, 128, "qk", 1536), (128, 128, "v", 512)]),
              (0, 512, [(0, 512, "qk", 0)]), (1536, 512, [(0, 512, "gq", 512)])]
        HG, QG = (0, 6), (2, 8)
        NGR = 12

        def skipped(i, c):
            return isinstance(i, int) and i == 0 and c >= 3

        def first_qk(i, u):
            return TURNS * NGR + 4 * u if isinstance(i, int) and i == TURNS - 1 else (i + 1) * NGR + QG[u]

        QKG = [([1024 + j * P for j in range(4)], "k", 0), ([1536], "k", 4),
               ([j * P for j in range(4)], "q", 0), ([512 + j * P for j in range(4)], "q", 4)]
        xa, rope = a["tokens"], a["k_rope"]

        @block.sync
        def _(sp):
            sp.dma_start(gq[:], a["q_norm_g"].broadcast_to([P, HD])).then_inc(s_gain, 16)
            sp.dma_start(gk[:], a["k_norm_g"].broadcast_to([P, HD])).then_inc(s_gain, 16)
            for u in range(2):
                sp.dma_start(xt[u][:], xa[u * P:(u + 1) * P, :]).then_inc(s_x[u], 16)
                sp.dma_start(rt[u][:], rope[u * P:(u + 1) * P]).then_inc(s_rt[u], 16)

            def store(i, u):
                sp.wait_ge(s_Te, first_qk(i, u) + 4)
                sp.dma_start(qT_d[ds(i * 2 + u, 1)].rearrange("o p n -> (o p) n"),
                             qTs[:].rearrange("p j n -> p (j n)")).then_inc(s_qd, 16)

            def turn(i, first=False):
                for u in range(2):
                    sp.wait_ge(s_T, i * NGR + (HG[u] + 2))
                    sp.dma_start(xt[u][:], xa[ds(i * (2 * P) + (2 + u) * P, P), :]).then_inc(s_x[u], 16)
                    if not first:
                        store(i - 1, u)
                for u in range(2):
                    sp.wait_ge(s_rope, i * 2 + (u + 1))
                    sp.dma_start(rt[u][:], rope[ds(i * (2 * P) + (2 + u) * P, P)]).then_inc(s_rt[u], 16)

            turn(0, True)
            with sp.Fori(1, TURNS - 1) as i:
                turn(i)
            for t in (TURNS - 2, TURNS - 1):
                for u in range(2):
                    store(t, u)
            sp.wait_ge(s_qd, KT_N * 16)

        @block.scalar
        def _(act):
            def square(i, u):
                act.wait_ge(s_x[u], i * 16 + 16)
                if not (isinstance(i, int) and i + u == 0):
                    act.wait_ge(s_sq, i * 2 + u)
                act.activation(junk[:], xt[u][:], ACT.Square, scale=D ** -0.5, accum_out=ssq[:, u, 0:1]).then_inc(s_sq, 1)

            def out_h(i, u):
                for g in range(2):
                    act.wait_ge(s_T, i * NGR + (HG[u] + g + 1))
                    act.activation(hT[u][:, 4 * g:4 * g + 4], psT[:, (HG[u] + g) % 3].rearrange("p (k n) -> p k n", k=4),
                                   ACT.Copy).then_inc(s_Te, 5 if isinstance(i, int) and i == 0 and g == 1 else 1)

            def out_chunk(i, u, c):
                if skipped(i, c):
                    return
                act.wait_ge(s_ch, i * 10 + (5 * u + c + 1))
                if c == 1 and u == 1:
                    act.wait_ge(s_rope, i * 2 + 1)
                if c == 1 and u == 0 and not (isinstance(i, int) and i == 0):
                    act.wait_ge(s_rope, i * 2)
                for o, w, kind, at in CH[c][2]:
                    src = psC[:, c, o:o + w]
                    if kind == "gq":
                        src = src.rearrange("p (a j d) -> p a j d", a=2, d=HD)
                        dst = qk[:, at:at + w].rearrange("p (j a d) -> p a j d", a=2, d=HD)
                    elif kind == "qk":
                        dst = qk[:, at:at + w]
                    else:
                        dst = vv[:, ds(i * 2 + u, 1), at:at + w].rearrange("p o n -> p (o n)")
                    ins = act.activation(dst, src, ACT.Copy)
                ins.then_inc(s_che, 3 if skipped(i, 3) and c == 2 else 1)

            def out_qk(i, u, first=False):
                for g, (cols, kind, at) in enumerate(QKG):
                    n = g + (4 * u if isinstance(i, int) and i == TURNS - 1 else QG[u])
                    act.wait_ge(s_T, first_qk(i, u) + (g + 1))
                    w = len(cols) * P
                    src = psT[:, n % 3, 0:w].rearrange("p (k n) -> p k n", n=P)
                    if kind == "k":
                        dst = kT[:, at:at + len(cols), ds(i * (2 * P) + u * P, P)]
                    else:
                        dst = qTs[:, at:at + 4]
                        if at == 0 and (u == 1 or not first):
                            act.wait_ge(s_qd, i * 32 + 16 * u)
                    act.activation(dst, src, ACT.Copy).then_inc(s_Te, 1)

            def turn(i, first=False, second=False, last=False):
                for u in range(2):
                    out_h(i, u)
                    if u == 1 and not last:
                        square(i + 1, 0)
                    if not first:
                        out_qk(i - 1, u, second)
                    for c in range(5):
                        out_chunk(i, u, c)
                        if c == 2 and u == 1 and not last:
                            square(i + 1, 1)

            square(0, 0)
            square(0, 1)
            turn(0, first=True)
            turn(1, second=True)
            with act.Fori(2, TURNS - 1) as i:
                turn(i)
            turn(TURNS - 1, last=True)
            out_qk(TURNS - 1, 0)
            out_qk(TURNS - 1, 1)

        @block.gpsimd
        def _(pool):
            def rstd_h(i, u, own):
                pool.wait_ge(s_sq, i * 2 + (u + 1))
                nc.gpsimd.tensor_tensor(ssq[:, u, 1:2], ssq[:, u, 0:1], mhalf[:, 16:17], ALU.add).then_inc(s_pool, 1)
                pool.wait_ge(s_pool, own)
                nc.gpsimd.tensor_tensor(ssq[:, u, 1:2], ssq[:, u, 1:2], mhalf[:, 0:1], ALU.pow).then_inc(s_rh, 1)

            def rstd_heads(i, u, own):
                pool.wait_ge(s_hv, i * 2 + (u + 1))
                nc.gpsimd.tensor_tensor(hss[:, 16:26], hss[:, 0:10], mhalf[:, 16:26], ALU.add).then_inc(s_pool, 1)
                pool.wait_ge(s_pool, own)
                nc.gpsimd.tensor_tensor(hss[:, 16:26], hss[:, 16:26], mhalf[:, 0:10], ALU.pow).then_inc(s_rr, 1)

            def turn(i, last):
                rstd_heads(i, 0, i * 4 + 3)
                if not last:
                    rstd_h(i + 1, 0, i * 4 + 4)
                    rstd_h(i + 1, 1, i * 4 + 5)
                rstd_heads(i, 1, i * 4 + (4 if last else 6))

            rstd_h(0, 0, 1)
            rstd_h(0, 1, 2)
            with pool.Fori(0, TURNS - 1) as i:
                turn(i, False)
            turn(TURNS - 1, True)

        @block.vector
        def _(dve):
            HEAD, STEPS = 3, 2 * (1 + 6 + 1)

            def make_h(step, u, i):
                dve.wait_ge(s_rh, i * 2 + (u + 1))
                sc = ssq[:, u, 1:2]
                ra, rb = (A1C, B1C) if isinstance(i, int) and i == 0 else (A1, B1)
                step(nc.vector.scalar_tensor_tensor(xt[u][:], xt[u][:], sc, rows[:, ra], ALU.mult, ALU.mult))
                nc.vector.tensor_tensor(xt[u][:], xt[u][:], rows[:, rb], ALU.add).then_inc(s_h, 1)

            def rotary(step, u, i):
                dve.wait_ge(s_che, i * 10 + (5 * u + 5))
                ctx = isinstance(i, int) and i == 0
                if u == 1:
                    dve.wait_ge(s_T, first_qk(i, 0) + 4)
                elif not ctx:
                    dve.wait_ge(s_T, i * NGR + (QG[1] + 4))
                normed = [(1536, 2, gk, 8), (512, 8, gq, 0)][:1 if ctx else 2]
                at0 = 1024 if ctx else 0
                nh0 = (QKW - at0) // HD
                for at, nh, gain, hs in normed:
                    X = qk[:, at:at + nh * HD].rearrange("p (h d) -> p h d", d=HD)
                    J = t2[:, at:at + nh * HD].rearrange("p (h d) -> p h d", d=HD)
                    step(nc.vector.scalar_tensor_tensor(J, X, 1.0 / HD, X, ALU.mult, ALU.mult))
                    ins = nc.vector.tensor_reduce(hss[:, hs:hs + nh], J, AX.X, ALU.add)
                ins.then_inc(s_hv, 1)
                dve.wait_ge(s_rr, i * 2 + (u + 1))
                for at, nh, gain, hs in normed:
                    X = qk[:, at:at + nh * HD].rearrange("p (h d) -> p h d", d=HD)
                    r = hss[:, 16 + hs:16 + hs + nh]
                    step(nc.vector.tensor_tensor(X, X, r.unsqueeze(2).broadcast_to([P, nh, HD]), ALU.mult))
                    step(nc.vector.tensor_tensor(X, X, gain[:].unsqueeze(1).broadcast_to([P, nh, HD]), ALU.mult))
                dve.wait_ge(s_rt[u], i * 16 + 16)
                cosb = rt[u][:, 0:1, :].broadcast_to([P, nh0, HD])
                nc.vector.tensor_tensor(t1[:, at0:].rearrange("p (h d) -> p h d", d=HD),
                                        qk[:, at0:].rearrange("p (h d) -> p h d", d=HD), cosb, ALU.mult)
                for f in range(2):
                    X5 = qk[:, at0:].rearrange("p (h f s d) -> p f h s d", f=2, s=2, d=16)[:, f]
                    T5 = t2[:, at0:].rearrange("p (h f s d) -> p f h s d", f=2, s=2, d=16)[:, f]
                    S5 = rt[u][:, 1, :].rearrange("p (f s d) -> p f s d", f=2, s=2)[:, f]
                    for s_ in range(2):
                        ins = nc.vector.tensor_tensor(T5[:, :, s_], X5[:, :, 1 - s_],
                                                      S5[:, s_:s_ + 1].broadcast_to([P, nh0, 16]), ALU.mult)
                step(ins)
                nc.vector.tensor_tensor(t1[:, at0:], t1[:, at0:], t2[:, at0:], ALU.add).then_inc(s_rope, 1)

            def turn(i, last, base):
                step = chain(dve, s_dve, base)
                rotary(step, 0, i)
                if not last:
                    make_h(step, 0, i + 1)
                    make_h(step, 1, i + 1)
                rotary(step, 1, i)
                assert step.n[0] == (10 if isinstance(i, int) and i == 0 else 14 if last else STEPS), step.n[0]

            dve.wait_ge(s_gain, 32)
            step = chain(dve, s_dve)
            nc.vector.memset(t1[:, 0:1024], 0.0)
            step(nc.vector.memset(hss[:], 1.0))
            make_h(step, 0, 0)
            make_h(step, 1, 0)
            turn(0, False, HEAD)
            with dve.Fori(1, TURNS - 1) as i:
                turn(i, False, i * STEPS + (HEAD - 6))
            turn(TURNS - 1, True, (TURNS - 1) * STEPS + (HEAD - 6))

        @block.tensor
        def _(pe):
            def bank_free(i, n):
                if isinstance(i, int) and i * NGR + n < 3:
                    return
                pe.wait_ge(s_Te, i * NGR + (n - 2))

            def t_h(i, u):
                pe.wait_ge(s_h, i * 2 + (u + 1))
                for g in range(2):
                    bank_free(i, HG[u] + g)
                    for k in range(4):
                        c = (4 * g + k) * P
                        last = nc.tensor.transpose(psT[:, (HG[u] + g) % 3, k * P:(k + 1) * P], xt[u][:, c:c + P], ident[:])
                    last.then_inc(s_T, 5 if isinstance(i, int) and i == 0 and g == 1 else 1)

            def chunks(i, u):
                for c, (src, w, _) in enumerate(CH):
                    if skipped(i, c):
                        continue
                    if c == 0:
                        pe.wait_ge(s_Te, i * NGR + (HG[u] + 2))
                    if not (isinstance(i, int) and i == 0 and u == 0):
                        pe.wait_ge(s_che, i * 10 + (5 * (u - 1) + c + 1))
                    for k in range(KD):
                        last = nc.tensor.matmul(psC[:, c, 0:w], hT[u][:, k], w_in[:, k, src:src + w],
                                                start=(k == 0), stop=(k == KD - 1))
                    last.then_inc(s_ch, 3 if skipped(i, 3) and c == 2 else 1)

            def t_qk(i, u):
                pe.wait_ge(s_rope, i * 2 + (u + 1))
                for g, (cols, _, _) in enumerate(QKG):
                    n = g + (4 * u if isinstance(i, int) and i == TURNS - 1 else QG[u])
                    pe.wait_ge(s_Te, first_qk(i, u) + (g - 2))
                    for k, c in enumerate(cols):
                        last = nc.tensor.transpose(psT[:, n % 3, k * P:(k + 1) * P], t1[:, c:c + P], ident[:])
                    last.then_inc(s_T, 1)

            def turn(i, first=False):
                for u in range(2):
                    t_h(i, u)
                    if not first:
                        t_qk(i - 1, u)
                    chunks(i, u)

            pe.wait_ge(s_win, 16)
            turn(0, True)
            with pe.Fori(1, TURNS) as i:
                turn(i)
            t_qk(TURNS - 1, 0)
            t_qk(TURNS - 1, 1)


def attention(b, a, ident, nlam, mhalf, kT, vv, qT_d, o_d):
    nc = b.nc
    CW = [(0, 512), (512, 512), (1024, 256)]
    with ExitStack() as ph:
        qT = b.sb(ph, "qT", [P, NP, P])
        pr = b.sb(ph, "probs", [P, 2, KEYS])
        pT = b.sb(ph, "probsT", [P, 2, KT_N, P])
        mx = b.sb(ph, "chunk_max", [P, 4, 4])
        nb = b.sb(ph, "neg_max", [P, 4])
        sm = b.sb(ph, "chunk_sum", [P, 4, 4])
        rs = b.sb(ph, "row_scale", [P, 8])
        o1 = b.sb(ph, "o_first", [P, DIFF_V])
        o2 = b.sb(ph, "o_diff", [P, DIFF_V])
        oj = b.sb(ph, "o_square", [P, DIFF_V])
        ob = b.sb(ph, "o_tile", [P, D])
        sg = b.sb(ph, "sub_gain", [P, DIFF_V])
        psS = b.pb(ph, "ps_scores", [P, 3, 512])
        psP = b.pb(ph, "ps_probsT", [P, 3, 512])
        psO = b.pb(ph, "ps_out", [P, 2, 512])
        s_q = [b.sem(ph, f"qT_loaded{h}") for h in range(2)]
        s_g = b.sem(ph, "sub_gain_loaded")
        s_qk = b.sem(ph, "scores_chunk")
        s_nb = b.sem(ph, "neg_max_ready")
        s_exp = b.sem(ph, "probs_chunk")
        s_tp = b.sem(ph, "probsT_chunk")
        s_pta = b.sem(ph, "probsT_by_act")
        s_ptd = b.sem(ph, "probsT_by_dve")
        s_pv = b.sem(ph, "pv_done")
        s_of = b.sem(ph, "o_bank_read")
        s_ov = b.sem(ph, "o_mean_square")
        s_or = b.sem(ph, "o_rstd")
        s_ob = b.sem(ph, "o_part")
        s_od = b.sem(ph, "o_stored")
        s_obfree = b.sem(ph, "o_tile_free")
        s_carry = b.sem(ph, "a_carry")
        s_dve = b.sem(ph, "a_dve")
        block = ph.enter_context(nc.Block())
        C3 = 3 * NH

        def half(tile, h):
            return qT_d[ds(tile, 1)].rearrange("o p n -> (o p) n")[:, h * 512:(h + 1) * 512]

        @block.sync
        def _(sp):
            sp.dma_start(sg[:], a["subln_g"].broadcast_to([P, DIFF_V])).then_inc(s_g, 16)
            for h in range(2):
                sp.dma_start(qT[:, 4 * h:4 * h + 4].rearrange("p j n -> p (j n)"), half(NC, h)).then_inc(s_q[h], 16)
            with sp.Fori(0, NT - 1) as i:
                for h in range(2):
                    sp.wait_ge(s_qk, i * C3 + (h + 1) * (C3 // 2))
                    sp.dma_start(qT[:, 4 * h:4 * h + 4].rearrange("p j n -> p (j n)"), half(i + (NC + 1), h)).then_inc(s_q[h], 16)

        @block.gpsimd
        def _(pool):
            pool.sem_inc(s_obfree, 1)
            with pool.Fori(0, NT) as i:
                for p in range(DH):
                    pool.wait_ge(s_ov, i * DH + (p + 1))
                    nc.gpsimd.tensor_tensor(rs[:, 5:6], rs[:, 3:4], mhalf[:, 0:1], ALU.pow).then_inc(s_or, 1)
                pool.wait_ge(s_ob, i * DH + DH)
                pool.wait_ge(s_of, i * NH + (NH + 2))
                pool.sem_inc(s_carry, 1)
                pool.dma_start(o_d[ds(i * P, P), :], ob[:]).then_inc(s_od, 16)
                pool.wait_ge(s_od, i * 16 + 16)
                pool.sem_inc(s_obfree, 1)

        @block.scalar
        def _(act):
            act.sem_inc(s_exp, 3)
            with act.Fori(0, NT) as i:
                def exps(k):
                    act.wait_ge(s_nb, i * NH + (k + 1))
                    for j, (o, w) in enumerate(CW):
                        act.activation(pr[:, k % 2, o:o + w], psS[:, j, 0:w], ACT.Exp, bias=nb[:, k % 4:k % 4 + 1],
                                       scale=SCALE, accum_out=sm[:, k % 4, j:j + 1]).then_inc(s_exp, 1)

                exps(0)
                for k in range(NH):
                    for j in (0, 2):
                        o, w = CW[j]
                        act.wait_ge(s_tp, i * C3 + (3 * k + j + 1))
                        act.activation(pT[:, k % 2, o // P:(o + w) // P], psP[:, j, 0:w].rearrange("p (t n) -> p t n", n=P),
                                       ACT.Copy).then_inc(s_pta, 1)
                    if k + 1 < NH:
                        exps(k + 1)

        @block.vector
        def _(dve):
            dve.sem_inc(s_of, 2)
            dve.wait_ge(s_g, 16)
            first = chain(dve, s_dve)
            first(nc.vector.tensor_scalar_mul(sg[:], sg[:], 1.0 - LAM_INIT))
            STEPS = NH * 3 + DH * (2 + 3) + GH * 2
            with dve.Fori(0, NT) as i:
                step = chain(dve, s_dve, i * STEPS + 1)

                def maxes(k):
                    for j, (o, w) in enumerate(CW):
                        dve.wait_ge(s_qk, i * C3 + (3 * k + j + 1))
                        ins = nc.vector.reduce_max(mx[:, k % 4, j:j + 1], psS[:, j, 0:w], AX.X)
                        if j == 1:
                            step(ins)
                    step(ins)
                    step(nc.vector.reduce_max(mx[:, k % 4, 3:4], mx[:, k % 4, 0:3], AX.X))
                    nc.vector.tensor_scalar_mul(nb[:, k % 4:k % 4 + 1], mx[:, k % 4, 3:4], -SCALE).then_inc(s_nb, 1)

                def finish(k):
                    p, h = divmod(k, 2)
                    dve.wait_ge(s_pv, i * NH + (k + 1))
                    r = rs[:, 0:1]
                    step(nc.vector.reduce_sum(r, sm[:, k % 4, 0:3], AX.X))
                    step(nc.vector.reciprocal(rs[:, 1:2], r))
                    r = rs[:, 1:2]
                    if p < DH and h == 0:
                        nc.vector.tensor_scalar_mul(o1[:], psO[:, k % 2, 0:DIFF_V], r).then_inc(s_of, 1)
                    elif p < DH:
                        step(nc.vector.tensor_tensor(rs[:, 2:3], r, nlam[:], ALU.mult))
                        dve.wait_ge(s_of, i * NH + (k + 2))
                        nc.vector.scalar_tensor_tensor(o2[:], psO[:, k % 2, 0:DIFF_V], rs[:, 2:3], o1[:], ALU.mult, ALU.add).then_inc(s_of, 1)
                        dve.wait_ge(s_of, i * NH + (k + 3))
                        nc.vector.tensor_tensor_reduce(out=oj[:], in0=o2[:], in1=o2[:], scale=1.0 / DIFF_V, scalar=EPS,
                                                       op0=ALU.mult, op1=ALU.add, accum_out=rs[:, 3:4]).then_inc(s_ov, 1)
                        dve.wait_ge(s_or, i * DH + (p + 1))
                        nc.vector.scalar_tensor_tensor(ob[:, p * DIFF_V:(p + 1) * DIFF_V], o2[:], rs[:, 5:6], sg[:],
                                                       ALU.mult, ALU.mult).then_inc(s_ob, 1)
                    else:
                        j = p - DH
                        at = 512 + (j + 4 * h) * HD
                        nc.vector.tensor_scalar_mul(ob[:, at:at + HD], psO[:, k % 2, 0:HD], r).then_inc(s_of, 1)

                maxes(0)
                for k in range(NH):
                    if k + 1 < NH:
                        maxes(k + 1)
                    o, w = CW[1]
                    dve.wait_ge(s_tp, i * C3 + (3 * k + 2))
                    nc.vector.tensor_copy(pT[:, k % 2, o // P:(o + w) // P], psP[:, 1, 0:w].rearrange("p (t n) -> p t n", n=P)).then_inc(s_ptd, 1)
                    if k == 1:
                        dve.wait_ge(s_obfree, i + 1)
                    if k >= 1:
                        finish(k - 1)
                finish(NH - 1)
                assert step.n[0] == STEPS, step.n[0]

        @block.tensor
        def _(pe):
            with pe.Fori(0, NT) as i:
                def qk_(k):
                    p, h = divmod(k, 2)
                    kp = min(p, 4)
                    if k % 8 == 0:
                        pe.wait_ge(s_q[k // 8], i * 16 + 16)
                    for j, (o, w) in enumerate(CW):
                        pe.wait_ge(s_exp, i * C3 + (3 * k + j + 1))
                        nc.tensor.matmul(psS[:, j, 0:w], qT[h * HD:(h + 1) * HD, p], kT[h * HD:(h + 1) * HD, kp, o:o + w],
                                         start=True, stop=True).then_inc(s_qk, 1)

                qk_(0)
                for k in range(NH):
                    if k + 1 < NH:
                        qk_(k + 1)
                    for j, (o, w) in enumerate(CW):
                        pe.wait_ge(s_exp, i * C3 + (3 * k + j + 4))
                        for t in range(w // P):
                            last = nc.tensor.transpose(psP[:, j, t * P:(t + 1) * P], pr[:, k % 2, o + t * P:o + (t + 1) * P], ident[:])
                        last.then_inc(s_tp, 1)
                    p, h = divmod(k, 2)
                    c, w = (p * DIFF_V, DIFF_V) if p < DH else (512 + h * HD, HD)
                    for t in range(KT_N):
                        if t == 0:
                            pe.wait_ge(s_of, i * NH + (k + 1))
                            pe.wait_ge(s_pta, i * (2 * NH) + (2 * k + 1))
                        if t == 4:
                            pe.wait_ge(s_ptd, i * NH + (k + 1))
                        if t == 8:
                            pe.wait_ge(s_pta, i * (2 * NH) + (2 * k + 2))
                        last = nc.tensor.matmul(psO[:, k % 2, 0:w], pT[:, k % 2, t], vv[:, t, c:c + w],
                                                start=(t == 0), stop=(t == KT_N - 1))
                    last.then_inc(s_pv, 1)


def output_and_router(b, a, ident, rows, mhalf, x1, entry, mask, o_d, h2_d, y_d):
    nc = b.nc
    TURNS = NT // 2
    with ExitStack() as ph:
        w_o = b.sb(ph, "w_out_sb", [P, KD, D])
        w_r = b.sb(ph, "w_router_sb", [P, KD, E])
        w_g = b.sb(ph, "w_shared_gu", [P, KD, 2 * FE])
        w_d = b.sb(ph, "w_shared_down", [P, 2, D])
        bias = b.sb(ph, "router_bias_row", [P, E])
        ot = [b.sb(ph, f"o_in{u}", [P, D]) for u in range(2)]
        xr = [b.sb(ph, f"x_in{u}", [P, D]) for u in range(2)]
        oT = [b.sb(ph, f"oT{u}", [P, KD, P]) for u in range(2)]
        hT = [b.sb(ph, f"h2T{u}", [P, KD, P]) for u in range(2)]
        h2 = [b.sb(ph, f"h2_row{u}", [P, D]) for u in range(2)]
        tmp = b.sb(ph, "row_tmp", [P, D])
        rwb = b.sb(ph, "weight_piece", [P, 3, E], BF16)
        yb = [b.sb(ph, f"y_shared{u}", [P, D]) for u in range(2)]
        aT = b.sb(ph, "act_T", [P, 2, P])
        ga = [b.sb(ph, f"gate_a{u}", [P, FE]) for u in range(2)]
        gb = b.sb(ph, "gate_b", [P, FE])
        junk = b.sb(ph, "square_junk", [P, D], BF16)
        ms = b.sb(ph, "mean_squares", [P, 2, 8])
        sc = b.sb(ph, "scores", [P, 2, E])
        rw = b.sb(ph, "router_work", [P, 6, E])
        g8 = b.sb(ph, "group_top", [P, NG, 8])
        r8 = b.sb(ph, "router_small", [P, 6, 8])
        psT = b.pb(ph, "ps_t", [P, 2, 512])
        psY = b.pb(ph, "ps_y", [P, 4, 512])
        psR = b.pb(ph, "ps_r", [P, 512])
        psG = b.pb(ph, "ps_g", [P, 512])
        S = {n: b.sem(ph, "r_" + n) for n in (
            "weights", "T", "Te", "proj", "sqP", "rs1", "x1", "sqX", "rs2", "h2", "logit", "expR", "gu", "expG",
            "act", "down", "yout", "routed", "h2_stored", "y_stored", "dve", "pool", "hold", "carry")}
        s_o = [b.sem(ph, f"o_loaded{u}") for u in range(2)]
        s_xr = [b.sem(ph, f"xr_loaded{u}") for u in range(2)]
        block = ph.enter_context(nc.Block())
        GR = 10
        GO, GHT, GA = (0, 2), (4, 6), (8, 9)
        NW = 6

        @block.sync
        def _(sp):
            for u in range(2):
                sp.dma_start(ot[u][:], o_d[u * P:(u + 1) * P, :]).then_inc(s_o[u], 16)
                sp.dma_start(xr[u][:], a["tokens"][CTX + u * P:CTX + (u + 1) * P, :]).then_inc(s_xr[u], 16)
            with sp.Fori(0, TURNS - 1) as i:
                for u in range(2):
                    sp.wait_ge(S["T"], i * GR + (GO[u] + 2))
                    sp.dma_start(ot[u][:], o_d[ds(i * (2 * P) + (2 + u) * P, P), :]).then_inc(s_o[u], 16)
                    sp.wait_ge(S["x1"], i * 2 + (u + 1))
                    sp.dma_start(xr[u][:], a["tokens"][ds(i * (2 * P) + (CTX + (2 + u) * P), P), :]).then_inc(s_xr[u], 16)

        @block.gpsimd
        def _(pool):
            with pool.Fori(0, TURNS) as i:
                for u in range(2):
                    m = ms[:, u]
                    pool.wait_ge(S["sqP"], i * 4 + (2 * u + 2))
                    nc.gpsimd.tensor_tensor(m[:, 2:3], m[:, 0:1], m[:, 1:2], ALU.add).then_inc(S["pool"], 1)
                    pool.wait_ge(S["pool"], i * 6 + (3 * u + 1))
                    nc.gpsimd.tensor_tensor(m[:, 3:4], m[:, 2:3], mhalf[:, 16:17], ALU.add).then_inc(S["pool"], 1)
                    pool.wait_ge(S["pool"], i * 6 + (3 * u + 2))
                    nc.gpsimd.tensor_tensor(m[:, 4:5], m[:, 3:4], mhalf[:, 0:1], ALU.pow).then_inc(S["rs1"], 1)
                    pool.wait_ge(S["sqX"], i * 2 + (u + 1))
                    nc.gpsimd.tensor_tensor(m[:, 6:7], m[:, 5:6], mhalf[:, 16:17], ALU.add).then_inc(S["pool"], 1)
                    pool.wait_ge(S["pool"], i * 6 + (3 * u + 3))
                    nc.gpsimd.tensor_tensor(m[:, 7:8], m[:, 6:7], mhalf[:, 0:1], ALU.pow).then_inc(S["rs2"], 1)
                    pool.wait_ge(S["h2"], i * 2 + (u + 1))
                    pool.sem_inc(S["carry"], 1)
                    pool.dma_start(h2_d[ds(i * (2 * P) + u * P, P), :], h2[u][:]).then_inc(S["h2_stored"], 16)
                for u in range(2):
                    pool.wait_ge(S["yout"], i * 2 + (u + 3))
                    pool.sem_inc(S["carry"], 1)
                    pool.dma_start(y_d[ds(i * (2 * P) + u * P, P), :], yb[u][:]).then_inc(S["y_stored"], 16)
                pool.wait_ge(S["h2_stored"], i * 32 + 32)
                pool.wait_ge(S["y_stored"], i * 32 + 32)
                pool.sem_inc(S["hold"], 1)

        @block.scalar
        def _(act):
            act.dma_start(w_o[:], a["w_out"][0].rearrange("(k p) n -> p k n", p=P)).then_inc(S["weights"], 16)
            act.dma_start(w_r[:], a["w_router"][0].rearrange("(p k) n -> p k n", k=KD)).then_inc(S["weights"], 16)
            act.dma_start(w_g[:, :, 0:FE], a["w_sh_gate"][0].rearrange("(p k) n -> p k n", k=KD)).then_inc(S["weights"], 16)
            act.dma_start(w_g[:, :, FE:], a["w_sh_up"][0].rearrange("(p k) n -> p k n", k=KD)).then_inc(S["weights"], 16)
            act.dma_start(w_d[:], a["w_sh_down"][0].rearrange("(k p) n -> p k n", p=P)).then_inc(S["weights"], 16)
            act.dma_start(bias[:], a["router_bias"].broadcast_to([P, E])).then_inc(S["weights"], 16)
            act.sem_inc(S["Te"], 2)
            act.sem_inc(S["yout"], 2)
            act.sem_inc(S["expR"], 1)
            with act.Fori(0, TURNS) as i:
                def out_T(dst, n, w=4):
                    act.wait_ge(S["T"], i * GR + (n + 1))
                    act.activation(dst, psT[:, n % 2, 0:w * P].rearrange("p (k n) -> p k n", n=P), ACT.Copy).then_inc(S["Te"], 1)

                def squares(u):
                    for h in range(2):
                        act.wait_ge(S["proj"], i * 4 + (2 * u + h + 1))
                        act.activation(junk[:, h * 512:(h + 1) * 512], psY[:, 2 * u + h], ACT.Square, scale=D ** -0.5,
                                       accum_out=ms[:, u, h:h + 1]).then_inc(S["sqP"], 1)
                    act.wait_ge(S["sqP"], i * 4 + (2 * u + 2))
                    act.wait_ge(S["x1"], i * 2 + (u + 1))
                    act.activation(junk[:], x1[:, ds(i * 2 + u, 1)].rearrange("p o n -> p (o n)"), ACT.Square,
                                   scale=D ** -0.5, accum_out=ms[:, u, 5:6]).then_inc(S["sqX"], 1)
                    act.wait_ge(S["sqX"], i * 2 + (u + 1))

                def exps(u):
                    act.wait_ge(S["logit"], i * 2 + (u + 1))
                    act.activation(sc[:, u], psR[:, 0:E], ACT.Exp, scale=-1.0).then_inc(S["expR"], 1)
                    act.wait_ge(S["gu"], i * 2 + (u + 1))
                    act.activation(ga[u][:], psG[:, 0:FE], ACT.Exp, scale=-1.0).then_inc(S["expG"], 1)

                def y_out(u):
                    for h in range(2):
                        act.wait_ge(S["down"], i * 4 + (2 * u + h + 1))
                        ins = act.activation(yb[u][:, h * 512:(h + 1) * 512], psY[:, 2 * u + h], ACT.Copy)
                    ins.then_inc(S["yout"], 1)

                for u in range(2):
                    for g in range(2):
                        out_T(oT[u][:, 4 * g:4 * g + 4], GO[u] + g)
                squares(0)
                for g in range(2):
                    out_T(hT[0][:, 4 * g:4 * g + 4], GHT[0] + g)
                squares(1)
                exps(0)
                for g in range(2):
                    out_T(hT[1][:, 4 * g:4 * g + 4], GHT[1] + g)
                exps(1)
                for u in range(2):
                    out_T(aT[:], GA[u], 2)
                    if u == 0:
                        act.wait_ge(S["hold"], i + 1)
                    y_out(u)

        @block.vector
        def _(dve):
            STEPS = 2 * (2 + 3 + 23)
            dve.sem_inc(S["hold"], 1)
            dve.sem_inc(S["act"], 1)
            dve.wait_ge(S["weights"], NW * 16)
            with dve.Fori(0, TURNS) as i:
                step = chain(dve, S["dve"], i * STEPS)

                def residual(u):
                    X = x1[:, ds(i * 2 + u, 1)].rearrange("p o n -> p (o n)")
                    dve.wait_ge(s_xr[u], i * 16 + 16)
                    dve.wait_ge(S["rs1"], i * 2 + (u + 1))
                    Y = psY[:, 2 * u:2 * u + 2].rearrange("p b n -> p (b n)")
                    step(nc.vector.scalar_tensor_tensor(tmp[:], Y, ms[:, u, 4:5], rows[:, G1], ALU.mult, ALU.mult))
                    nc.vector.tensor_tensor(X, tmp[:], xr[u][:], ALU.add).then_inc(S["x1"], 1)
                    dve.wait_ge(S["rs2"], i * 2 + (u + 1))
                    dve.wait_ge(S["x1"], i * 2 + (u + 1))
                    step(nc.vector.scalar_tensor_tensor(tmp[:], X, ms[:, u, 7:8], rows[:, A2], ALU.mult, ALU.mult))
                    if u == 0:
                        dve.wait_ge(S["hold"], i + 1)
                    nc.vector.tensor_tensor(h2[u][:].rearrange("p (k q) -> p q k", k=KD), tmp[:].rearrange("p (q k) -> p q k", k=KD),
                                            rows[:, B2].rearrange("p (q k) -> p q k", k=KD), ALU.add).then_inc(S["h2"], 1)

                def shared_act(u):
                    dve.wait_ge(S["expG"], i * 2 + (u + 1))
                    step(nc.vector.tensor_scalar_add(gb[:], ga[u][:], 1.0))
                    step(nc.vector.reciprocal(gb[:], gb[:]))
                    step(nc.vector.tensor_tensor(gb[:], gb[:], psG[:, 0:FE], ALU.mult))
                    nc.vector.tensor_tensor(ga[u][:], gb[:], psG[:, FE:2 * FE], ALU.mult).then_inc(S["act"], 1)

                def route(u):
                    def steph(ins):
                        step(ins)
                        dve.sem_inc(S["carry"], 1)
                    s, sel, m, W = sc[:, u], rw[:, 0], rw[:, 1], rw[:, 2]
                    dve.wait_ge(S["expR"], i * 2 + (u + 2))
                    step(nc.vector.tensor_scalar_add(s, s, 1.0))
                    step(nc.vector.reciprocal(s, s))
                    steph(nc.vector.tensor_tensor(sel, s, bias[:], ALU.add))
                    for g in range(NG):
                        ins = nc.vector.max(g8[:, g], sel[:, g * 8:(g + 1) * 8])
                    step(ins)
                    steph(nc.vector.tensor_tensor(r8[:, 0], g8[:, :, 0], g8[:, :, 1], ALU.add))
                    step(nc.vector.max(r8[:, 1], r8[:, 0]))
                    steph(nc.vector.memset(r8[:, 1, TOPG:8], -BIG))
                    step(nc.vector.match_replace(r8[:, 2], r8[:, 1], r8[:, 0], BIG))
                    step(nc.vector.tensor_scalar(r8[:, 3], r8[:, 2], BIG / 2, None, ALU.is_ge))
                    step(nc.vector.tensor_scalar(r8[:, 4], r8[:, 3], -1.0, BIG, ALU.add, ALU.mult))
                    v3 = lambda t: t.rearrange("p (g e) -> p g e", g=NG)
                    gm = r8[:, 3].unsqueeze(2).broadcast_to([P, NG, 8])
                    pen = r8[:, 4].unsqueeze(2).broadcast_to([P, NG, 8])
                    step(nc.vector.tensor_tensor(v3(m), v3(sel), gm, ALU.mult))
                    steph(nc.vector.tensor_tensor(v3(m), v3(m), pen, ALU.add))
                    steph(nc.vector.max(r8[:, 5], m))
                    step(nc.vector.match_replace(W, r8[:, 5], m, BIG))
                    step(nc.vector.tensor_scalar(rw[:, 3], W, BIG / 2, None, ALU.is_ge))
                    M = mask[:, ds(i * 2 + u, 1)].rearrange("p o e -> p (o e)")
                    nc.vector.tensor_copy(M, rw[:, 3])
                    step(nc.vector.tensor_tensor_reduce(out=W, in0=s, in1=rw[:, 3], scale=1.0, scalar=0.0, op0=ALU.mult,
                                                        op1=ALU.add, accum_out=r8[:, 1, 0:1]))
                    step(nc.vector.reciprocal(r8[:, 1, 1:2], r8[:, 1, 0:1]))
                    step(nc.vector.tensor_scalar(W, W, r8[:, 1, 1:2], ROUTED_SCALE, ALU.mult, ALU.mult))
                    EN = entry[:, ds(i * 2 + u, 1)].rearrange("p o e c -> p (o e) c")
                    for c in range(3):
                        step(nc.vector.tensor_copy(rwb[:, c], W))
                        ins = nc.vector.tensor_copy(EN[:, :, 2 + c], rwb[:, c])
                        if c < 2:
                            step(nc.vector.tensor_tensor(W, W, rwb[:, c], ALU.subtract))
                    ins.then_inc(S["routed"], 1)

                residual(0)
                residual(1)
                shared_act(0)
                route(0)
                shared_act(1)
                route(1)
                assert step.n[0] == STEPS, step.n[0]

        @block.tensor
        def _(pe):
            pe.wait_ge(S["weights"], NW * 16)
            with pe.Fori(0, TURNS) as i:
                def free(n):
                    pe.wait_ge(S["Te"], i * GR + (n + 1))

                def t8(src, n0):
                    for g in range(2):
                        free(n0 + g)
                        for k in range(4):
                            c = (4 * g + k) * P
                            last = nc.tensor.transpose(psT[:, (n0 + g) % 2, k * P:(k + 1) * P], src[:, c:c + P], ident[:])
                        last.then_inc(S["T"], 1)

                for u in range(2):
                    pe.wait_ge(s_o[u], i * 16 + 16)
                    t8(ot[u], GO[u])
                    pe.wait_ge(S["Te"], i * GR + (GO[u] + 4))
                    pe.wait_ge(S["yout"], i * 2 + (u + 1))
                    for h in range(2):
                        for k in range(KD):
                            last = nc.tensor.matmul(psY[:, 2 * u + h], oT[u][:, k], w_o[:, k, h * 512:(h + 1) * 512],
                                                    start=(k == 0), stop=(k == KD - 1))
                        last.then_inc(S["proj"], 1)
                for u in range(2):
                    pe.wait_ge(S["h2"], i * 2 + (u + 1))
                    t8(h2[u], GHT[u])
                    pe.wait_ge(S["Te"], i * GR + (GHT[u] + 4))
                    pe.wait_ge(S["expR"], i * 2 + (u + 1))
                    for k in range(KD):
                        last = nc.tensor.matmul(psR[:, 0:E], hT[u][:, k], w_r[:, k], start=(k == 0), stop=(k == KD - 1))
                    last.then_inc(S["logit"], 1)
                    pe.wait_ge(S["act"], i * 2 + (u + 1))
                    for k in range(KD):
                        last = nc.tensor.matmul(psG[:], hT[u][:, k], w_g[:, k], start=(k == 0), stop=(k == KD - 1))
                    last.then_inc(S["gu"], 1)
                for u in range(2):
                    pe.wait_ge(S["act"], i * 2 + (u + 2))
                    free(GA[u])
                    for k in range(2):
                        last = nc.tensor.transpose(psT[:, GA[u] % 2, k * P:(k + 1) * P], ga[u][:, k * P:(k + 1) * P], ident[:])
                    last.then_inc(S["T"], 1)
                    pe.wait_ge(S["Te"], i * GR + (GA[u] + 3))
                    for h in range(2):
                        for k in range(2):
                            last = nc.tensor.matmul(psY[:, 2 * u + h], aT[:, k], w_d[:, k, h * 512:(h + 1) * 512],
                                                    start=(k == 0), stop=(k == 1))
                        last.then_inc(S["down"], 1)


def routing_tables(b, a, ident, entry, mask, rank, tab):
    nc = b.nc
    with ExitStack() as ph:
        before = b.sb(ph, "before", [P, P])
        part = b.sb(ph, "partition", [P, 1])
        bb = b.sb(ph, "before_bf", [P, P], BF16)
        ones = b.sb(ph, "ones_bf", [P, P], BF16)
        w = b.sb(ph, "table_work", [P, 12, E])
        one = b.sb(ph, "ones_row", [P, E])
        ci = b.sb(ph, "count_int", [P, E], I32)
        col = b.sb(ph, "columns", [P, 8])
        cl = b.sb(ph, "block_columns", [P, 6])
        ps = b.pb(ph, "ps_rank", [P, 512])
        pc = b.pb(ph, "ps_count", [P, 512])
        pt = b.pb(ph, "ps_table", [P, 2, 512])
        s_ld = b.sem(ph, "t_loaded")
        s_cst = b.sem(ph, "t_const")
        s_rk = b.sem(ph, "t_rank")
        s_col = b.sem(ph, "t_cols")
        s_row = b.sem(ph, "t_rows")
        s_dve = b.sem(ph, "t_dve")
        block = ph.enter_context(nc.Block())

        @block.sync
        def _(sp):
            sp.dma_start(before[:], a["k_before"]).then_inc(s_ld, 16)
            sp.dma_start(part[:], a["k_part"]).then_inc(s_ld, 16)

        @block.gpsimd
        def _(pool):
            pool.wait_ge(s_ld, 32)
            for t in range(NT):
                nc.gpsimd.memset(entry[:, t, :, 0], float(t))
            nc.gpsimd.memset(entry[:, :, :, NPC - 1], 1.0)
            nc.gpsimd.tensor_copy(entry[:, :, :, 1].rearrange("p t e -> p (t e)"), part[:].broadcast_to([P, NT * E]))

        @block.vector
        def _(dve):
            step = chain(dve, s_dve)
            dve.wait_ge(s_ld, 32)
            nc.vector.memset(one[:], 1.0)
            nc.vector.memset(ones[:], 1.0)
            nc.vector.tensor_copy(bb[:], before[:]).then_inc(s_cst, 1)
            dve.wait_ge(s_rk, 2)
            mf = mask[:].rearrange("p t e -> p (t e)")
            rk = rank[:].rearrange("p t e -> p (t e)")
            step(nc.vector.scalar_tensor_tensor(rk, ps[:], 1.0, mf, ALU.add, ALU.mult))
            step(nc.vector.tensor_scalar_add(rk, rk, -1.0))
            cf, nbk, cum, ne, od, cmp, t0, t1, t2, t3 = (w[:, j] for j in range(10))
            step(nc.vector.tensor_scalar_add(cf, pc[:, 0:E], P - 1.0))
            step(nc.vector.tensor_copy(ci[:], cf))
            step(nc.vector.tensor_single_scalar(ci[:], ci[:], 7, ALU.arith_shift_right))
            step(nc.vector.tensor_copy(nbk, ci[:]))
            step(nc.vector.tensor_tensor_scan(cum, one[:], nbk, 0.0, ALU.mult, ALU.add))
            step(nc.vector.tensor_scalar_min(ne, nbk, 1.0))
            step(nc.vector.tensor_tensor_scan(od, one[:], ne, 0.0, ALU.mult, ALU.add))
            lastb, pcl, st, p3 = (col[:, j:j + 1] for j in range(4))
            step(nc.vector.tensor_scalar_add(lastb, cum[:, E - 1:E], -1.0))
            step(nc.vector.tensor_tensor(pcl, part[:], lastb, ALU.min))
            step(nc.vector.tensor_scalar(cmp, cum, pcl, None, ALU.is_le))
            step(nc.vector.tensor_tensor(t0, cmp, nbk, ALU.mult))
            step(nc.vector.tensor_tensor(t1, cmp, ne, ALU.mult))
            step(nc.vector.reduce_sum(cl[:, 0:1], cmp, AX.X))
            step(nc.vector.reduce_sum(st, t0, AX.X))
            step(nc.vector.reduce_sum(cl[:, 2:3], t1, AX.X))
            step(nc.vector.tensor_tensor(cl[:, 1:2], part[:], st, ALU.subtract))
            step(nc.vector.tensor_scalar_min(cl[:, 1:2], cl[:, 1:2], 8.0))
            step(nc.vector.tensor_scalar(t2, od, part[:], None, ALU.is_le))
            step(nc.vector.reduce_sum(cl[:, 3:4], t2, AX.X))
            step(nc.vector.tensor_scalar_add(p3, part[:], -(WS - 1.0)))
            step(nc.vector.tensor_scalar(t3, od, p3, None, ALU.is_le))
            step(nc.vector.tensor_tensor(t3, t3, nbk, ALU.mult))
            step(nc.vector.reduce_sum(cl[:, 4:5], t3, AX.X))
            step(nc.vector.tensor_scalar_min(cl[:, 3:4], cl[:, 3:4], E - 1.0))
            nc.vector.tensor_copy(cl[:, 5:6], lastb).then_inc(s_col, 1)
            dve.wait_ge(s_row, 1)
            for c in range(6):
                nc.vector.tensor_copy(tab[0:1, c, 0:P], pt[0:1, c // 3, (c % 3) * P:(c % 3 + 1) * P])
                step(nc.vector.tensor_copy(tab[0:1, c, P:P + 8],
                                           pt[0:1, c // 3, (c % 3 + 1) * P - 1:(c % 3 + 1) * P].broadcast_to([1, 8])))
            step(nc.vector.tensor_scalar_add(cl[0:1, 0:1], cum[0:1, E - 1:E], 0.0))
            step(nc.vector.tensor_copy(tab[0:1, 5, 0:1], cl[0:1, 0:1]))
            step(nc.vector.tensor_copy(tab[0:1, 5, 1:2], od[0:1, E - 1:E]))
            step(nc.vector.tensor_scalar_add(tab[0:1, 5, 2:3], tab[0:1, 5, 0:1], 1))
            nc.vector.tensor_single_scalar(tab[0:1, 5, 2:3], tab[0:1, 5, 2:3], 1, ALU.arith_shift_right)

        @block.tensor
        def _(pe):
            pe.wait_ge(s_cst, 1)
            for t in range(NT):
                nc.tensor.matmul(ps[:, t * E:(t + 1) * E], bb[:], mask[:, t], start=True, stop=(t == 0))
                for q in range(t):
                    nc.tensor.matmul(ps[:, t * E:(t + 1) * E], ones[:], mask[:, q], start=False, stop=(q == t - 1))
            for t in range(NT):
                last = nc.tensor.matmul(pc[:, 0:E], ones[:], mask[:, t], start=(t == 0), stop=(t == NT - 1))
            last.then_inc(s_rk, 2)
            pe.wait_ge(s_col, 1)
            for c in range(6):
                last = nc.tensor.matmul(pt[0:1, c // 3, (c % 3) * P:(c % 3 + 1) * P], cl[:, c:c + 1], ident[:],
                                        start=True, stop=True)
            last.then_inc(s_row, 1)


def experts(b, a, ident, entry, rank, tab, h2_d, y_d):
    nc = b.nc
    RING = 8
    with ExitStack() as ph:
        wgu = b.sb(ph, "w_gate_up", [P, WS, KD, 2 * FE])
        wdn = b.sb(ph, "w_down", [P, WS, 2, D])
        count = b.sb(ph, "count_row", [P, 9 * P])
        part = b.sb(ph, "partition_p", [P, 2])
        oh = b.sb(ph, "one_hot", [P, NT, P], BF16)
        xg = [b.sb(ph, f"gathered{u}", [P, D]) for u in range(2)]
        hT = b.sb(ph, "gatheredT", [P, KD, P])
        ga = b.sb(ph, "e_gate_a", [P, FE])
        gb = b.sb(ph, "e_gate_b", [P, FE])
        aT = b.sb(ph, "e_act_T", [P, 2, P])
        yb = [b.sb(ph, f"e_y{u}", [P, D]) for u in range(2)]
        pc = b.sb(ph, "e_pieces", [P, 8])
        tk = b.sb(ph, "e_token", [P, 4])
        wr = b.sb(ph, "e_weight_ring", [P, RING])
        sr = b.sb(ph, "e_target_ring", [P, RING])
        wn = b.sb(ph, "e_weight", [P, 2])
        zero = b.sb(ph, "e_zero", [P, D])
        ti = [b.sb(ph, f"e_gather_index{u}", [P, 1], U32) for u in range(2)]
        si = [b.sb(ph, f"e_target_index{u}", [P, 1], U32) for u in range(2)]
        psX = b.pb(ph, "ps_x", [P, 2, 512])
        psG = b.pb(ph, "ps_gu", [P, 512])
        psA = b.pb(ph, "ps_a", [P, 512])
        psY = b.pb(ph, "ps_ye", [P, 2, 512])
        psI = b.pb(ph, "ps_i", [P, 512])
        S = {n: b.sem(ph, "e_" + n) for n in (
            "const", "oh", "pieces", "piecesout", "tok", "xT", "hT", "gu", "exp", "act", "aTp",
            "aT", "dn", "y0", "y1", "target", "scat", "scatok", "landed", "dve", "carry", "zeroed")}
        s_gather = [b.sem(ph, f"e_gathered{u}") for u in range(2)]
        s_w = [b.sem(ph, f"e_weights_loaded{u}") for u in range(WS)]
        block = ph.enter_context(nc.Block())

        def read(eng, c, at, hi):
            return eng.value_load(tab[0:1, c, ds(at, 1)], min_val=0, max_val=hi)

        def blocks(eng, body):
            turns = eng.value_load(tab[0:1, 5, 2:3], min_val=1, max_val=NBLK // 2)
            with eng.Fori(0, turns) as i:
                for u in range(2):
                    body(i, i * 2 + u, u)
            return turns

        @block.sync
        def _(sp):
            sp.dma_start(count[:], a["k_count"]).then_inc(S["const"], 16)
            sp.dma_start(part[:, 0:1], a["k_part"]).then_inc(S["const"], 16)
            loaded = sp.value_load(tab[0:1, 5, 1:2], min_val=1, max_val=E)

            def load(n, u):
                e = read(sp, 3, n, E - 1)
                sp.dma_start(wgu[:, u, :, 0:FE], a["w_exp_gate"][0, ds(e, 1)].rearrange("o (p k) n -> (o p) k n", k=KD)).then_inc(s_w[u], 16)
                sp.dma_start(wgu[:, u, :, FE:], a["w_exp_up"][0, ds(e, 1)].rearrange("o (p k) n -> (o p) k n", k=KD)).then_inc(s_w[u], 16)
                sp.dma_start(wdn[:, u], a["w_exp_down"][0, ds(e, 1)].rearrange("o (k p) n -> p (o k) n", p=P)).then_inc(s_w[u], 16)

            load(0, 0)
            with sp.Fori(0, E // WS) as i:
                for u in range(WS):
                    n = i * WS + (u + 1)
                    with sp.If(n < loaded):
                        done = read(sp, 4, n, NBLK)
                        sp.wait_ge(S["dn"], done * 2 + 1)
                        load(n, (u + 1) % WS)
                        sp.wait_ge(s_w[u], i * 48 + 48)
                        sp.sem_inc(S["landed"], 1)
            for u in range(WS):
                with sp.If(((loaded + (WS - 1)) & (WS - 1)) == u):
                    sp.wait_ge(s_w[u], ((loaded + (WS - 1)) // WS) * 48)
                    sp.sem_inc(S["landed"], 1)

        @block.gpsimd
        def _(pool):
            def gather(n, u, first=False):
                pool.wait_ge(S["tok"], n + 1)
                if not first:
                    pool.wait_ge(S["xT"], n * 2 - 2)
                pool.sem_inc(S["carry"], 1)
                pool.indirect_dma_start(xg[u][:], None, h2_d, bass.IndirectOffsetOnAxis(ap=ti[u][:, 0:1], axis=0),
                                        bounds_check=SEQ - 1).then_inc(s_gather[u], 16)

            def body(i, n, u):
                gather(n + 3, 1 - u)
                pool.wait_ge(S["scat"], n * 16 + 16)
                pool.sem_inc(S["scatok"], 1)
                pool.wait_ge(S["y0"], n + 2)
                pool.wait_ge(S["y1"], n + 2)
                pool.sem_inc(S["carry"], 1)
                pool.indirect_dma_start(y_d, bass.IndirectOffsetOnAxis(ap=si[u][:, 0:1], axis=0), yb[u][:], None,
                                        bounds_check=SEQ + P - 1, compute_op=ALU.add).then_inc(S["scat"], 16)

            nc.gpsimd.memset(zero[:], 0.0).then_inc(S["zeroed"], 1)
            pool.wait_ge(S["zeroed"], 1)
            pool.dma_start(y_d[SEQ:SEQ + P, :], zero[:]).then_inc(S["scat"], 16)
            pool.sem_inc(S["scatok"], 1)
            gather(0, 0, True)
            gather(1, 1, True)
            gather(2, 0)
            turns = blocks(pool, body)
            pool.wait_ge(s_gather[0], turns * 16 + 32)
            pool.wait_ge(s_gather[1], turns * 16 + 16)
            pool.wait_ge(S["scat"], turns * 32 + 16)

        @block.scalar
        def _(act):
            def out_x(n):
                for g in range(2):
                    act.wait_ge(S["xT"], n * 2 + (g + 1))
                    act.activation(hT[:, 4 * g:4 * g + 4], psX[:, g].rearrange("p (k n) -> p k n", n=P), ACT.Copy).then_inc(S["hT"], 1)

            def out_exp(n):
                act.wait_ge(S["gu"], n + 1)
                act.activation(ga[:], psG[:, 0:FE], ACT.Exp, scale=-1.0).then_inc(S["exp"], 1)

            def out_a(n):
                act.wait_ge(S["aTp"], n + 1)
                act.activation(aT[:], psA[:, 0:2 * P].rearrange("p (k n) -> p k n", n=P), ACT.Copy).then_inc(S["aT"], 1)

            def body(i, n, u):
                out_exp(n + 1)
                out_x(n + 2)
                act.wait_ge(S["target"], n + 1)
                act.wait_ge(S["dn"], n * 2 + 2)
                act.activation(yb[u][:, 0:512], psY[:, 0], ACT.Copy, scale=wn[:, u:u + 1]).then_inc(S["y0"], 1)
                out_a(n + 1)

            act.sem_inc(S["y0"], 1)
            out_x(0)
            out_exp(0)
            out_x(1)
            out_a(0)
            blocks(act, body)

        @block.vector
        def _(dve):
            HEAD, STEPS = 1 + 4 * 6 + 3, 3 + 6 + 1
            dve.wait_ge(S["const"], 32)
            dve.sem_inc(S["y1"], 1)
            first = chain(dve, S["dve"])
            first(nc.vector.tensor_scalar_add(part[:, 1:2], part[:, 0:1], float(SEQ)))

            def one_hot(n, head=False):
                e = read(dve, 0, n, E - 1)
                j = read(dve, 1, n, 8)
                if not head:
                    dve.wait_ge(S["pieces"], n)
                nc.vector.tensor_tensor(oh[:], count[:, ds(j * P, P)].unsqueeze(1).broadcast_to([P, NT, P]),
                                        rank[:, :, ds(e, 1)].broadcast_to([P, NT, P]), ALU.is_equal).then_inc(S["oh"], 1)

            def indices(n, turn, u, step, head=False):
                dve.wait_ge(S["pieces"], n + 1)
                nc.vector.tensor_copy(pc[:, 0:NPC], psI[:, 0:NPC]).then_inc(S["piecesout"], 1)
                dve.wait_ge(S["piecesout"], n + 1)
                at = n & (RING - 1)
                W, T = wr[:, ds(at, 1)], sr[:, ds(at, 1)]
                step(nc.vector.scalar_tensor_tensor(tk[:, 0:1], pc[:, 0:1], float(P), pc[:, 1:2], ALU.mult, ALU.add))
                step(nc.vector.tensor_scalar(tk[:, 1:2], pc[:, NPC - 1:NPC], -1.0, 1.0, ALU.mult, ALU.add))
                step(nc.vector.tensor_tensor(tk[:, 1:2], tk[:, 1:2], part[:, 1:2], ALU.mult))
                step(nc.vector.tensor_tensor(T, tk[:, 0:1], tk[:, 1:2], ALU.add))
                step(nc.vector.tensor_tensor(tk[:, 2:3], pc[:, 2:3], pc[:, 3:4], ALU.add))
                step(nc.vector.tensor_tensor(W, tk[:, 2:3], pc[:, 4:5], ALU.add))
                if not head:
                    dve.wait_ge(s_gather[u], turn * 16)
                nc.vector.tensor_copy(ti[u][:], tk[:, 0:1]).then_inc(S["tok"], 1)

            def gate(n, step):
                dve.wait_ge(S["exp"], n + 1)
                step(nc.vector.tensor_scalar_add(gb[:], ga[:], 1.0))
                step(nc.vector.reciprocal(gb[:], gb[:]))
                step(nc.vector.tensor_tensor(gb[:], gb[:], psG[:, 0:FE], ALU.mult))
                nc.vector.tensor_tensor(ga[:], gb[:], psG[:, FE:2 * FE], ALU.mult).then_inc(S["act"], 1)

            def body(i, n, u):
                step = chain(dve, S["dve"], n * STEPS + HEAD)
                dve.wait_ge(S["scatok"], n + 1)
                step(nc.vector.tensor_copy(wn[:, u:u + 1], wr[:, ds(n & (RING - 1), 1)]))
                nc.vector.tensor_copy(si[u][:], sr[:, ds(n & (RING - 1), 1)]).then_inc(S["target"], 1)
                gate(n + 1, step)
                dve.wait_ge(S["dn"], n * 2 + 3)
                nc.vector.tensor_scalar_mul(yb[u][:, 512:1024], psY[:, 1], wn[:, u:u + 1]).then_inc(S["y1"], 1)
                indices(n + 4, i + 2, u, step)
                one_hot(n + 5)
                assert step.n[0] == STEPS

            one_hot(0, True)
            indices(0, 0, 0, first, True)
            one_hot(1)
            indices(1, 0, 1, first, True)
            one_hot(2)
            indices(2, 1, 0, first)
            one_hot(3)
            gate(0, first)
            indices(3, 1, 1, first)
            one_hot(4)
            assert first.n[0] == HEAD
            blocks(dve, body)

        @block.tensor
        def _(pe):
            def pieces(n, head=False):
                e = read(pe, 0, n, E - 1)
                pe.wait_ge(S["oh"], n + 1)
                if not head:
                    pe.wait_ge(S["piecesout"], n)
                for t in range(NT):
                    last = nc.tensor.matmul(psI[:, 0:NPC], oh[:, t], entry[:, t, ds(e, 1)].rearrange("p o c -> p (o c)"),
                                            start=(t == 0), stop=(t == NT - 1))
                last.then_inc(S["pieces"], 1)

            def t_x(turn, u):
                pe.wait_ge(s_gather[u], turn * 16 + 16)
                for g in range(2):
                    for k in range(4):
                        c = (4 * g + k) * P
                        last = nc.tensor.transpose(psX[:, g, k * P:(k + 1) * P], xg[u][:, c:c + P], ident[:])
                    last.then_inc(S["xT"], 1)

            def gate_up(n):
                q = read(pe, 2, n, E - 1)
                pe.wait_ge(S["landed"], q + 1)
                pe.wait_ge(S["hT"], n * 2 + 2)
                for k in range(KD):
                    last = nc.tensor.matmul(psG[:], hT[:, k], wgu[:, ds(q & (WS - 1), 1), k].rearrange("p o n -> p (o n)"),
                                            start=(k == 0), stop=(k == KD - 1))
                last.then_inc(S["gu"], 1)

            def down(n):
                q = read(pe, 2, n, E - 1)
                pe.wait_ge(S["aT"], n + 1)
                pe.wait_ge(S["y0"], n + 1)
                pe.wait_ge(S["y1"], n + 1)
                for h in range(2):
                    for k in range(2):
                        last = nc.tensor.matmul(psY[:, h], aT[:, k], wdn[:, ds(q & (WS - 1), 1), k, h * 512:(h + 1) * 512].rearrange("p o n -> p (o n)"),
                                                start=(k == 0), stop=(k == 1))
                    last.then_inc(S["dn"], 1)

            def t_a(n):
                pe.wait_ge(S["act"], n + 1)
                for k in range(2):
                    last = nc.tensor.transpose(psA[:, k * P:(k + 1) * P], ga[:, k * P:(k + 1) * P], ident[:])
                last.then_inc(S["aTp"], 1)

            def body(i, n, u):
                gate_up(n + 1)
                t_x(i + 1, u)
                down(n)
                pieces(n + 4)
                t_a(n + 1)

            pe.sem_inc(S["dn"], 1)
            pieces(0, True)
            pieces(1)
            t_x(0, 0)
            pieces(2)
            gate_up(0)
            pieces(3)
            t_x(0, 1)
            t_a(0)
            blocks(pe, body)


def final(b, a, rows, mhalf, x1, y_d, out):
    nc = b.nc
    with ExitStack() as ph:
        yt = b.sb(ph, "y_tiles", [P, NT, D])
        junk = b.sb(ph, "f_square", [P, 2, D], BF16)
        ms = b.sb(ph, "f_mean", [P, 3, NT])
        s_y = [b.sem(ph, f"y_loaded{t}") for t in range(NT)]
        s_sq = b.sem(ph, "f_sq")
        s_rs = b.sem(ph, "f_rs")
        s_pool = b.sem(ph, "f_pool")
        s_o = b.sem(ph, "f_out")
        s_dve = b.sem(ph, "f_dve")
        s_st = b.sem(ph, "f_stored")
        block = ph.enter_context(nc.Block())

        @block.sync
        def _(sp):
            for t in range(NT):
                sp.dma_start(yt[:, t], y_d[t * P:(t + 1) * P, :]).then_inc(s_y[t], 16)
            for t in range(NT):
                sp.wait_ge(s_o, t + 1)
                sp.dma_start(out[0, t * P:(t + 1) * P, :], yt[:, t]).then_inc(s_st, 16)
            sp.wait_ge(s_st, NT * 16)

        @block.scalar
        def _(act):
            for t in range(NT):
                act.wait_ge(s_y[t], 16)
                if t >= 2:
                    act.wait_ge(s_sq, t - 1)
                act.activation(junk[:, t % 2], yt[:, t], ACT.Square, scale=D ** -0.5, accum_out=ms[:, 0, t:t + 1]).then_inc(s_sq, 1)

        @block.gpsimd
        def _(pool):
            for t in range(NT):
                pool.wait_ge(s_sq, t + 1)
                nc.gpsimd.tensor_tensor(ms[:, 1, t:t + 1], ms[:, 0, t:t + 1], mhalf[:, 16:17], ALU.add).then_inc(s_pool, 1)
                pool.wait_ge(s_pool, t + 1)
                nc.gpsimd.tensor_tensor(ms[:, 2, t:t + 1], ms[:, 1, t:t + 1], mhalf[:, 0:1], ALU.pow).then_inc(s_rs, 1)

        @block.vector
        def _(dve):
            step = chain(dve, s_dve)
            for t in range(NT):
                dve.wait_ge(s_rs, t + 1)
                step(nc.vector.scalar_tensor_tensor(yt[:, t], yt[:, t], ms[:, 2, t:t + 1], rows[:, G2], ALU.mult, ALU.mult))
                nc.vector.tensor_tensor(yt[:, t], yt[:, t], x1[:, t], ALU.add).then_inc(s_o, 1)


def ds(start, size):
    return bass.ds(start, size)


def program(nc, a, out):
    b = Build(nc)
    qT_d = nc.dram_tensor("qT_scratch", [KT_N, P, NP * P], F32).ap()
    o_d = nc.dram_tensor("o_scratch", [SEQ, D], F32).ap()
    h2_d = nc.dram_tensor("h2_scratch", [SEQ, D], F32).ap()
    y_d = nc.dram_tensor("y_scratch", [SEQ + P, D], F32).ap()
    with ExitStack() as top:
        ident = b.sb(top, "ident", [P, P])
        rows = b.sb(top, "mod_rows", [P, 8, D])
        nlam = b.sb(top, "neg_lambda", [P, 1])
        mhalf = b.sb(top, "minus_half_eps", [P, 32])
        s_win = b.sem(top, "w_in_loaded")
        with ExitStack() as kv:
            with ExitStack() as ph:
                w_in = ph.enter_context(nc.sbuf_tensor("w_in_sb", [P, KD, INW], F32, side="right"))
                modulation(b, a, ident, rows, nlam, mhalf, w_in, s_win)
                kT = b.sb(kv, "kT", [P, 5, KEYS])
                vv = b.sb(kv, "values", [P, KT_N, VW])
                projections(b, a, ident, rows, mhalf, w_in, s_win, kT, vv, qT_d)
            attention(b, a, ident, nlam, mhalf, kT, vv, qT_d, o_d)
        x1 = b.sb(top, "x1", [P, NT, D])
        entry = b.sb(top, "entries", [P, NT, E, NPC], BF16)
        mask = b.sb(top, "chosen", [P, NT, E], BF16)
        output_and_router(b, a, ident, rows, mhalf, x1, entry, mask, o_d, h2_d, y_d)
        rank = b.sb(top, "rank", [P, NT, E])
        tab = b.sb(top, "block_table", [1, 6, P + 8], I32)
        routing_tables(b, a, ident, entry, mask, rank, tab)
        experts(b, a, ident, entry, rank, tab, h2_d, y_d)
        final(b, a, rows, mhalf, x1, y_d, out)


def rope_table():
    n = HD // 4
    inv = np.float32(10000.0) ** (-np.arange(n, dtype=np.float32) / np.float32(n))
    row = np.repeat(np.arange(SEQ // GRID_W), GRID_W).astype(np.float32)[:, None] * inv
    col = np.tile(np.arange(GRID_W), SEQ // GRID_W).astype(np.float32)[:, None] * inv
    t = np.zeros((KEYS, 2, HD), np.float32)
    t[:, 0] = 1.0
    t[CTX:, 0] = np.concatenate([np.cos(row)] * 2 + [np.cos(col)] * 2, axis=1)
    t[CTX:, 1] = np.concatenate([-np.sin(row), np.sin(row), -np.sin(col), np.sin(col)], axis=1)
    return t


def kernel(**inputs):
    import concourse.bacc as bacc
    from concourse.bass_utils import run_bass_kernel_spmd

    nc = bacc.Bacc("TRN2", target_bir_lowering=False, num_devices=1)
    host = {k: np.ascontiguousarray(v) for k, v in inputs.items() if k not in ("x", "ctx")}
    host["tokens"] = np.concatenate([np.asarray(inputs["ctx"])[0], np.asarray(inputs["x"])[0]], axis=0)
    select = np.zeros((2, 2, P), np.float32)
    select[0, 0] = select[1, 1] = 1.0
    tok = np.arange(P)
    host["k_ident"] = np.eye(P, dtype=np.float32)
    host["k_select"] = select
    host["k_rope"] = rope_table()
    host["k_before"] = (tok[:, None] < tok[None, :]).astype(np.float32)
    host["k_count"] = np.ascontiguousarray(np.broadcast_to(np.arange(9 * P, dtype=np.float32), (P, 9 * P)))
    host["k_part"] = np.arange(P, dtype=np.float32)[:, None]
    arrays, a = {}, {}
    for name, v in host.items():
        v = np.ascontiguousarray(v)
        arrays[f"in_{name}"] = v
        a[name] = nc.dram_tensor(f"in_{name}", v.shape, mybir.dt.from_np(v.dtype), kind="ExternalInput").ap()
    out = nc.dram_tensor("out", (1, SEQ, D), F32, kind="ExternalOutput").ap()
    program(nc, a, out)
    r = run_bass_kernel_spmd(nc, [arrays], core_ids=[0])
    return r.results[0]["out"]
```

```python
import math
from contextlib import ExitStack

import numpy as np

import concourse.bass as bass
from concourse import mybir

F32 = mybir.dt.float32
F32R = mybir.dt.float32r
BF16 = mybir.dt.bfloat16
I32 = mybir.dt.int32
U32 = mybir.dt.uint32
ALU = mybir.AluOpType
ACT = mybir.ActivationFunctionType
AX = mybir.AxisListType

P = 128
D = 1024
KD = D // P
SEQ, CTX = 1024, 256
NT, NC = SEQ // P, CTX // P
KT_N = NT + NC
KEYS = SEQ + CTX
HD = 64
DH, GH, GKV = 4, 8, 2
NP = 8
NH = 2 * NP
QKW = 1664
NHEADS = QKW // HD
VW = 640
INW = 2304
E, FE = 64, 256
NG, TOPG, TOPK = 8, 4, 8
GRID_W = 64
ROUTED_SCALE = 2.5
LAM_INIT = 0.8 - 0.6 * math.exp(-0.3 * 0)
EPS = 1e-6
BIG = 1e30
DIFF_V = 2 * HD
NBLK = SEQ * TOPK // P + E
WS = 4
NPC = 6
SCALE = HD ** -0.5



class Build:

    def __init__(self, nc):
        self.nc = nc

    def sb(self, st, name, shape, dt=F32):
        return st.enter_context(self.nc.sbuf_tensor(name, shape, dt))

    def pb(self, st, name, shape, dt=F32):
        return st.enter_context(self.nc.psum_tensor(name, shape, dt))

    def sem(self, st, name):
        return st.enter_context(self.nc.semaphore(name))


def chain(eng, s, start=0):
    n = [0]

    def step(ins):
        n[0] += 1
        ins.then_inc(s, 1)
        eng.wait_ge(s, start + n[0])
    step.n = n
    return step


A1, B1, A1C, B1C = range(4)
A2, B2, G1, G2 = range(4)


def spread(eng, mod_d, dst, table, s_):
    for r, (who, src) in enumerate(table):
        eng.dma_start(dst[:, r], mod_d[who:who + 1, src, :].broadcast_to([P, D])).then_inc(s_, 16)


def modulation(b, a, ident, rows1, rows, nlam, mhalf, w_in, s_win, mod_d):
    nc = b.nc
    SL, SW = 4, 256
    NS = 6 * D // SW
    with ExitStack() as ph:
        ring = b.sb(ph, "w_mod_ring", [P, SL, KD, SW])
        cs = b.sb(ph, "c_cols", [P, 2, KD])
        sg = b.sb(ph, "c_sig", [P, 2, KD])
        silu = b.sb(ph, "c_silu", [P, KD, 2])
        mrow = b.sb(ph, "mod_row", [2, 6, D])
        brow = b.sb(ph, "b_mod_row", [2, 6 * D])
        grow = b.sb(ph, "gain_row", [2, 4, D])
        lamv = b.sb(ph, "lambda_vecs", [P, 4, HD])
        lamj = b.sb(ph, "lambda_prod", [P, 2, HD])
        lamt = b.sb(ph, "lambda_terms", [P, 8])
        ps = b.pb(ph, "ps_mod", [P, SL, 512])
        s_c = b.sem(ph, "c_loaded")
        s_small = b.sem(ph, "small_loaded")
        s_slab = [b.sem(ph, f"slab_loaded{u}") for u in range(SL)]
        s_exp = b.sem(ph, "m_exp")
        s_silu = b.sem(ph, "silu_ready")
        s_lam = b.sem(ph, "lambda_sums")
        s_prod = b.sem(ph, "slab_multiplied")
        s_row = b.sem(ph, "row_part_out")
        s_rows = b.sem(ph, "rows_ready")
        s_stored = b.sem(ph, "rows_stored")
        s_rows1 = b.sem(ph, "first_rows_loaded")
        s_dve = b.sem(ph, "m_dve")
        block = ph.enter_context(nc.Block())
        NSMALL = 1 + 1 + 4 + 4
        EARLY = 2 * D // SW // SL
        WT = 4

        @block.gpsimd
        def _(pool):
            nc.gpsimd.memset(mhalf[:, 0:16], -0.5)
            nc.gpsimd.memset(mhalf[:, 16:32], EPS)

        @block.sync
        def _(sp):
            sp.dma_start(cs[:, 0, :], a["c"].rearrange("o (p k) -> (o p) k", k=KD)).then_inc(s_c, 16)
            sp.dma_start(cs[:, 1, :], a["c_ctx"].rearrange("(p k) -> p k", k=KD)).then_inc(s_c, 16)
            wm = a["w_mod"][0].rearrange("(p k) n -> p k n", k=KD)
            for u in range(SL):
                sp.dma_start(ring[:, u], wm[:, :, u * SW:(u + 1) * SW]).then_inc(s_slab[u], 16)

            def turn(i, with_w_in):
                for u in range(SL):
                    sp.wait_ge(s_prod, i * SL + (u - SL + 1))
                    sp.dma_start(ring[:, u], wm[:, :, ds(i * (SL * SW) + u * SW, SW)]).then_inc(s_slab[u], 16)
                    if with_w_in and u % (SL * WT // KD) == 1:
                        k = i * (KD // WT) + (u // (SL * WT // KD) - KD // WT)
                        sp.dma_start(w_in[:, ds(k, 1)].rearrange("p o n -> p (o n)"),
                                     a["w_in"][0, ds(k * P, P), :]).then_inc(s_win, 16)

            with sp.Fori(1, WT + 1) as i:
                turn(i, True)
            with sp.Fori(WT + 1, NS // SL) as i:
                turn(i, False)

        @block.scalar
        def _(act):
            act.dma_start(ident[:], a["k_ident"]).then_inc(s_small, 16)
            act.dma_start(brow[:], a["b_mod"].broadcast_to([2, 6 * D])).then_inc(s_small, 16)
            for j, g in enumerate(("g_pre_mix", "g_post_mix", "g_pre_ffn", "g_post_ffn")):
                act.dma_start(grow[:, j], a[g].broadcast_to([2, D])).then_inc(s_small, 16)
            for j, v in enumerate(("lambda_q1", "lambda_k1", "lambda_q2", "lambda_k2")):
                act.dma_start(lamv[:, j], a[v].broadcast_to([P, HD])).then_inc(s_small, 16)
            act.wait_ge(s_c, 32)
            act.activation(sg[:], cs[:], ACT.Exp, scale=-1.0).then_inc(s_exp, 1)
            act.wait_ge(s_lam, 1)
            act.activation(lamt[:, 2:4], lamt[:, 0:2], ACT.Exp).then_inc(s_exp, 1)
            act.wait_ge(s_rows, 1)
            act.dma_start(mod_d[:, 0:2], mrow[:, 0:2]).then_inc(s_stored, 16)
            act.wait_ge(s_stored, 16)
            spread(act, mod_d, rows1, [(0, 1), (0, 0), (1, 1), (1, 0)], s_rows1)
            act.wait_ge(s_rows, 2)
            act.dma_start(mod_d[:, 2:6], mrow[:, 2:6]).then_inc(s_stored, 16)
            act.wait_ge(s_stored, 32)
            act.wait_ge(s_rows1, 4 * 16)

        @block.vector
        def _(dve):
            step = chain(dve, s_dve)
            dve.wait_ge(s_c, 32)
            dve.wait_ge(s_exp, 1)
            step(nc.vector.tensor_scalar_add(sg[:], sg[:], 1.0))
            step(nc.vector.reciprocal(sg[:], sg[:]))
            nc.vector.tensor_tensor(silu[:].rearrange("p k c -> p c k"), sg[:], cs[:], ALU.mult).then_inc(s_silu, 1)
            dve.wait_ge(s_small, NSMALL * 16)
            step(nc.vector.tensor_tensor(lamj[:, 0], lamv[:, 0], lamv[:, 1], ALU.mult))
            step(nc.vector.tensor_tensor(lamj[:, 1], lamv[:, 2], lamv[:, 3], ALU.mult))
            nc.vector.tensor_reduce(lamt[:, 0:2], lamj[:], AX.X, ALU.add).then_inc(s_lam, 1)
            dve.wait_ge(s_exp, 2)
            step(nc.vector.tensor_tensor(lamt[:, 4:5], lamt[:, 3:4], lamt[:, 2:3], ALU.subtract))
            step(nc.vector.tensor_scalar_add(nlam[:], lamt[:, 4:5], -LAM_INIT))
            mflat = mrow[:].rearrange("c s d -> c (s d)")

            def bias(first, last):
                with dve.Fori(first, last) as i:
                    for u in range(SL):
                        dve.wait_ge(s_prod, i * SL + u + 1)
                        at = i * (SL * SW) + u * SW
                        nc.vector.tensor_tensor(mflat[:, ds(at, SW)], ps[0:2, u, 0:SW], brow[:, ds(at, SW)], ALU.add).then_inc(s_row, 1)
                dve.wait_ge(s_row, last * SL)

            bias(0, EARLY)
            nc.vector.scalar_tensor_tensor(mrow[:, 1], mrow[:, 1], 1.0, grow[:, 0], ALU.add, ALU.mult).then_inc(s_rows, 1)
            bias(EARLY, NS // SL)
            nc.vector.scalar_tensor_tensor(mrow[:, 4], mrow[:, 4], 1.0, grow[:, 2], ALU.add, ALU.mult)
            nc.vector.tensor_tensor(mrow[:, 2], mrow[:, 2], grow[:, 1], ALU.mult)
            nc.vector.tensor_tensor(mrow[:, 5], mrow[:, 5], grow[:, 3], ALU.mult).then_inc(s_rows, 1)

        @block.tensor
        def _(pe):
            pe.wait_ge(s_silu, 1)
            with pe.Fori(0, NS // SL) as i:
                for u in range(SL):
                    pe.wait_ge(s_slab[u], i * 16 + 16)
                    if u == 0:
                        with pe.If(i > 0):
                            pe.wait_ge(s_row, i * SL)
                            pe.nop()
                    for k in range(KD):
                        last = nc.tensor.matmul(ps[0:2, u, 0:SW], silu[:, k], ring[:, u, k], start=(k == 0), stop=(k == KD - 1))
                    last.then_inc(s_prod, 1)


def projections(b, a, ident, rows, later_rows, s_rows2, mod_d, mhalf, w_in, s_win, vv, qT_d, kT_d):
    nc = b.nc
    TURNS = KT_N // 2
    with ExitStack() as ph:
        kT = b.sb(ph, "kT", [P, 5, KEYS])
        xt = [b.sb(ph, f"x_tile{u}", [P, D]) for u in range(2)]
        hT = [b.sb(ph, f"hT{u}", [P, KD, P]) for u in range(2)]
        qk = b.sb(ph, "qk_rows", [P, QKW])
        t1 = b.sb(ph, "rope_a", [P, QKW])
        t2 = b.sb(ph, "rope_b", [P, QKW])
        rt = [b.sb(ph, f"rope_table{u}", [P, 2, HD]) for u in range(2)]
        junk = b.sb(ph, "square_out", [P, D], BF16)
        ssq = b.sb(ph, "sum_squares", [P, 2, 2])
        hss = b.sb(ph, "head_squares", [P, 32])
        gq = b.sb(ph, "q_gain", [P, HD])
        gk = b.sb(ph, "k_gain", [P, HD])
        qTs = b.sb(ph, "qT_stage", [P, NP, P])
        psT = b.pb(ph, "ps_transpose", [P, 3, 512])
        psC = b.pb(ph, "ps_chunk", [P, 5, 512])
        s_x = [b.sem(ph, f"x_loaded{u}") for u in range(2)]
        s_rt = [b.sem(ph, f"rope_loaded{u}") for u in range(2)]
        s_gain = b.sem(ph, "gain_loaded")
        s_sq = b.sem(ph, "sum_square")
        s_h = b.sem(ph, "h_ready")
        s_T = b.sem(ph, "group_transposed")
        s_Te = b.sem(ph, "group_out")
        s_ch = b.sem(ph, "chunk_done")
        s_che = b.sem(ph, "chunk_out")
        s_rh = b.sem(ph, "h_rstd")
        s_hv = b.sem(ph, "head_mean_square")
        s_rr = b.sem(ph, "head_rstd")
        s_pool = b.sem(ph, "p_pool")
        s_rope = b.sem(ph, "rope_done")
        s_qd = b.sem(ph, "qT_stored")
        s_kd = b.sem(ph, "kT_stored")
        s_dve = b.sem(ph, "p_dve")
        block = ph.enter_context(nc.Block())
        CH = [(1024, 512, [(0, 512, "v", 0)]), (512, 512, [(0, 512, "qk", 1024)]),
              (2048, 256, [(0, 128, "qk", 1536), (128, 128, "v", 512)]),
              (0, 512, [(0, 512, "qk", 0)]), (1536, 512, [(0, 512, "gq", 512)])]
        HG, QG = (0, 6), (2, 8)
        NGR = 12

        def skipped(i, c):
            return isinstance(i, int) and i == 0 and c >= 3

        def first_qk(i, u):
            return TURNS * NGR + 4 * u if isinstance(i, int) and i == TURNS - 1 else (i + 1) * NGR + QG[u]

        QKG = [([1024 + j * P for j in range(4)], "k", 0), ([1536], "k", 4),
               ([j * P for j in range(4)], "q", 0), ([512 + j * P for j in range(4)], "q", 4)]
        xa, rope = a["tokens"], a["k_rope"]

        @block.sync
        def _(sp):
            for u in range(2):
                sp.dma_start(xt[u][:], xa[u * P:(u + 1) * P, :]).then_inc(s_x[u], 16)
                sp.dma_start(rt[u][:], rope[u * P:(u + 1) * P]).then_inc(s_rt[u], 16)
            sp.dma_start(gq[:], a["q_norm_g"].broadcast_to([P, HD])).then_inc(s_gain, 16)
            sp.dma_start(gk[:], a["k_norm_g"].broadcast_to([P, HD])).then_inc(s_gain, 16)
            spread(sp, mod_d, later_rows, [(0, 4), (0, 3), (0, 2), (0, 5)], s_rows2)

            def store(i, u):
                sp.wait_ge(s_Te, first_qk(i, u) + 4)
                for h in range(2):
                    sp.dma_start(qT_d[ds(i * 2 + u, 1), :, :, h].rearrange("o p j n -> (o p) j n"),
                                 qTs[h * HD:(h + 1) * HD]).then_inc(s_qd, 16)

            def turn(i, first=False):
                for u in range(2):
                    sp.wait_ge(s_T, i * NGR + (HG[u] + 2))
                    sp.dma_start(xt[u][:], xa[ds(i * (2 * P) + (2 + u) * P, P), :]).then_inc(s_x[u], 16)
                    if not first:
                        store(i - 1, u)
                for u in range(2):
                    sp.wait_ge(s_rope, i * 2 + (u + 1))
                    sp.dma_start(rt[u][:], rope[ds(i * (2 * P) + (2 + u) * P, P)]).then_inc(s_rt[u], 16)

            turn(0, True)
            with sp.Fori(1, TURNS - 1) as i:
                turn(i)
            done = (TURNS - 1) * 2 * P
            for t in (TURNS - 2, TURNS - 1):
                for u in range(2):
                    store(t, u)
                cols = slice(0, done) if t == TURNS - 2 else slice(done, KEYS)
                sp.dma_start(kT_d[:, :, cols].rearrange("j p n -> p j n"), kT[:, :, cols]).then_inc(s_kd, 16)
            sp.wait_ge(s_qd, KT_N * 32)
            sp.wait_ge(s_kd, 32)

        @block.scalar
        def _(act):
            def square(i, u):
                act.wait_ge(s_x[u], i * 16 + 16)
                if not (isinstance(i, int) and i + u == 0):
                    act.wait_ge(s_sq, i * 2 + u)
                act.activation(junk[:], xt[u][:], ACT.Square, scale=D ** -0.5, accum_out=ssq[:, u, 0:1]).then_inc(s_sq, 1)

            def out_h(i, u):
                for g in range(2):
                    act.wait_ge(s_T, i * NGR + (HG[u] + g + 1))
                    act.activation(hT[u][:, 4 * g:4 * g + 4], psT[:, (HG[u] + g) % 3].rearrange("p (k n) -> p k n", k=4),
                                   ACT.Copy).then_inc(s_Te, 5 if isinstance(i, int) and i == 0 and g == 1 else 1)

            def out_chunk(i, u, c):
                if skipped(i, c):
                    return
                act.wait_ge(s_ch, i * 10 + (5 * u + c + 1))
                if c == 1 and u == 1:
                    act.wait_ge(s_rope, i * 2 + 1)
                if c == 1 and u == 0 and not (isinstance(i, int) and i == 0):
                    act.wait_ge(s_rope, i * 2)
                for o, w, kind, at in CH[c][2]:
                    src = psC[:, c, o:o + w]
                    if kind == "gq":
                        src = src.rearrange("p (a j d) -> p a j d", a=2, d=HD)
                        dst = qk[:, at:at + w].rearrange("p (j a d) -> p a j d", a=2, d=HD)
                    elif kind == "qk":
                        dst = qk[:, at:at + w]
                    else:
                        dst = vv[:, ds(i * 2 + u, 1), at:at + w].rearrange("p o n -> p (o n)")
                    ins = act.activation(dst, src, ACT.Copy)
                ins.then_inc(s_che, 3 if skipped(i, 3) and c == 2 else 1)

            def out_qk(i, u, first=False):
                for g, (cols, kind, at) in enumerate(QKG):
                    n = g + (4 * u if isinstance(i, int) and i == TURNS - 1 else QG[u])
                    act.wait_ge(s_T, first_qk(i, u) + (g + 1))
                    w = len(cols) * P
                    src = psT[:, n % 3, 0:w].rearrange("p (k n) -> p k n", n=P)
                    if kind == "k":
                        dst = kT[:, at:at + len(cols), ds(i * (2 * P) + u * P, P)]
                    else:
                        dst = qTs[:, at:at + 4]
                        if at == 0 and (u == 1 or not first):
                            act.wait_ge(s_qd, i * 64 + 32 * u)
                    act.activation(dst, src, ACT.Copy).then_inc(s_Te, 1)

            def turn(i, first=False, second=False, last=False):
                for u in range(2):
                    out_h(i, u)
                    if u == 1 and not last:
                        square(i + 1, 0)
                    if not first:
                        out_qk(i - 1, u, second)
                    for c in range(5):
                        out_chunk(i, u, c)
                        if c == 2 and u == 1 and not last:
                            square(i + 1, 1)

            square(0, 0)
            square(0, 1)
            turn(0, first=True)
            turn(1, second=True)
            with act.Fori(2, TURNS - 1) as i:
                turn(i)
            turn(TURNS - 1, last=True)
            out_qk(TURNS - 1, 0)
            out_qk(TURNS - 1, 1)

        @block.gpsimd
        def _(pool):
            def rstd_h(i, u, own):
                pool.wait_ge(s_sq, i * 2 + (u + 1))
                nc.gpsimd.tensor_tensor(ssq[:, u, 1:2], ssq[:, u, 0:1], mhalf[:, 16:17], ALU.add).then_inc(s_pool, 1)
                pool.wait_ge(s_pool, own)
                nc.gpsimd.tensor_tensor(ssq[:, u, 1:2], ssq[:, u, 1:2], mhalf[:, 0:1], ALU.pow).then_inc(s_rh, 1)

            def rstd_heads(i, u, own):
                pool.wait_ge(s_hv, i * 2 + (u + 1))
                nc.gpsimd.tensor_tensor(hss[:, 16:26], hss[:, 0:10], mhalf[:, 16:26], ALU.add).then_inc(s_pool, 1)
                pool.wait_ge(s_pool, own)
                nc.gpsimd.tensor_tensor(hss[:, 16:26], hss[:, 16:26], mhalf[:, 0:10], ALU.pow).then_inc(s_rr, 1)

            def turn(i, last):
                rstd_heads(i, 0, i * 4 + 3)
                if not last:
                    rstd_h(i + 1, 0, i * 4 + 4)
                    rstd_h(i + 1, 1, i * 4 + 5)
                rstd_heads(i, 1, i * 4 + (4 if last else 6))

            rstd_h(0, 0, 1)
            rstd_h(0, 1, 2)
            with pool.Fori(0, TURNS - 1) as i:
                turn(i, False)
            turn(TURNS - 1, True)

        @block.vector
        def _(dve):
            HEAD, STEPS = 3, 2 * (1 + 6 + 1)

            def make_h(step, u, i):
                dve.wait_ge(s_rh, i * 2 + (u + 1))
                sc = ssq[:, u, 1:2]
                ra, rb = (A1C, B1C) if isinstance(i, int) and i == 0 else (A1, B1)
                step(nc.vector.scalar_tensor_tensor(xt[u][:], xt[u][:], sc, rows[:, ra], ALU.mult, ALU.mult))
                nc.vector.tensor_tensor(xt[u][:], xt[u][:], rows[:, rb], ALU.add).then_inc(s_h, 1)

            def rotary(step, u, i):
                dve.wait_ge(s_che, i * 10 + (5 * u + 5))
                ctx = isinstance(i, int) and i == 0
                if u == 1:
                    dve.wait_ge(s_T, first_qk(i, 0) + 4)
                elif not ctx:
                    dve.wait_ge(s_T, i * NGR + (QG[1] + 4))
                normed = [(1536, 2, gk, 8), (512, 8, gq, 0)][:1 if ctx else 2]
                at0 = 1024 if ctx else 0
                nh0 = (QKW - at0) // HD
                for at, nh, gain, hs in normed:
                    X = qk[:, at:at + nh * HD].rearrange("p (h d) -> p h d", d=HD)
                    J = t2[:, at:at + nh * HD].rearrange("p (h d) -> p h d", d=HD)
                    step(nc.vector.scalar_tensor_tensor(J, X, 1.0 / HD, X, ALU.mult, ALU.mult))
                    ins = nc.vector.tensor_reduce(hss[:, hs:hs + nh], J, AX.X, ALU.add)
                ins.then_inc(s_hv, 1)
                dve.wait_ge(s_rr, i * 2 + (u + 1))
                if ctx and u == 0:
                    dve.wait_ge(s_gain, 32)
                for at, nh, gain, hs in normed:
                    X = qk[:, at:at + nh * HD].rearrange("p (h d) -> p h d", d=HD)
                    r = hss[:, 16 + hs:16 + hs + nh]
                    step(nc.vector.tensor_tensor(X, X, r.unsqueeze(2).broadcast_to([P, nh, HD]), ALU.mult))
                    step(nc.vector.tensor_tensor(X, X, gain[:].unsqueeze(1).broadcast_to([P, nh, HD]), ALU.mult))
                dve.wait_ge(s_rt[u], i * 16 + 16)
                cosb = rt[u][:, 0:1, :].broadcast_to([P, nh0, HD])
                nc.vector.tensor_tensor(t1[:, at0:].rearrange("p (h d) -> p h d", d=HD),
                                        qk[:, at0:].rearrange("p (h d) -> p h d", d=HD), cosb, ALU.mult)
                for f in range(2):
                    X5 = qk[:, at0:].rearrange("p (h f s d) -> p f h s d", f=2, s=2, d=16)[:, f]
                    T5 = t2[:, at0:].rearrange("p (h f s d) -> p f h s d", f=2, s=2, d=16)[:, f]
                    S5 = rt[u][:, 1, :].rearrange("p (f s d) -> p f s d", f=2, s=2)[:, f]
                    for s_ in range(2):
                        ins = nc.vector.tensor_tensor(T5[:, :, s_], X5[:, :, 1 - s_],
                                                      S5[:, s_:s_ + 1].broadcast_to([P, nh0, 16]), ALU.mult)
                step(ins)
                nc.vector.tensor_tensor(t1[:, at0:], t1[:, at0:], t2[:, at0:], ALU.add).then_inc(s_rope, 1)

            def turn(i, last, base):
                step = chain(dve, s_dve, base)
                rotary(step, 0, i)
                if not last:
                    make_h(step, 0, i + 1)
                    make_h(step, 1, i + 1)
                rotary(step, 1, i)
                assert step.n[0] == (10 if isinstance(i, int) and i == 0 else 14 if last else STEPS), step.n[0]

            step = chain(dve, s_dve)
            nc.vector.memset(t1[:, 0:1024], 0.0)
            step(nc.vector.memset(hss[:], 1.0))
            make_h(step, 0, 0)
            make_h(step, 1, 0)
            turn(0, False, HEAD)
            with dve.Fori(1, TURNS - 1) as i:
                turn(i, False, i * STEPS + (HEAD - 6))
            turn(TURNS - 1, True, (TURNS - 1) * STEPS + (HEAD - 6))

        @block.tensor
        def _(pe):
            def bank_free(i, n):
                if isinstance(i, int) and i * NGR + n < 3:
                    return
                pe.wait_ge(s_Te, i * NGR + (n - 2))

            def t_h(i, u):
                pe.wait_ge(s_h, i * 2 + (u + 1))
                for g in range(2):
                    bank_free(i, HG[u] + g)
                    for k in range(4):
                        c = (4 * g + k) * P
                        last = nc.tensor.transpose(psT[:, (HG[u] + g) % 3, k * P:(k + 1) * P], xt[u][:, c:c + P], ident[:])
                    last.then_inc(s_T, 5 if isinstance(i, int) and i == 0 and g == 1 else 1)

            def chunks(i, u):
                for c, (src, w, _) in enumerate(CH):
                    if skipped(i, c):
                        continue
                    if c == 0:
                        pe.wait_ge(s_Te, i * NGR + (HG[u] + 2))
                    if not (isinstance(i, int) and i == 0 and u == 0):
                        pe.wait_ge(s_che, i * 10 + (5 * (u - 1) + c + 1))
                    for k in range(KD):
                        last = nc.tensor.matmul(psC[:, c, 0:w], hT[u][:, k], w_in[:, k, src:src + w],
                                                start=(k == 0), stop=(k == KD - 1))
                    last.then_inc(s_ch, 3 if skipped(i, 3) and c == 2 else 1)

            def t_qk(i, u):
                pe.wait_ge(s_rope, i * 2 + (u + 1))
                for g, (cols, _, _) in enumerate(QKG):
                    n = g + (4 * u if isinstance(i, int) and i == TURNS - 1 else QG[u])
                    pe.wait_ge(s_Te, first_qk(i, u) + (g - 2))
                    for k, c in enumerate(cols):
                        last = nc.tensor.transpose(psT[:, n % 3, k * P:(k + 1) * P], t1[:, c:c + P], ident[:])
                    last.then_inc(s_T, 1)

            def turn(i, first=False):
                for u in range(2):
                    t_h(i, u)
                    if not first:
                        t_qk(i - 1, u)
                    chunks(i, u)

            pe.wait_ge(s_win, KD * 16)
            turn(0, True)
            with pe.Fori(1, TURNS) as i:
                turn(i)
            t_qk(TURNS - 1, 0)
            t_qk(TURNS - 1, 1)


def attention(b, a, ident, nlam, mhalf, vv, qT_d, kT_d, o_d):
    nc = b.nc
    NKH = 10
    KORDER = [8, 9, 0, 1, 2, 3, 4, 5, 6, 7]
    NAD = 4
    CW = [(0, 512), (512, 512), (1024, 256)]

    def pair(k):
        return (k // 2 + DH) % NP

    with ExitStack() as ph:
        qd = b.sb(ph, "q_twice", [P, 2, NP * P])
        q2 = b.sb(ph, "q_high_low", [P, 2, NP * P], F32R)
        ks = b.sb(ph, "k_twice", [P, 3, KEYS])
        kh = b.sb(ph, "k_high", [P, NKH, KEYS], F32R)
        kl = b.sb(ph, "k_low", [P, NKH, KEYS], F32R)
        pr = b.sb(ph, "probs", [P, 2, KEYS])
        pT = b.sb(ph, "probsT", [P, 2, KT_N, P])
        mx = b.sb(ph, "chunk_max", [P, 4, 4])
        nb = b.sb(ph, "neg_max", [P, 4])
        sm = b.sb(ph, "chunk_sum", [P, 4, 4])
        rs = b.sb(ph, "row_scale", [P, 8])
        o1 = b.sb(ph, "o_first", [P, DIFF_V])
        o2 = b.sb(ph, "o_diff", [P, DIFF_V])
        oj = b.sb(ph, "o_square", [P, DIFF_V])
        ob = b.sb(ph, "o_tile", [P, D])
        sg = b.sb(ph, "sub_gain", [P, DIFF_V])
        psS = b.pb(ph, "ps_scores", [P, 3, 512])
        psP = b.pb(ph, "ps_probsT", [P, 3, 512])
        psO = b.pb(ph, "ps_out", [P, 2, 512])
        s_q = [b.sem(ph, f"qT_loaded{h}") for h in range(2)]
        s_qh = [b.sem(ph, f"q_high_ready{h}") for h in range(2)]
        s_ql = [b.sem(ph, f"q_low_ready{h}") for h in range(2)]
        s_ka = [b.sem(ph, f"k_loaded{h}") for h in range(NAD)]
        s_ks = [b.sem(ph, f"k_last_loaded{h}") for h in range(NKH - NAD)]
        s_kh = b.sem(ph, "k_high_ready")
        s_kl = b.sem(ph, "k_low_ready")
        s_kph = b.sem(ph, "k_high_by_pool")
        s_kpl = b.sem(ph, "k_low_by_pool")
        s_g = b.sem(ph, "sub_gain_loaded")
        s_qk = b.sem(ph, "scores_chunk")
        s_nb = b.sem(ph, "neg_max_ready")
        s_exp = b.sem(ph, "probs_chunk")
        s_tp = b.sem(ph, "probsT_chunk")
        s_pta = b.sem(ph, "probsT_by_act")
        s_ptd = b.sem(ph, "probsT_by_dve")
        s_pv = b.sem(ph, "pv_done")
        s_of = b.sem(ph, "o_bank_read")
        s_ov = b.sem(ph, "o_mean_square")
        s_or = b.sem(ph, "o_rstd")
        s_ob = b.sem(ph, "o_part")
        s_od = b.sem(ph, "o_stored")
        s_obfree = b.sem(ph, "o_tile_free")
        s_carry = b.sem(ph, "a_carry")
        s_dve = b.sem(ph, "a_dve")
        block = ph.enter_context(nc.Block())
        C3 = 3 * NH

        HALF = NP // 2

        def k_slot(n):
            return ks[:, (n - 4) % 3] if n >= 4 else (pr if n < 2 else pT[:].rearrange("p a t n -> p a (t n)"))[:, n % 2]

        def q_high(act, t, h):
            act.wait_ge(s_q[h], t * 32 + 32)
            act.activation(q2[:, h], qd[:, h], ACT.Copy).then_inc(s_qh[h], 1)

        def q_low(dve, t, h):
            dve.wait_ge(s_qh[h], t + 1)
            nc.vector.tensor_tensor(q2[HD:P, h], qd[HD:P, h], q2[HD:P, h].bitcast(F32), ALU.subtract).then_inc(s_ql[h], 1)

        @block.sync
        def _(sp):
            sp.dma_start(sg[:], a["subln_g"].broadcast_to([P, DIFF_V])).then_inc(s_g, 16)

            def load_q(tile, h):
                for r in range(2):
                    sp.dma_start(qd[r * HD:(r + 1) * HD, h].rearrange("p (j a n) -> p j a n", j=HALF, a=2),
                                 qT_d[ds(tile, 1), :, (1 - h) * HALF:(2 - h) * HALF].rearrange("o p j a n -> (o p) j a n")).then_inc(s_q[h], 16)

            def load_k(n):
                p, h = divmod(KORDER[n], 2)
                for r in range(2):
                    rr = slice(r * HD, (r + 1) * HD)
                    s_ = s_ka[n] if n < NAD else s_ks[n - NAD]
                    sp.dma_start(k_slot(n)[rr], kT_d[p, h * HD:(h + 1) * HD, :]).then_inc(s_, 16)

            load_k(0)
            load_q(NC, 0)
            for n in range(1, NAD + 3):
                load_k(n)
            load_q(NC, 1)
            for n in range(NAD + 3, NKH):
                sp.wait_ge(s_kpl, n - NAD - 2)
                load_k(n)
            with sp.Fori(0, NT - 1) as i:
                for h in range(2):
                    sp.wait_ge(s_ql[h], i + 1)
                    sp.sem_inc(s_carry, 1)
                    load_q(i + (NC + 1), h)
            sp.wait_ge(s_ql[0], NT)
            load_q(NC, 0)

        @block.gpsimd
        def _(pool):
            pool.sem_inc(s_obfree, 1)
            for n in range(NAD, NKH):
                hd = KORDER[n]
                pool.wait_ge(s_ks[n - NAD], 32)
                nc.gpsimd.tensor_copy(kh[:, hd], k_slot(n)).then_inc(s_kph, 1)
                pool.wait_ge(s_kph, n - NAD + 1)
                nc.gpsimd.tensor_tensor(kl[:, hd], k_slot(n), kh[:, hd].bitcast(F32), ALU.subtract).then_inc(s_kpl, 1)
            with pool.Fori(0, NT) as i:
                for p in range(DH):
                    pool.wait_ge(s_ov, i * DH + (p + 1))
                    nc.gpsimd.tensor_tensor(rs[:, 5:6], rs[:, 3:4], mhalf[:, 0:1], ALU.pow).then_inc(s_or, 1)
                pool.wait_ge(s_ob, i * DH + DH)
                pool.wait_ge(s_of, i * NH + (NH + 2))
                pool.sem_inc(s_carry, 1)
                pool.dma_start(o_d[ds(i * P, P), :], ob[:]).then_inc(s_od, 16)
                pool.wait_ge(s_od, i * 16 + 16)
                pool.sem_inc(s_obfree, 1)

        @block.scalar
        def _(act):
            act.sem_inc(s_exp, 3)
            for n in range(NAD):
                act.wait_ge(s_ka[n], 32)
                act.activation(kh[:, KORDER[n]], k_slot(n), ACT.Copy).then_inc(s_kh, 1)
                if n == 0:
                    q_high(act, 0, 0)

            def exps(i, k):
                act.wait_ge(s_nb, i * NH + (k + 1))
                for j, (o, w) in enumerate(CW):
                    act.activation(pr[:, k % 2, o:o + w], psS[:, j, 0:w], ACT.Exp, bias=nb[:, k % 4:k % 4 + 1],
                                   scale=SCALE, accum_out=sm[:, k % 4, j:j + 1]).then_inc(s_exp, 1)

            exps(0, 0)
            with act.Fori(0, NT) as i:
                for k in range(NH):
                    for j in (0, 2):
                        o, w = CW[j]
                        act.wait_ge(s_tp, i * C3 + (3 * k + j + 1))
                        act.activation(pT[:, k % 2, o // P:(o + w) // P], psP[:, j, 0:w].rearrange("p (t n) -> p t n", n=P),
                                       ACT.Copy).then_inc(s_pta, 1)
                    exps(i, k + 1)
                    if k == 2:
                        q_high(act, i, 1)
                    if k == 10:
                        act.wait_ge(s_qk, i * C3 + C3 // 2)
                        q_high(act, i + 1, 0)

        @block.vector
        def _(dve):
            dve.sem_inc(s_of, 2)
            dve.wait_ge(s_g, 16)
            first = chain(dve, s_dve)
            first(nc.vector.tensor_scalar_mul(sg[:], sg[:], 1.0 - LAM_INIT))
            for n in range(NAD):
                hd = KORDER[n]
                dve.wait_ge(s_kh, n + 1)
                nc.vector.tensor_tensor(kl[:, hd], k_slot(n), kh[:, hd].bitcast(F32), ALU.subtract).then_inc(s_kl, 1)
                if n == 0:
                    q_low(dve, 0, 0)
            STEPS = NH * 3 + DH * (2 + 3) + GH * 2

            def maxes(step, i, k):
                for j, (o, w) in enumerate(CW):
                    dve.wait_ge(s_qk, i * C3 + (3 * k + j + 1))
                    ins = nc.vector.reduce_max(mx[:, k % 4, j:j + 1], psS[:, j, 0:w], AX.X)
                    if j == 1:
                        step(ins)
                step(ins)
                step(nc.vector.reduce_max(mx[:, k % 4, 3:4], mx[:, k % 4, 0:3], AX.X))
                nc.vector.tensor_scalar_mul(nb[:, k % 4:k % 4 + 1], mx[:, k % 4, 3:4], -SCALE).then_inc(s_nb, 1)

            maxes(first, 0, 0)
            with dve.Fori(0, NT) as i:
                step = chain(dve, s_dve, i * STEPS + 4)

                def finish(k):
                    p, h = pair(k), k % 2
                    dve.wait_ge(s_pv, i * NH + (k + 1))
                    r = rs[:, 0:1]
                    step(nc.vector.reduce_sum(r, sm[:, k % 4, 0:3], AX.X))
                    step(nc.vector.reciprocal(rs[:, 1:2], r))
                    r = rs[:, 1:2]
                    if p < DH and h == 0:
                        nc.vector.tensor_scalar_mul(o1[:], psO[:, k % 2, 0:DIFF_V], r).then_inc(s_of, 1)
                    elif p < DH:
                        step(nc.vector.tensor_tensor(rs[:, 2:3], r, nlam[:], ALU.mult))
                        dve.wait_ge(s_of, i * NH + (k + 2))
                        nc.vector.scalar_tensor_tensor(o2[:], psO[:, k % 2, 0:DIFF_V], rs[:, 2:3], o1[:], ALU.mult, ALU.add).then_inc(s_of, 1)
                        dve.wait_ge(s_of, i * NH + (k + 3))
                        nc.vector.tensor_tensor_reduce(out=oj[:], in0=o2[:], in1=o2[:], scale=1.0 / DIFF_V, scalar=EPS,
                                                       op0=ALU.mult, op1=ALU.add, accum_out=rs[:, 3:4]).then_inc(s_ov, 1)
                        dve.wait_ge(s_or, i * DH + (p + 1))
                        nc.vector.scalar_tensor_tensor(ob[:, p * DIFF_V:(p + 1) * DIFF_V], o2[:], rs[:, 5:6], sg[:],
                                                       ALU.mult, ALU.mult).then_inc(s_ob, 1)
                    else:
                        j = p - DH
                        at = 512 + (j + 4 * h) * HD
                        nc.vector.tensor_scalar_mul(ob[:, at:at + HD], psO[:, k % 2, 0:HD], r).then_inc(s_of, 1)

                for k in range(NH):
                    maxes(step, i, k + 1)
                    o, w = CW[1]
                    dve.wait_ge(s_tp, i * C3 + (3 * k + 2))
                    nc.vector.tensor_copy(pT[:, k % 2, o // P:(o + w) // P], psP[:, 1, 0:w].rearrange("p (t n) -> p t n", n=P)).then_inc(s_ptd, 1)
                    if k == 2:
                        dve.wait_ge(s_obfree, i + 1)
                    if k >= 2:
                        finish(k - 2)
                    if k == 3:
                        q_low(dve, i, 1)
                    if k == 11:
                        q_low(dve, i + 1, 0)
                finish(NH - 2)
                finish(NH - 1)
                assert step.n[0] == STEPS, step.n[0]

        @block.tensor
        def _(pe):
            def qk_(i, k):
                p, h = pair(k), k % 2
                hd = min(p, 4) * 2 + h
                if k % 8 == 0:
                    pe.wait_ge(s_ql[(k // 8) % 2], i + (k // NH + 1))
                n = KORDER.index(hd)
                if n < NAD:
                    pe.wait_ge(s_kl, n + 1)
                else:
                    pe.wait_ge(s_kpl, n - NAD + 1)
                at = (k % 8) * P
                for j, (o, w) in enumerate(CW):
                    pe.wait_ge(s_exp, i * C3 + (3 * k + j + 1))
                    for part in (kh, kl):
                        last = nc.tensor.matmul(psS[:, j, 0:w], q2[:, (k // 8) % 2, at:at + P], part[:, hd, o:o + w],
                                                start=(part is kh), stop=(part is kl))
                    last.then_inc(s_qk, 1)

            def pv(i, k):
                p, h = pair(k), k % 2
                c, w = (p * DIFF_V, DIFF_V) if p < DH else (512 + h * HD, HD)
                for t in range(KT_N):
                    if t == 0:
                        pe.wait_ge(s_of, i * NH + (k + 1))
                        pe.wait_ge(s_pta, i * (2 * NH) + (2 * k + 1))
                    if t == 4:
                        pe.wait_ge(s_ptd, i * NH + (k + 1))
                    if t == 8:
                        pe.wait_ge(s_pta, i * (2 * NH) + (2 * k + 2))
                    last = nc.tensor.matmul(psO[:, k % 2, 0:w], pT[:, k % 2, t], vv[:, t, c:c + w],
                                            start=(t == 0), stop=(t == KT_N - 1))
                last.then_inc(s_pv, 1)

            qk_(0, 0)
            with pe.Fori(0, NT) as i:
                for k in range(NH):
                    qk_(i, k + 1)
                    for j, (o, w) in enumerate(CW):
                        pe.wait_ge(s_exp, i * C3 + (3 * k + j + 4))
                        if k >= 1:
                            if j == 1:
                                pe.wait_ge(s_ptd, i * NH + k)
                            else:
                                pe.wait_ge(s_pta, i * (2 * NH) + (2 * k - 1 + j // 2))
                        for t in range(w // P):
                            last = nc.tensor.transpose(psP[:, j, t * P:(t + 1) * P], pr[:, k % 2, o + t * P:o + (t + 1) * P], ident[:])
                        last.then_inc(s_tp, 1)
                    if k >= 1:
                        pv(i, k - 1)
                pv(i, NH - 1)


def output_and_router(b, a, ident, rows, s_rows2, mhalf, x1, entry, mask, before, part, count, o_d, h2_d, y_d):
    nc = b.nc
    TURNS = NT // 2
    with ExitStack() as ph:
        w_o = b.sb(ph, "w_out_sb", [P, KD, D])
        w_r = b.sb(ph, "w_router_sb", [P, KD, E])
        w_g = b.sb(ph, "w_shared_gu", [P, KD, 2 * FE])
        w_d = b.sb(ph, "w_shared_down", [P, 2, D])
        bias = b.sb(ph, "router_bias_row", [P, E])
        ot = [b.sb(ph, f"o_in{u}", [P, D]) for u in range(2)]
        xr = [b.sb(ph, f"x_in{u}", [P, D]) for u in range(2)]
        oT = [b.sb(ph, f"oT{u}", [P, KD, P]) for u in range(2)]
        hT = [b.sb(ph, f"h2T{u}", [P, KD, P]) for u in range(2)]
        h2 = [b.sb(ph, f"h2_row{u}", [P, D]) for u in range(2)]
        tmp = b.sb(ph, "row_tmp", [P, D])
        rwb = b.sb(ph, "weight_piece", [P, 3, E], BF16)
        yb = [b.sb(ph, f"y_shared{u}", [P, D]) for u in range(2)]
        aT = b.sb(ph, "act_T", [P, 2, P])
        ga = [b.sb(ph, f"gate_a{u}", [P, FE]) for u in range(2)]
        gb = b.sb(ph, "gate_b", [P, FE])
        junk = b.sb(ph, "square_junk", [P, D], BF16)
        ms = b.sb(ph, "mean_squares", [P, 2, 8])
        sc = b.sb(ph, "scores", [P, 2, E])
        rw = b.sb(ph, "router_work", [P, 6, E])
        g8 = b.sb(ph, "group_top", [P, NG, 8])
        r8 = b.sb(ph, "router_small", [P, 6, 8])
        psT = b.pb(ph, "ps_t", [P, 2, 512])
        psY = b.pb(ph, "ps_y", [P, 4, 512])
        psR = b.pb(ph, "ps_r", [P, 512])
        psG = b.pb(ph, "ps_g", [P, 512])
        S = {n: b.sem(ph, "r_" + n) for n in (
            "weights", "T", "Te", "proj", "sqP", "rs1", "x1", "sqX", "rs2", "h2", "logit", "expR", "gu", "expG",
            "act", "down", "yout", "routed", "h2_stored", "y_stored", "dve", "pool", "hold", "carry", "const")}
        s_o = [b.sem(ph, f"o_loaded{u}") for u in range(2)]
        s_wo = [b.sem(ph, f"w_out_loaded{h}") for h in range(2)]
        s_xr = [b.sem(ph, f"xr_loaded{u}") for u in range(2)]
        block = ph.enter_context(nc.Block())
        GR = 10
        GO, GHT, GA = (0, 2), (4, 6), (8, 9)
        NW = 5

        @block.sync
        def _(sp):
            for u in range(2):
                sp.dma_start(ot[u][:], o_d[u * P:(u + 1) * P, :]).then_inc(s_o[u], 16)
                sp.dma_start(xr[u][:], a["tokens"][CTX + u * P:CTX + (u + 1) * P, :]).then_inc(s_xr[u], 16)
            sp.dma_start(before[:], a["k_before"]).then_inc(S["const"], 16)
            sp.dma_start(part[:, 0:1], a["k_part"]).then_inc(S["const"], 16)
            sp.dma_start(count[:], a["k_count"]).then_inc(S["const"], 16)
            with sp.Fori(0, TURNS - 1) as i:
                for u in range(2):
                    sp.wait_ge(S["T"], i * GR + (GO[u] + 2))
                    sp.dma_start(ot[u][:], o_d[ds(i * (2 * P) + (2 + u) * P, P), :]).then_inc(s_o[u], 16)
                    sp.wait_ge(S["x1"], i * 2 + (u + 1))
                    sp.dma_start(xr[u][:], a["tokens"][ds(i * (2 * P) + (CTX + (2 + u) * P), P), :]).then_inc(s_xr[u], 16)
            sp.wait_ge(S["const"], 48)

        @block.gpsimd
        def _(pool):
            with pool.Fori(0, TURNS) as i:
                for u in range(2):
                    m = ms[:, u]
                    pool.wait_ge(S["sqP"], i * 4 + (2 * u + 2))
                    nc.gpsimd.tensor_tensor(m[:, 2:3], m[:, 0:1], m[:, 1:2], ALU.add).then_inc(S["pool"], 1)
                    pool.wait_ge(S["pool"], i * 6 + (3 * u + 1))
                    nc.gpsimd.tensor_tensor(m[:, 3:4], m[:, 2:3], mhalf[:, 16:17], ALU.add).then_inc(S["pool"], 1)
                    pool.wait_ge(S["pool"], i * 6 + (3 * u + 2))
                    nc.gpsimd.tensor_tensor(m[:, 4:5], m[:, 3:4], mhalf[:, 0:1], ALU.pow).then_inc(S["rs1"], 1)
                    pool.wait_ge(S["sqX"], i * 2 + (u + 1))
                    nc.gpsimd.tensor_tensor(m[:, 6:7], m[:, 5:6], mhalf[:, 16:17], ALU.add).then_inc(S["pool"], 1)
                    pool.wait_ge(S["pool"], i * 6 + (3 * u + 3))
                    nc.gpsimd.tensor_tensor(m[:, 7:8], m[:, 6:7], mhalf[:, 0:1], ALU.pow).then_inc(S["rs2"], 1)
                    pool.wait_ge(S["h2"], i * 2 + (u + 1))
                    pool.sem_inc(S["carry"], 1)
                    pool.dma_start(h2_d[ds(i * (2 * P) + u * P, P), :], h2[u][:]).then_inc(S["h2_stored"], 16)
                for u in range(2):
                    pool.wait_ge(S["yout"], i * 2 + (u + 3))
                    pool.sem_inc(S["carry"], 1)
                    pool.dma_start(y_d[ds(i * (2 * P) + u * P, P), :], yb[u][:]).then_inc(S["y_stored"], 16)
                pool.wait_ge(S["h2_stored"], i * 32 + 32)
                pool.wait_ge(S["y_stored"], i * 32 + 32)
                pool.sem_inc(S["hold"], 1)

        @block.scalar
        def _(act):
            for h in range(2):
                cols = slice(h * 512, (h + 1) * 512)
                act.dma_start(w_o[:, :, cols], a["w_out"][0, :, cols].rearrange("(k p) n -> p k n", p=P)).then_inc(s_wo[h], 16)
            act.dma_start(w_r[:], a["w_router"][0].rearrange("(p k) n -> p k n", k=KD)).then_inc(S["weights"], 16)
            act.dma_start(w_g[:, :, 0:FE], a["w_sh_gate"][0].rearrange("(p k) n -> p k n", k=KD)).then_inc(S["weights"], 16)
            act.dma_start(w_g[:, :, FE:], a["w_sh_up"][0].rearrange("(p k) n -> p k n", k=KD)).then_inc(S["weights"], 16)
            act.dma_start(w_d[:], a["w_sh_down"][0].rearrange("(k p) n -> p k n", p=P)).then_inc(S["weights"], 16)
            act.dma_start(bias[:], a["router_bias"].broadcast_to([P, E])).then_inc(S["weights"], 16)
            act.sem_inc(S["Te"], 2)
            act.sem_inc(S["yout"], 2)
            act.sem_inc(S["expR"], 1)
            with act.Fori(0, TURNS) as i:
                def out_T(dst, n, w=4):
                    act.wait_ge(S["T"], i * GR + (n + 1))
                    act.activation(dst, psT[:, n % 2, 0:w * P].rearrange("p (k n) -> p k n", n=P), ACT.Copy).then_inc(S["Te"], 1)

                def squares(u):
                    for h in range(2):
                        act.wait_ge(S["proj"], i * 4 + (2 * u + h + 1))
                        act.activation(junk[:, h * 512:(h + 1) * 512], psY[:, 2 * u + h], ACT.Square, scale=D ** -0.5,
                                       accum_out=ms[:, u, h:h + 1]).then_inc(S["sqP"], 1)
                    act.wait_ge(S["sqP"], i * 4 + (2 * u + 2))
                    act.wait_ge(S["x1"], i * 2 + (u + 1))
                    act.activation(junk[:], x1[:, ds(i * 2 + u, 1)].rearrange("p o n -> p (o n)"), ACT.Square,
                                   scale=D ** -0.5, accum_out=ms[:, u, 5:6]).then_inc(S["sqX"], 1)
                    act.wait_ge(S["sqX"], i * 2 + (u + 1))

                def exps(u):
                    act.wait_ge(S["logit"], i * 2 + (u + 1))
                    act.activation(sc[:, u], psR[:, 0:E], ACT.Exp, scale=-1.0).then_inc(S["expR"], 1)
                    act.wait_ge(S["gu"], i * 2 + (u + 1))
                    act.activation(ga[u][:], psG[:, 0:FE], ACT.Exp, scale=-1.0).then_inc(S["expG"], 1)

                def y_out(u):
                    for h in range(2):
                        act.wait_ge(S["down"], i * 4 + (2 * u + h + 1))
                        ins = act.activation(yb[u][:, h * 512:(h + 1) * 512], psY[:, 2 * u + h], ACT.Copy)
                    ins.then_inc(S["yout"], 1)

                for u in range(2):
                    for g in range(2):
                        out_T(oT[u][:, 4 * g:4 * g + 4], GO[u] + g)
                squares(0)
                for g in range(2):
                    out_T(hT[0][:, 4 * g:4 * g + 4], GHT[0] + g)
                squares(1)
                exps(0)
                for g in range(2):
                    out_T(hT[1][:, 4 * g:4 * g + 4], GHT[1] + g)
                exps(1)
                for u in range(2):
                    out_T(aT[:], GA[u], 2)
                    if u == 0:
                        act.wait_ge(S["hold"], i + 1)
                    y_out(u)

        @block.vector
        def _(dve):
            STEPS = 2 * (2 + 3 + 23)
            dve.sem_inc(S["hold"], 1)
            dve.sem_inc(S["act"], 1)
            dve.wait_ge(S["weights"], NW * 16)
            dve.wait_ge(s_rows2, 4 * 16)
            with dve.Fori(0, TURNS) as i:
                step = chain(dve, S["dve"], i * STEPS)

                def residual(u):
                    X = x1[:, ds(i * 2 + u, 1)].rearrange("p o n -> p (o n)")
                    dve.wait_ge(s_xr[u], i * 16 + 16)
                    dve.wait_ge(S["rs1"], i * 2 + (u + 1))
                    Y = psY[:, 2 * u:2 * u + 2].rearrange("p b n -> p (b n)")
                    step(nc.vector.scalar_tensor_tensor(tmp[:], Y, ms[:, u, 4:5], rows[:, G1], ALU.mult, ALU.mult))
                    nc.vector.tensor_tensor(X, tmp[:], xr[u][:], ALU.add).then_inc(S["x1"], 1)
                    dve.wait_ge(S["rs2"], i * 2 + (u + 1))
                    dve.wait_ge(S["x1"], i * 2 + (u + 1))
                    step(nc.vector.scalar_tensor_tensor(tmp[:], X, ms[:, u, 7:8], rows[:, A2], ALU.mult, ALU.mult))
                    if u == 0:
                        dve.wait_ge(S["hold"], i + 1)
                    nc.vector.tensor_tensor(h2[u][:].rearrange("p (k q) -> p q k", k=KD), tmp[:].rearrange("p (q k) -> p q k", k=KD),
                                            rows[:, B2].rearrange("p (q k) -> p q k", k=KD), ALU.add).then_inc(S["h2"], 1)

                def shared_act(u):
                    dve.wait_ge(S["expG"], i * 2 + (u + 1))
                    step(nc.vector.tensor_scalar_add(gb[:], ga[u][:], 1.0))
                    step(nc.vector.reciprocal(gb[:], gb[:]))
                    step(nc.vector.tensor_tensor(gb[:], gb[:], psG[:, 0:FE], ALU.mult))
                    nc.vector.tensor_tensor(ga[u][:], gb[:], psG[:, FE:2 * FE], ALU.mult).then_inc(S["act"], 1)

                def route(u):
                    def steph(ins):
                        step(ins)
                        dve.sem_inc(S["carry"], 1)
                    s, sel, m, W = sc[:, u], rw[:, 0], rw[:, 1], rw[:, 2]
                    dve.wait_ge(S["expR"], i * 2 + (u + 2))
                    step(nc.vector.tensor_scalar_add(s, s, 1.0))
                    step(nc.vector.reciprocal(s, s))
                    steph(nc.vector.tensor_tensor(sel, s, bias[:], ALU.add))
                    for g in range(NG):
                        ins = nc.vector.max(g8[:, g], sel[:, g * 8:(g + 1) * 8])
                    step(ins)
                    steph(nc.vector.tensor_tensor(r8[:, 0], g8[:, :, 0], g8[:, :, 1], ALU.add))
                    step(nc.vector.max(r8[:, 1], r8[:, 0]))
                    steph(nc.vector.memset(r8[:, 1, TOPG:8], -BIG))
                    step(nc.vector.match_replace(r8[:, 2], r8[:, 1], r8[:, 0], BIG))
                    step(nc.vector.tensor_scalar(r8[:, 3], r8[:, 2], BIG / 2, None, ALU.is_ge))
                    step(nc.vector.tensor_scalar(r8[:, 4], r8[:, 3], -1.0, BIG, ALU.add, ALU.mult))
                    v3 = lambda t: t.rearrange("p (g e) -> p g e", g=NG)
                    gm = r8[:, 3].unsqueeze(2).broadcast_to([P, NG, 8])
                    pen = r8[:, 4].unsqueeze(2).broadcast_to([P, NG, 8])
                    step(nc.vector.tensor_tensor(v3(m), v3(sel), gm, ALU.mult))
                    steph(nc.vector.tensor_tensor(v3(m), v3(m), pen, ALU.add))
                    steph(nc.vector.max(r8[:, 5], m))
                    step(nc.vector.match_replace(W, r8[:, 5], m, BIG))
                    step(nc.vector.tensor_scalar(rw[:, 3], W, BIG / 2, None, ALU.is_ge))
                    M = mask[:, ds(i * 2 + u, 1)].rearrange("p o e -> p (o e)")
                    nc.vector.tensor_copy(M, rw[:, 3])
                    step(nc.vector.tensor_tensor_reduce(out=W, in0=s, in1=rw[:, 3], scale=1.0, scalar=0.0, op0=ALU.mult,
                                                        op1=ALU.add, accum_out=r8[:, 1, 0:1]))
                    step(nc.vector.reciprocal(r8[:, 1, 1:2], r8[:, 1, 0:1]))
                    step(nc.vector.tensor_scalar(W, W, r8[:, 1, 1:2], ROUTED_SCALE, ALU.mult, ALU.mult))
                    EN = entry[:, ds(i * 2 + u, 1)].rearrange("p o e c -> p (o e) c")
                    for c in range(3):
                        step(nc.vector.tensor_copy(rwb[:, c], W))
                        ins = nc.vector.tensor_copy(EN[:, :, 2 + c], rwb[:, c])
                        if c < 2:
                            step(nc.vector.tensor_tensor(W, W, rwb[:, c], ALU.subtract))
                    ins.then_inc(S["routed"], 1)

                residual(0)
                residual(1)
                shared_act(0)
                route(0)
                shared_act(1)
                route(1)
                assert step.n[0] == STEPS, step.n[0]

        @block.tensor
        def _(pe):
            with pe.Fori(0, TURNS) as i:
                def free(n):
                    pe.wait_ge(S["Te"], i * GR + (n + 1))

                def t8(src, n0):
                    for g in range(2):
                        free(n0 + g)
                        for k in range(4):
                            c = (4 * g + k) * P
                            last = nc.tensor.transpose(psT[:, (n0 + g) % 2, k * P:(k + 1) * P], src[:, c:c + P], ident[:])
                        last.then_inc(S["T"], 1)

                for u in range(2):
                    pe.wait_ge(s_o[u], i * 16 + 16)
                    t8(ot[u], GO[u])
                    pe.wait_ge(S["Te"], i * GR + (GO[u] + 4))
                    pe.wait_ge(S["yout"], i * 2 + (u + 1))
                    for h in range(2):
                        pe.wait_ge(s_wo[h], 16)
                        for k in range(KD):
                            last = nc.tensor.matmul(psY[:, 2 * u + h], oT[u][:, k], w_o[:, k, h * 512:(h + 1) * 512],
                                                    start=(k == 0), stop=(k == KD - 1))
                        last.then_inc(S["proj"], 1)
                pe.wait_ge(S["weights"], NW * 16)
                for u in range(2):
                    pe.wait_ge(S["h2"], i * 2 + (u + 1))
                    t8(h2[u], GHT[u])
                    pe.wait_ge(S["Te"], i * GR + (GHT[u] + 4))
                    pe.wait_ge(S["expR"], i * 2 + (u + 1))
                    for k in range(KD):
                        last = nc.tensor.matmul(psR[:, 0:E], hT[u][:, k], w_r[:, k], start=(k == 0), stop=(k == KD - 1))
                    last.then_inc(S["logit"], 1)
                    pe.wait_ge(S["act"], i * 2 + (u + 1))
                    for k in range(KD):
                        last = nc.tensor.matmul(psG[:], hT[u][:, k], w_g[:, k], start=(k == 0), stop=(k == KD - 1))
                    last.then_inc(S["gu"], 1)
                for u in range(2):
                    pe.wait_ge(S["act"], i * 2 + (u + 2))
                    free(GA[u])
                    for k in range(2):
                        last = nc.tensor.transpose(psT[:, GA[u] % 2, k * P:(k + 1) * P], ga[u][:, k * P:(k + 1) * P], ident[:])
                    last.then_inc(S["T"], 1)
                    pe.wait_ge(S["Te"], i * GR + (GA[u] + 3))
                    for h in range(2):
                        for k in range(2):
                            last = nc.tensor.matmul(psY[:, 2 * u + h], aT[:, k], w_d[:, k, h * 512:(h + 1) * 512],
                                                    start=(k == 0), stop=(k == 1))
                        last.then_inc(S["down"], 1)


def routing_tables(b, ident, before, part, entry, mask, rank, tab):
    nc = b.nc
    with ExitStack() as ph:
        bb = b.sb(ph, "before_bf", [P, P], BF16)
        ones = b.sb(ph, "ones_bf", [P, P], BF16)
        w = b.sb(ph, "table_work", [P, 12, E])
        one = b.sb(ph, "ones_row", [P, E])
        ci = b.sb(ph, "count_int", [P, E], I32)
        col = b.sb(ph, "columns", [P, 8])
        cl = b.sb(ph, "block_columns", [P, 6])
        ps = b.pb(ph, "ps_rank", [P, 512])
        pc = b.pb(ph, "ps_count", [P, 512])
        pt = b.pb(ph, "ps_table", [P, 2, 512])
        s_cst = b.sem(ph, "t_const")
        s_rk = b.sem(ph, "t_rank")
        s_col = b.sem(ph, "t_cols")
        s_row = b.sem(ph, "t_rows")
        s_dve = b.sem(ph, "t_dve")
        block = ph.enter_context(nc.Block())

        @block.gpsimd
        def _(pool):
            for t in range(NT):
                nc.gpsimd.memset(entry[:, t, :, 0], float(t))
            nc.gpsimd.memset(entry[:, :, :, NPC - 1], 1.0)
            nc.gpsimd.tensor_copy(entry[:, :, :, 1].rearrange("p t e -> p (t e)"), part[:, 0:1].broadcast_to([P, NT * E]))

        @block.vector
        def _(dve):
            step = chain(dve, s_dve)
            nc.vector.memset(one[:], 1.0)
            nc.vector.memset(ones[:], 1.0)
            nc.vector.tensor_copy(bb[:], before[:]).then_inc(s_cst, 1)
            dve.wait_ge(s_rk, 2)
            mf = mask[:].rearrange("p t e -> p (t e)")
            rk = rank[:].rearrange("p t e -> p (t e)")
            step(nc.vector.scalar_tensor_tensor(rk, ps[:], 1.0, mf, ALU.add, ALU.mult))
            step(nc.vector.tensor_scalar_add(rk, rk, -1.0))
            cf, nbk, cum, ne, od, cmp, t0, t1, t2, t3 = (w[:, j] for j in range(10))
            step(nc.vector.tensor_scalar_add(cf, pc[:, 0:E], P - 1.0))
            step(nc.vector.tensor_copy(ci[:], cf))
            step(nc.vector.tensor_single_scalar(ci[:], ci[:], 7, ALU.arith_shift_right))
            step(nc.vector.tensor_copy(nbk, ci[:]))
            step(nc.vector.tensor_tensor_scan(cum, one[:], nbk, 0.0, ALU.mult, ALU.add))
            step(nc.vector.tensor_scalar_min(ne, nbk, 1.0))
            step(nc.vector.tensor_tensor_scan(od, one[:], ne, 0.0, ALU.mult, ALU.add))
            lastb, pcl, st, p3 = (col[:, j:j + 1] for j in range(4))
            step(nc.vector.tensor_scalar_add(lastb, cum[:, E - 1:E], -1.0))
            step(nc.vector.tensor_tensor(pcl, part[:, 0:1], lastb, ALU.min))
            step(nc.vector.tensor_scalar(cmp, cum, pcl, None, ALU.is_le))
            step(nc.vector.tensor_tensor(t0, cmp, nbk, ALU.mult))
            step(nc.vector.tensor_tensor(t1, cmp, ne, ALU.mult))
            step(nc.vector.reduce_sum(cl[:, 0:1], cmp, AX.X))
            step(nc.vector.reduce_sum(st, t0, AX.X))
            step(nc.vector.reduce_sum(cl[:, 2:3], t1, AX.X))
            step(nc.vector.tensor_tensor(cl[:, 1:2], part[:, 0:1], st, ALU.subtract))
            step(nc.vector.tensor_scalar_min(cl[:, 1:2], cl[:, 1:2], 8.0))
            step(nc.vector.tensor_scalar(t2, od, part[:, 0:1], None, ALU.is_le))
            step(nc.vector.reduce_sum(cl[:, 3:4], t2, AX.X))
            step(nc.vector.tensor_scalar_add(p3, part[:, 0:1], -(WS - 1.0)))
            step(nc.vector.tensor_scalar(t3, od, p3, None, ALU.is_le))
            step(nc.vector.tensor_tensor(t3, t3, nbk, ALU.mult))
            step(nc.vector.reduce_sum(cl[:, 4:5], t3, AX.X))
            step(nc.vector.tensor_scalar_min(cl[:, 3:4], cl[:, 3:4], E - 1.0))
            nc.vector.tensor_copy(cl[:, 5:6], lastb).then_inc(s_col, 1)
            dve.wait_ge(s_row, 1)
            for c in range(6):
                nc.vector.tensor_copy(tab[0:1, c, 0:P], pt[0:1, c // 3, (c % 3) * P:(c % 3 + 1) * P])
                step(nc.vector.tensor_copy(tab[0:1, c, P:P + 8],
                                           pt[0:1, c // 3, (c % 3 + 1) * P - 1:(c % 3 + 1) * P].broadcast_to([1, 8])))
            step(nc.vector.tensor_scalar_add(cl[0:1, 0:1], cum[0:1, E - 1:E], 0.0))
            step(nc.vector.tensor_copy(tab[0:1, 5, 0:1], cl[0:1, 0:1]))
            step(nc.vector.tensor_copy(tab[0:1, 5, 1:2], od[0:1, E - 1:E]))
            step(nc.vector.tensor_scalar_add(tab[0:1, 5, 2:3], tab[0:1, 5, 0:1], 1))
            nc.vector.tensor_single_scalar(tab[0:1, 5, 2:3], tab[0:1, 5, 2:3], 1, ALU.arith_shift_right)

        @block.tensor
        def _(pe):
            pe.wait_ge(s_cst, 1)
            for t in range(NT):
                nc.tensor.matmul(ps[:, t * E:(t + 1) * E], bb[:], mask[:, t], start=True, stop=(t == 0))
                for q in range(t):
                    nc.tensor.matmul(ps[:, t * E:(t + 1) * E], ones[:], mask[:, q], start=False, stop=(q == t - 1))
            for t in range(NT):
                last = nc.tensor.matmul(pc[:, 0:E], ones[:], mask[:, t], start=(t == 0), stop=(t == NT - 1))
            last.then_inc(s_rk, 2)
            pe.wait_ge(s_col, 1)
            for c in range(6):
                last = nc.tensor.matmul(pt[0:1, c // 3, (c % 3) * P:(c % 3 + 1) * P], cl[:, c:c + 1], ident[:],
                                        start=True, stop=True)
            last.then_inc(s_row, 1)


def experts(b, a, ident, part, count, entry, rank, tab, h2_d, y_d):
    nc = b.nc
    RING = 8
    with ExitStack() as ph:
        wgu = b.sb(ph, "w_gate_up", [P, WS, KD, 2 * FE])
        wdn = b.sb(ph, "w_down", [P, WS, 2, D])
        oh = b.sb(ph, "one_hot", [P, NT, P], BF16)
        xg = [b.sb(ph, f"gathered{u}", [P, D]) for u in range(2)]
        hT = b.sb(ph, "gatheredT", [P, KD, P])
        ga = b.sb(ph, "e_gate_a", [P, FE])
        gb = b.sb(ph, "e_gate_b", [P, FE])
        aH = b.sb(ph, "e_actT_high", [P, 2, P], F32R)
        aL = b.sb(ph, "e_actT_low", [P, 2, P], F32R)
        dh = b.sb(ph, "w_down_high", [P, 2, D], F32R)
        dl = b.sb(ph, "w_down_low", [P, 2, D], F32R)
        yb = [b.sb(ph, f"e_y{u}", [P, D]) for u in range(2)]
        pc = b.sb(ph, "e_pieces", [P, 8])
        tk = b.sb(ph, "e_token", [P, 4])
        wr = b.sb(ph, "e_weight_ring", [P, RING])
        sr = b.sb(ph, "e_target_ring", [P, RING])
        wn = b.sb(ph, "e_weight", [P, 2])
        ti = [b.sb(ph, f"e_gather_index{u}", [P, 1], U32) for u in range(2)]
        si = [b.sb(ph, f"e_target_index{u}", [P, 1], U32) for u in range(2)]
        psX = b.pb(ph, "ps_x", [P, 2, 512])
        psG = b.pb(ph, "ps_gu", [P, 512])
        psA = b.pb(ph, "ps_a", [P, 512])
        psY = b.pb(ph, "ps_ye", [P, 2, 512])
        psI = b.pb(ph, "ps_i", [P, 512])
        S = {n: b.sem(ph, "e_" + n) for n in (
            "oh", "pieces", "piecesout", "tok", "xT", "hT", "gu", "exp", "act", "aTp",
            "aH", "aL", "dh", "dl", "dn", "y0", "y1", "target", "scat", "scatok", "landed", "dve", "carry", "zeroed")}
        s_gather = [b.sem(ph, f"e_gathered{u}") for u in range(2)]
        s_w = [b.sem(ph, f"e_weights_loaded{u}") for u in range(WS)]
        block = ph.enter_context(nc.Block())

        def read(eng, c, at, hi):
            return eng.value_load(tab[0:1, c, ds(at, 1)], min_val=0, max_val=hi)

        def blocks(eng, body):
            turns = eng.value_load(tab[0:1, 5, 2:3], min_val=1, max_val=NBLK // 2)
            with eng.Fori(0, turns) as i:
                for u in range(2):
                    body(i, i * 2 + u, u)
            return turns

        @block.sync
        def _(sp):
            loaded = sp.value_load(tab[0:1, 5, 1:2], min_val=1, max_val=E)

            def load(n, u):
                e = read(sp, 3, n, E - 1)
                sp.dma_start(wgu[:, u, :, 0:FE], a["w_exp_gate"][0, ds(e, 1)].rearrange("o (p k) n -> (o p) k n", k=KD)).then_inc(s_w[u], 16)
                sp.dma_start(wgu[:, u, :, FE:], a["w_exp_up"][0, ds(e, 1)].rearrange("o (p k) n -> (o p) k n", k=KD)).then_inc(s_w[u], 16)
                sp.dma_start(wdn[:, u], a["w_exp_down"][0, ds(e, 1)].rearrange("o (k p) n -> p (o k) n", p=P)).then_inc(s_w[u], 16)

            load(0, 0)
            sp.wait_ge(s_gather[1], 16)
            with sp.Fori(0, E // WS) as i:
                for u in range(WS):
                    n = i * WS + (u + 1)
                    with sp.If(n < loaded):
                        done = read(sp, 4, n, NBLK)
                        sp.wait_ge(S["dn"], done * 2 + 1)
                        load(n, (u + 1) % WS)
                        sp.wait_ge(s_w[u], i * 48 + 48)
                        sp.sem_inc(S["landed"], 1)
            for u in range(WS):
                with sp.If(((loaded + (WS - 1)) & (WS - 1)) == u):
                    sp.wait_ge(s_w[u], ((loaded + (WS - 1)) // WS) * 48)
                    sp.sem_inc(S["landed"], 1)

        @block.gpsimd
        def _(pool):
            def gather(n, u, first=False):
                pool.wait_ge(S["tok"], n + 1)
                if not first:
                    pool.wait_ge(S["xT"], n * 2 - 2)
                pool.sem_inc(S["carry"], 1)
                pool.indirect_dma_start(xg[u][:], None, h2_d, bass.IndirectOffsetOnAxis(ap=ti[u][:, 0:1], axis=0),
                                        bounds_check=SEQ - 1).then_inc(s_gather[u], 16)

            def body(i, n, u):
                gather(n + 3, 1 - u)
                pool.wait_ge(S["scat"], n * 16 + 16)
                pool.sem_inc(S["scatok"], 1)
                pool.wait_ge(S["y0"], n + 2)
                pool.wait_ge(S["y1"], n + 2)
                pool.sem_inc(S["carry"], 1)
                pool.indirect_dma_start(y_d, bass.IndirectOffsetOnAxis(ap=si[u][:, 0:1], axis=0), yb[u][:], None,
                                        bounds_check=SEQ + P - 1, compute_op=ALU.add).then_inc(S["scat"], 16)

            nc.gpsimd.memset(yb[1][:], 0.0).then_inc(S["zeroed"], 1)
            pool.wait_ge(S["zeroed"], 1)
            pool.dma_start(y_d[SEQ:SEQ + P, :], yb[1][:]).then_inc(S["scat"], 16)
            pool.sem_inc(S["scatok"], 1)
            gather(0, 0, True)
            gather(1, 1, True)
            gather(2, 0)
            turns = blocks(pool, body)
            pool.wait_ge(s_gather[0], turns * 16 + 32)
            pool.wait_ge(s_gather[1], turns * 16 + 16)
            pool.wait_ge(S["scat"], turns * 32 + 16)

        @block.scalar
        def _(act):
            def out_x(n):
                for g in range(2):
                    act.wait_ge(S["xT"], n * 2 + (g + 1))
                    act.activation(hT[:, 4 * g:4 * g + 4], psX[:, g].rearrange("p (k n) -> p k n", n=P), ACT.Copy).then_inc(S["hT"], 1)

            def out_exp(n):
                act.wait_ge(S["gu"], n + 1)
                act.activation(ga[:], psG[:, 0:FE], ACT.Exp, scale=-1.0).then_inc(S["exp"], 1)

            def out_a(n):
                act.wait_ge(S["aTp"], n + 1)
                act.activation(aH[:], psA[:, 0:2 * P].rearrange("p (k n) -> p k n", n=P), ACT.Copy).then_inc(S["aH"], 1)

            def down_high(n, head=False):
                q = read(act, 2, n, E - 1)
                act.wait_ge(S["landed"], q + 1)
                if not head:
                    act.wait_ge(S["dn"], n * 2 + 1)
                act.activation(dh[:], wdn[:, ds(q & (WS - 1), 1)].rearrange("p o k n -> p (o k) n"), ACT.Copy).then_inc(S["dh"], 1)

            def body(i, n, u):
                out_exp(n + 1)
                out_x(n + 2)
                act.wait_ge(S["target"], n + 1)
                act.wait_ge(S["dn"], n * 2 + 2)
                act.activation(yb[u][:, 0:512], psY[:, 0], ACT.Copy, scale=wn[:, u:u + 1]).then_inc(S["y0"], 1)
                down_high(n + 1)
                out_a(n + 1)

            act.sem_inc(S["y0"], 1)
            out_x(0)
            out_exp(0)
            out_x(1)
            down_high(0, True)
            out_a(0)
            blocks(act, body)

        @block.vector
        def _(dve):
            HEAD, STEPS = 1 + 4 * 6 + 3, 3 + 6 + 1
            dve.sem_inc(S["y1"], 1)
            first = chain(dve, S["dve"])
            first(nc.vector.tensor_scalar_add(part[:, 1:2], part[:, 0:1], float(SEQ)))

            def one_hot(n, head=False):
                e = read(dve, 0, n, E - 1)
                j = read(dve, 1, n, 8)
                if not head:
                    dve.wait_ge(S["pieces"], n)
                nc.vector.tensor_tensor(oh[:], count[:, ds(j * P, P)].unsqueeze(1).broadcast_to([P, NT, P]),
                                        rank[:, :, ds(e, 1)].broadcast_to([P, NT, P]), ALU.is_equal).then_inc(S["oh"], 1)

            def indices(n, turn, u, step, head=False):
                dve.wait_ge(S["pieces"], n + 1)
                nc.vector.tensor_copy(pc[:, 0:NPC], psI[:, 0:NPC]).then_inc(S["piecesout"], 1)
                dve.wait_ge(S["piecesout"], n + 1)
                at = n & (RING - 1)
                W, T = wr[:, ds(at, 1)], sr[:, ds(at, 1)]
                step(nc.vector.scalar_tensor_tensor(tk[:, 0:1], pc[:, 0:1], float(P), pc[:, 1:2], ALU.mult, ALU.add))
                step(nc.vector.tensor_scalar(tk[:, 1:2], pc[:, NPC - 1:NPC], -1.0, 1.0, ALU.mult, ALU.add))
                step(nc.vector.tensor_tensor(tk[:, 1:2], tk[:, 1:2], part[:, 1:2], ALU.mult))
                step(nc.vector.tensor_tensor(T, tk[:, 0:1], tk[:, 1:2], ALU.add))
                step(nc.vector.tensor_tensor(tk[:, 2:3], pc[:, 2:3], pc[:, 3:4], ALU.add))
                step(nc.vector.tensor_tensor(W, tk[:, 2:3], pc[:, 4:5], ALU.add))
                if not head:
                    dve.wait_ge(s_gather[u], turn * 16)
                nc.vector.tensor_copy(ti[u][:], tk[:, 0:1]).then_inc(S["tok"], 1)

            def gate(n, step):
                dve.wait_ge(S["exp"], n + 1)
                step(nc.vector.tensor_scalar_add(gb[:], ga[:], 1.0))
                step(nc.vector.reciprocal(gb[:], gb[:]))
                step(nc.vector.tensor_tensor(gb[:], gb[:], psG[:, 0:FE], ALU.mult))
                nc.vector.tensor_tensor(ga[:], gb[:], psG[:, FE:2 * FE], ALU.mult).then_inc(S["act"], 1)

            def down_low(n):
                dve.wait_ge(S["dh"], n + 1)
                q = read(dve, 2, n, E - 1)
                nc.vector.tensor_tensor(dl[:], wdn[:, ds(q & (WS - 1), 1)].rearrange("p o k n -> p (o k) n"),
                                        dh[:].bitcast(F32), ALU.subtract).then_inc(S["dl"], 1)

            def act_low(n):
                dve.wait_ge(S["aH"], n + 1)
                nc.vector.tensor_tensor(aL[:], psA[:, 0:2 * P].rearrange("p (k n) -> p k n", n=P),
                                        aH[:].bitcast(F32), ALU.subtract).then_inc(S["aL"], 1)

            def body(i, n, u):
                step = chain(dve, S["dve"], n * STEPS + HEAD)
                dve.wait_ge(S["scatok"], n + 1)
                step(nc.vector.tensor_copy(wn[:, u:u + 1], wr[:, ds(n & (RING - 1), 1)]))
                nc.vector.tensor_copy(si[u][:], sr[:, ds(n & (RING - 1), 1)]).then_inc(S["target"], 1)
                gate(n + 1, step)
                dve.wait_ge(S["dn"], n * 2 + 3)
                nc.vector.tensor_scalar_mul(yb[u][:, 512:1024], psY[:, 1], wn[:, u:u + 1]).then_inc(S["y1"], 1)
                indices(n + 4, i + 2, u, step)
                down_low(n + 1)
                one_hot(n + 5)
                act_low(n + 1)
                assert step.n[0] == STEPS

            one_hot(0, True)
            indices(0, 0, 0, first, True)
            one_hot(1)
            indices(1, 0, 1, first, True)
            one_hot(2)
            indices(2, 1, 0, first)
            one_hot(3)
            gate(0, first)
            indices(3, 1, 1, first)
            one_hot(4)
            down_low(0)
            act_low(0)
            assert first.n[0] == HEAD
            blocks(dve, body)

        @block.tensor
        def _(pe):
            def pieces(n, head=False):
                e = read(pe, 0, n, E - 1)
                pe.wait_ge(S["oh"], n + 1)
                if not head:
                    pe.wait_ge(S["piecesout"], n)
                for t in range(NT):
                    last = nc.tensor.matmul(psI[:, 0:NPC], oh[:, t], entry[:, t, ds(e, 1)].rearrange("p o c -> p (o c)"),
                                            start=(t == 0), stop=(t == NT - 1))
                last.then_inc(S["pieces"], 1)

            def t_x(turn, u):
                pe.wait_ge(s_gather[u], turn * 16 + 16)
                for g in range(2):
                    for k in range(4):
                        c = (4 * g + k) * P
                        last = nc.tensor.transpose(psX[:, g, k * P:(k + 1) * P], xg[u][:, c:c + P], ident[:])
                    last.then_inc(S["xT"], 1)

            def gate_up(n, q):
                pe.wait_ge(S["landed"], q + 1)
                pe.wait_ge(S["hT"], n * 2 + 2)
                for k in range(KD):
                    last = nc.tensor.matmul(psG[:], hT[:, k], wgu[:, ds(q & (WS - 1), 1), k].rearrange("p o n -> p (o n)"),
                                            start=(k == 0), stop=(k == KD - 1))
                last.then_inc(S["gu"], 1)

            def down(n):
                pe.wait_ge(S["aL"], n + 1)
                pe.wait_ge(S["dl"], n + 1)
                pe.wait_ge(S["y0"], n + 1)
                pe.wait_ge(S["y1"], n + 1)
                for h in range(2):
                    for j, (A, W) in enumerate(((aH, dh), (aH, dl), (aL, dh))):
                        for k in range(2):
                            last = nc.tensor.matmul(psY[:, h], A[:, k], W[:, k, h * 512:(h + 1) * 512],
                                                    start=(j + k == 0), stop=(j + k == 3))
                    last.then_inc(S["dn"], 1)

            def t_a(n):
                pe.wait_ge(S["act"], n + 1)
                for k in range(2):
                    last = nc.tensor.transpose(psA[:, k * P:(k + 1) * P], ga[:, k * P:(k + 1) * P], ident[:])
                last.then_inc(S["aTp"], 1)

            def body(i, n, u):
                q = read(pe, 2, n + 1, E - 1)
                t_a(n)
                gate_up(n + 1, q)
                t_x(i + 1, u)
                down(n)
                pieces(n + 4)

            pe.sem_inc(S["dn"], 1)
            pieces(0, True)
            pieces(1)
            t_x(0, 0)
            pieces(2)
            gate_up(0, read(pe, 2, 0, E - 1))
            pieces(3)
            t_x(0, 1)
            turns = blocks(pe, body)
            t_a(turns * 2)


def final(b, a, rows, mhalf, x1, y_d, out):
    nc = b.nc
    with ExitStack() as ph:
        yt = b.sb(ph, "y_tiles", [P, NT, D])
        junk = b.sb(ph, "f_square", [P, 2, D], BF16)
        ms = b.sb(ph, "f_mean", [P, 3, NT])
        s_y = [b.sem(ph, f"y_loaded{t}") for t in range(NT)]
        s_sq = b.sem(ph, "f_sq")
        s_rs = b.sem(ph, "f_rs")
        s_pool = b.sem(ph, "f_pool")
        s_o = b.sem(ph, "f_out")
        s_dve = b.sem(ph, "f_dve")
        s_st = b.sem(ph, "f_stored")
        block = ph.enter_context(nc.Block())

        @block.sync
        def _(sp):
            for t in range(NT):
                sp.dma_start(yt[:, t], y_d[t * P:(t + 1) * P, :]).then_inc(s_y[t], 16)
            for t in range(NT):
                sp.wait_ge(s_o, t + 1)
                sp.dma_start(out[0, t * P:(t + 1) * P, :], yt[:, t]).then_inc(s_st, 16)
            sp.wait_ge(s_st, NT * 16)

        @block.scalar
        def _(act):
            for t in range(NT):
                act.wait_ge(s_y[t], 16)
                if t >= 2:
                    act.wait_ge(s_sq, t - 1)
                act.activation(junk[:, t % 2], yt[:, t], ACT.Square, scale=D ** -0.5, accum_out=ms[:, 0, t:t + 1]).then_inc(s_sq, 1)

        @block.gpsimd
        def _(pool):
            for t in range(NT):
                pool.wait_ge(s_sq, t + 1)
                nc.gpsimd.tensor_tensor(ms[:, 1, t:t + 1], ms[:, 0, t:t + 1], mhalf[:, 16:17], ALU.add).then_inc(s_pool, 1)
                pool.wait_ge(s_pool, t + 1)
                nc.gpsimd.tensor_tensor(ms[:, 2, t:t + 1], ms[:, 1, t:t + 1], mhalf[:, 0:1], ALU.pow).then_inc(s_rs, 1)

        @block.vector
        def _(dve):
            step = chain(dve, s_dve)
            for t in range(NT):
                dve.wait_ge(s_rs, t + 1)
                step(nc.vector.scalar_tensor_tensor(yt[:, t], yt[:, t], ms[:, 2, t:t + 1], rows[:, G2], ALU.mult, ALU.mult))
                nc.vector.tensor_tensor(yt[:, t], yt[:, t], x1[:, t], ALU.add).then_inc(s_o, 1)


def ds(start, size):
    return bass.ds(start, size)


def program(nc, a, out):
    b = Build(nc)
    qT_d = nc.dram_tensor("qT_scratch", [KT_N, HD, NP, 2, P], F32).ap()
    kT_d = nc.dram_tensor("kT_scratch", [5, P, KEYS], F32).ap()
    mod_d = nc.dram_tensor("mod_scratch", [2, 6, D], F32).ap()
    o_d = nc.dram_tensor("o_scratch", [SEQ, D], F32).ap()
    h2_d = nc.dram_tensor("h2_scratch", [SEQ, D], F32).ap()
    y_d = nc.dram_tensor("y_scratch", [SEQ + P, D], F32).ap()
    with ExitStack() as top:
        ident = b.sb(top, "ident", [P, P])
        rows = b.sb(top, "mod_rows", [P, 4, D])
        nlam = b.sb(top, "neg_lambda", [P, 1])
        mhalf = b.sb(top, "minus_half_eps", [P, 32])
        s_win = b.sem(top, "w_in_loaded")
        s_rows2 = b.sem(top, "later_rows_loaded")
        with ExitStack() as kv:
            with ExitStack() as ph:
                w_in = ph.enter_context(nc.sbuf_tensor("w_in_sb", [P, KD, INW], F32, side="right"))
                rows1 = ph.enter_context(nc.sbuf_tensor("first_norm_rows", [P, 4, D], F32, side="right"))
                modulation(b, a, ident, rows1, rows, nlam, mhalf, w_in, s_win, mod_d)
                vv = b.sb(kv, "values", [P, KT_N, VW])
                projections(b, a, ident, rows1, rows, s_rows2, mod_d, mhalf, w_in, s_win, vv, qT_d, kT_d)
            attention(b, a, ident, nlam, mhalf, vv, qT_d, kT_d, o_d)
        x1 = b.sb(top, "x1", [P, NT, D])
        entry = b.sb(top, "entries", [P, NT, E, NPC], BF16)
        mask = b.sb(top, "chosen", [P, NT, E], BF16)
        before = b.sb(top, "before", [P, P])
        part = b.sb(top, "partition", [P, 2])
        count = b.sb(top, "count_row", [P, 9 * P])
        output_and_router(b, a, ident, rows, s_rows2, mhalf, x1, entry, mask, before, part, count, o_d, h2_d, y_d)
        rank = b.sb(top, "rank", [P, NT, E])
        tab = b.sb(top, "block_table", [1, 6, P + 8], I32)
        routing_tables(b, ident, before, part, entry, mask, rank, tab)
        experts(b, a, ident, part, count, entry, rank, tab, h2_d, y_d)
        final(b, a, rows, mhalf, x1, y_d, out)


def rope_table():
    n = HD // 4
    inv = np.float32(10000.0) ** (-np.arange(n, dtype=np.float32) / np.float32(n))
    row = np.repeat(np.arange(SEQ // GRID_W), GRID_W).astype(np.float32)[:, None] * inv
    col = np.tile(np.arange(GRID_W), SEQ // GRID_W).astype(np.float32)[:, None] * inv
    t = np.zeros((KEYS, 2, HD), np.float32)
    t[:, 0] = 1.0
    t[CTX:, 0] = np.concatenate([np.cos(row)] * 2 + [np.cos(col)] * 2, axis=1)
    t[CTX:, 1] = np.concatenate([-np.sin(row), np.sin(row), -np.sin(col), np.sin(col)], axis=1)
    return t


def kernel(**inputs):
    import concourse.bacc as bacc
    from concourse.bass_utils import run_bass_kernel_spmd

    nc = bacc.Bacc("TRN2", target_bir_lowering=False, num_devices=1)
    host = {k: np.ascontiguousarray(v) for k, v in inputs.items() if k not in ("x", "ctx")}
    host["tokens"] = np.concatenate([np.asarray(inputs["ctx"])[0], np.asarray(inputs["x"])[0]], axis=0)
    tok = np.arange(P)
    host["k_ident"] = np.eye(P, dtype=np.float32)
    host["k_rope"] = rope_table()
    host["k_before"] = (tok[:, None] < tok[None, :]).astype(np.float32)
    host["k_count"] = np.ascontiguousarray(np.broadcast_to(np.arange(9 * P, dtype=np.float32), (P, 9 * P)))
    host["k_part"] = np.arange(P, dtype=np.float32)[:, None]
    arrays, a = {}, {}
    for name, v in host.items():
        v = np.ascontiguousarray(v)
        arrays[f"in_{name}"] = v
        a[name] = nc.dram_tensor(f"in_{name}", v.shape, mybir.dt.from_np(v.dtype), kind="ExternalInput").ap()
    out = nc.dram_tensor("out", (1, SEQ, D), F32, kind="ExternalOutput").ap()
    program(nc, a, out)
    r = run_bass_kernel_spmd(nc, [arrays], core_ids=[0])
    return r.results[0]["out"]
```
